# Optimizing a Trainium2 kernel written in Bass

```python
import jax, jax.numpy as jnp
from jax import lax
import numpy as np

D_MODEL = 2048
BATCH = 1
SEQ = 128
DEPTH = 1
DEC_BATCH = 1
DEC_SEQ = 512
PAST_LEN = 128

GRID_W = 64
N_MOD = 6
EPS = 1e-6

GLA_HEADS = 4
GLA_DK = D_MODEL // 16
GLA_DV = D_MODEL // 8
GLA_KW = GLA_HEADS * GLA_DK
GLA_VW = GLA_HEADS * GLA_DV
GLA_RANK = 16
GLA_TAU = 16.0
GLA_CHUNK = 64

SWA_HEADS = 16
SWA_KV_HEADS = 4
SWA_GROUP = SWA_HEADS // SWA_KV_HEADS
SWA_HEAD_DIM = 64
SWA_QW = SWA_HEADS * SWA_HEAD_DIM
SWA_KVW = SWA_KV_HEADS * SWA_HEAD_DIM
WINDOW = 128
SWA_BLOCK = 128
ROPE_BASE = 10000.0

N_EXPERTS = 16
EXPERT_FF = D_MODEL // 2
CAPACITY_FACTOR = 2

IN_WIDTHS = (GLA_KW, GLA_KW, GLA_VW, GLA_VW, GLA_RANK, GLA_RANK, SWA_QW, SWA_KVW, SWA_KVW, D_MODEL, D_MODEL)
IN_DIM = 2 * GLA_KW + 2 * GLA_VW + 2 * GLA_RANK + SWA_QW + 2 * SWA_KVW + 2 * D_MODEL

kernel_name = 'hybrid_gla_swa_ec_diffusion_step'

def rmsnorm(x, g):
    xf = x.astype(jnp.float32)
    y = xf * lax.rsqrt(jnp.mean(xf * xf, axis=-1, keepdims=True) + EPS)
    return (y * g.astype(jnp.float32)).astype(x.dtype)

def _split_in(p):
    cuts = [int(v) for v in np.cumsum(IN_WIDTHS)[:-1]]
    return jnp.split(p, cuts, axis=-1)

def axial_rope(x):
    s = x.shape[1]
    rows = s // GRID_W
    row = jnp.repeat(jnp.arange(rows), GRID_W).astype(jnp.float32)
    col = jnp.tile(jnp.arange(GRID_W), rows).astype(jnp.float32)
    half = SWA_HEAD_DIM // 2
    npair = half // 2
    inv_freq = ROPE_BASE ** (-jnp.arange(npair, dtype=jnp.float32) / npair)
    xf = x.astype(jnp.float32)

    def rot(xa, pos):
        ang = pos[:, None] * inv_freq[None, :]
        cos = jnp.cos(ang)[None, :, None, :]
        sin = jnp.sin(ang)[None, :, None, :]
        x1, x2 = xa[..., :npair], xa[..., npair:]
        return jnp.concatenate([x1 * cos - x2 * sin, x2 * cos + x1 * sin], axis=-1)

    out = jnp.concatenate([rot(xf[..., :half], row), rot(xf[..., half:], col)], axis=-1)
    return out.astype(x.dtype)

def gla_chunk_scan(q, k, v, g, s0):
    bsz, nh, s, dk = q.shape
    dv = v.shape[-1]
    c = GLA_CHUNK
    n = s // c
    q, k, g = [t.reshape(bsz, nh, n, c, dk) for t in (q, k, g)]
    v = v.reshape(bsz, nh, n, c, dv)
    b = jnp.cumsum(g, axis=3)
    b_last = b[:, :, :, -1:, :]
    q_in = q * jnp.exp(b)
    k_in = k * jnp.exp(-b)
    k_st = k * jnp.exp(b_last - b)
    causal = jnp.tril(jnp.ones((c, c), dtype=bool))
    a = jnp.where(causal, jnp.einsum('bhnik,bhnjk->bhnij', q_in, k_in), 0.0)
    o_intra = jnp.einsum('bhnij,bhnjv->bhniv', a, v)
    decay = jnp.exp(b_last[:, :, :, 0, :])

    def step(state, inp):
        q_c, k_c, v_c, d_c = inp
        o_c = jnp.einsum('bhik,bhkv->bhiv', q_c, state)
        state = d_c[..., None] * state + jnp.einsum('bhik,bhiv->bhkv', k_c, v_c)
        return state, o_c

    xs = (jnp.moveaxis(q_in, 2, 0), jnp.moveaxis(k_st, 2, 0), jnp.moveaxis(v, 2, 0), jnp.moveaxis(decay, 2, 0))
    s_fin, o_inter = lax.scan(step, s0, xs)
    o = o_intra + jnp.moveaxis(o_inter, 0, 2)
    return o.reshape(bsz, nh, s, dv), s_fin

def _to_heads(t, n_heads, d):
    bsz, s, _ = t.shape
    return t.reshape(bsz, s, n_heads, d).transpose(0, 2, 1, 3).astype(jnp.float32)

def gla_mixer(gq, gk, gv, gr, gaf, gab, w_dec_f, b_dec_f, w_dec_b, b_dec_b, g_gla, s0_f, s0_b):
    bsz, s, _ = gq.shape
    q = _to_heads(gq, GLA_HEADS, GLA_DK) * (GLA_DK ** -0.5)
    k = _to_heads(gk, GLA_HEADS, GLA_DK)
    v = _to_heads(gv, GLA_HEADS, GLA_DV)
    log_a_f = jax.nn.log_sigmoid((gaf @ w_dec_f + b_dec_f).astype(jnp.float32)) / GLA_TAU
    log_a_b = jax.nn.log_sigmoid((gab @ w_dec_b + b_dec_b).astype(jnp.float32)) / GLA_TAU
    g_f = _to_heads(log_a_f, GLA_HEADS, GLA_DK)
    g_b = _to_heads(log_a_b, GLA_HEADS, GLA_DK)
    o_f, st_f = gla_chunk_scan(q, k, v, g_f, s0_f.astype(jnp.float32))
    flip = lambda t: jnp.flip(t, axis=2)
    o_b, st_b = gla_chunk_scan(flip(q), flip(k), flip(v), flip(g_b), s0_b.astype(jnp.float32))
    o = o_f + flip(o_b)
    o = o * lax.rsqrt(jnp.mean(o * o, axis=-1, keepdims=True) + EPS) * g_gla.astype(jnp.float32).reshape(GLA_HEADS, 1, GLA_DV)
    o = o.transpose(0, 2, 1, 3).reshape(bsz, s, GLA_VW) * jax.nn.silu(gr.astype(jnp.float32))
    return o.astype(gq.dtype), st_f, st_b

def sink_softmax(score_list, sink):
    s_sink = sink.astype(jnp.float32).reshape(SWA_KV_HEADS, SWA_GROUP, 1, 1)
    m = s_sink
    for sc in score_list:
        m = jnp.maximum(m, jnp.max(sc, axis=-1, keepdims=True))
    ps = [jnp.exp(sc - m) for sc in score_list]
    den = jnp.exp(s_sink - m)
    for p in ps:
        den = den + jnp.sum(p, axis=-1, keepdims=True)
    return [p / den for p in ps]

def context_attention(q, k, v, sink):
    bsz, s, _, _ = q.shape
    nb = s // SWA_BLOCK
    scale = SWA_HEAD_DIM ** -0.5
    qb = jnp.moveaxis(q.reshape(bsz, nb, SWA_BLOCK, SWA_KV_HEADS, SWA_GROUP, SWA_HEAD_DIM), 1, 0).astype(jnp.float32)
    kf = k.astype(jnp.float32)
    vf = v.astype(jnp.float32)

    def one_block(q_blk):
        sc = jnp.einsum('bqhgd,bkhd->bhgqk', q_blk, kf) * scale
        (p,) = sink_softmax([sc], sink)
        return jnp.einsum('bhgqk,bkhd->bqhgd', p, vf)

    o = lax.map(one_block, qb)
    return jnp.moveaxis(o, 0, 1).reshape(bsz, s, SWA_QW).astype(q.dtype)

def latent_attention(q, k, v, ctx_k, ctx_v, sink):
    bsz, s, _, _ = q.shape
    blk = SWA_BLOCK
    nb = s // blk
    scale = SWA_HEAD_DIM ** -0.5
    pad = ((0, 0), (blk, blk), (0, 0), (0, 0))

    def band(t):
        tp = jnp.pad(t.astype(jnp.float32), pad).reshape(bsz, nb + 2, blk, SWA_KV_HEADS, SWA_HEAD_DIM)
        return jnp.concatenate([tp[:, :-2], tp[:, 1:-1], tp[:, 2:]], axis=2)

    kw, vw = band(k), band(v)
    qb = q.reshape(bsz, nb, blk, SWA_KV_HEADS, SWA_GROUP, SWA_HEAD_DIM).astype(jnp.float32)
    ckf = ctx_k.astype(jnp.float32)
    cvf = ctx_v.astype(jnp.float32)
    s_ctx = jnp.einsum('bnqhgd,bkhd->bnhgqk', qb, ckf) * scale
    s_band = jnp.einsum('bnqhgd,bnkhd->bnhgqk', qb, kw) * scale
    qi = jnp.arange(blk)[:, None]
    kj = jnp.arange(3 * blk)[None, :]
    in_window = jnp.abs(kj - blk - qi) <= WINDOW
    k_abs = jnp.arange(nb)[:, None] * blk - blk + jnp.arange(3 * blk)[None, :]
    in_seq = (k_abs >= 0) & (k_abs < s)
    mask = in_window[None, :, :] & in_seq[:, None, :]
    s_band = jnp.where(mask[None, :, None, None], s_band, -jnp.inf)
    p_ctx, p_band = sink_softmax([s_ctx, s_band], sink)
    o = jnp.einsum('bnhgqk,bkhd->bnqhgd', p_ctx, cvf) + jnp.einsum('bnhgqk,bnkhd->bnqhgd', p_band, vw)
    return o.reshape(bsz, s, SWA_QW).astype(q.dtype)

def expert_choice_ffn(h, w_router, w_gate, w_up, w_down):
    shp = h.shape
    xf = h.reshape(-1, shp[-1])
    n = xf.shape[0]
    cap = CAPACITY_FACTOR * n // N_EXPERTS
    aff = jax.nn.softmax((xf @ w_router).astype(jnp.float32), axis=-1)
    gate, idx = lax.top_k(aff.T, cap)
    xs = xf[idx]
    hid = jax.nn.silu(jnp.einsum('ecd,edf->ecf', xs, w_gate)) * jnp.einsum('ecd,edf->ecf', xs, w_up)
    ye = jnp.einsum('ecf,efd->ecd', hid, w_down) * gate[..., None].astype(xf.dtype)
    y = jnp.zeros_like(xf).at[idx.reshape(-1)].add(ye.reshape(-1, shp[-1]))
    return y.reshape(shp)

def trunk_layer(x, cond, is_latent, s0_f, s0_b, ctx_k, ctx_v,
                w_mod, b_mod, g_norm1, w_in, w_dec_f, b_dec_f, w_dec_b, b_dec_b, g_gla,
                attn_sink, w_branch_a, w_branch_b, w_out, g_norm2, w_router,
                w_exp_gate, w_exp_up, w_exp_down):
    bsz, s, _ = x.shape
    mod = jax.nn.silu(cond) @ w_mod + b_mod
    sh1, sc1, gt1, sh2, sc2, gt2 = [m[:, None, :] for m in jnp.split(mod, N_MOD, axis=-1)]
    h = rmsnorm(x, g_norm1) * (1 + sc1) + sh1
    gq, gk, gv, gr, gaf, gab, sq, sk, sv, gate_a, gate_b = _split_in(h @ w_in)
    o_gla, st_f, st_b = gla_mixer(gq, gk, gv, gr, gaf, gab, w_dec_f, b_dec_f, w_dec_b, b_dec_b, g_gla, s0_f, s0_b)
    q = sq.reshape(bsz, s, SWA_HEADS, SWA_HEAD_DIM)
    k = sk.reshape(bsz, s, SWA_KV_HEADS, SWA_HEAD_DIM)
    v = sv.reshape(bsz, s, SWA_KV_HEADS, SWA_HEAD_DIM)
    if is_latent:
        o_swa = latent_attention(axial_rope(q), axial_rope(k), v, ctx_k, ctx_v, attn_sink)
    else:
        o_swa = context_attention(q, k, v, attn_sink)
    merged = jax.nn.sigmoid(gate_a) * (o_gla @ w_branch_a) + jax.nn.sigmoid(gate_b) * (o_swa @ w_branch_b)
    x = x + gt1 * (merged @ w_out)
    h2 = rmsnorm(x, g_norm2) * (1 + sc2) + sh2
    x = x + gt2 * expert_choice_ffn(h2, w_router, w_exp_gate, w_exp_up, w_exp_down)
    return x, (st_f, st_b, k, v)

def setup_inputs(seed: int = 0) -> dict:
    key = jax.random.key(seed)
    ks = jax.random.split(key, 32)
    f32 = jnp.float32

    def nrm(k, shape, scale=1.0):
        return jax.random.normal(k, shape, f32) * scale

    L = DEPTH
    return {
        'x_prompt': nrm(ks[0], (BATCH, SEQ, D_MODEL)),
        'x_sample': nrm(ks[1], (DEC_BATCH, DEC_SEQ, D_MODEL)),
        'state_gla_fwd': nrm(ks[2], (DEC_BATCH, L, GLA_HEADS, GLA_DK, GLA_DV)),
        'state_gla_bwd': nrm(ks[3], (DEC_BATCH, L, GLA_HEADS, GLA_DK, GLA_DV)),
        'cache_k': nrm(ks[4], (DEC_BATCH, L, PAST_LEN, SWA_KV_HEADS, SWA_HEAD_DIM)),
        'cache_v': nrm(ks[5], (DEC_BATCH, L, PAST_LEN, SWA_KV_HEADS, SWA_HEAD_DIM)),
        'c': nrm(ks[6], (DEC_BATCH, D_MODEL)),
        'c_ctx': nrm(ks[7], (D_MODEL,)),
        'w_mod': nrm(ks[8], (L, D_MODEL, N_MOD * D_MODEL), 0.5 * D_MODEL ** -0.5),
        'b_mod': nrm(ks[9], (L, N_MOD * D_MODEL), 0.02),
        'g_norm1': 1.0 + nrm(ks[10], (L, D_MODEL), 0.02),
        'w_in': nrm(ks[11], (L, D_MODEL, IN_DIM), D_MODEL ** -0.5),
        'w_dec_f': nrm(ks[12], (L, GLA_RANK, GLA_KW), GLA_RANK ** -0.5),
        'b_dec_f': nrm(ks[13], (L, GLA_KW), 0.1),
        'w_dec_b': nrm(ks[14], (L, GLA_RANK, GLA_KW), GLA_RANK ** -0.5),
        'b_dec_b': nrm(ks[15], (L, GLA_KW), 0.1),
        'g_gla': 1.0 + nrm(ks[16], (L, GLA_VW), 0.02),
        'attn_sink': nrm(ks[17], (L, SWA_HEADS), 0.5),
        'w_branch_a': nrm(ks[18], (L, GLA_VW, D_MODEL), GLA_VW ** -0.5),
        'w_branch_b': nrm(ks[19], (L, SWA_QW, D_MODEL), SWA_QW ** -0.5),
        'w_out': nrm(ks[20], (L, D_MODEL, D_MODEL), D_MODEL ** -0.5),
        'g_norm2': 1.0 + nrm(ks[21], (L, D_MODEL), 0.02),
        'w_router': nrm(ks[22], (L, D_MODEL, N_EXPERTS), D_MODEL ** -0.5),
        'w_exp_gate': nrm(ks[23], (L, N_EXPERTS, D_MODEL, EXPERT_FF), D_MODEL ** -0.5),
        'w_exp_up': nrm(ks[24], (L, N_EXPERTS, D_MODEL, EXPERT_FF), D_MODEL ** -0.5),
        'w_exp_down': nrm(ks[25], (L, N_EXPERTS, EXPERT_FF, D_MODEL), EXPERT_FF ** -0.5),
        'g_final': 1.0 + nrm(ks[26], (D_MODEL,), 0.02),
    }

def reference(x_prompt, x_sample, state_gla_fwd, state_gla_bwd, cache_k, cache_v, c, c_ctx,
              w_mod, b_mod, g_norm1, w_in, w_dec_f, b_dec_f, w_dec_b, b_dec_b, g_gla, attn_sink,
              w_branch_a, w_branch_b, w_out, g_norm2, w_router, w_exp_gate, w_exp_up, w_exp_down,
              g_final):
    bp = x_prompt.shape[0]
    h_ctx = x_prompt
    h_lat = x_sample
    zero_state = jnp.zeros((bp, GLA_HEADS, GLA_DK, GLA_DV), jnp.float32)
    sf_list, sb_list, k_list, v_list = [], [], [], []
    for l in range(DEPTH):
        lp = (w_mod[l], b_mod[l], g_norm1[l], w_in[l], w_dec_f[l], b_dec_f[l], w_dec_b[l], b_dec_b[l],
              g_gla[l], attn_sink[l], w_branch_a[l], w_branch_b[l], w_out[l], g_norm2[l], w_router[l],
              w_exp_gate[l], w_exp_up[l], w_exp_down[l])
        h_ctx, (st_f, st_b, k_ctx, v_ctx) = trunk_layer(h_ctx, c_ctx[None, :], False, zero_state, zero_state,
                                                        None, None, *lp)
        sf_list.append(st_f)
        sb_list.append(st_b)
        k_list.append(k_ctx)
        v_list.append(v_ctx)
        h_lat, _ = trunk_layer(h_lat, c, True, state_gla_fwd[:, l], state_gla_bwd[:, l],
                               cache_k[:, l], cache_v[:, l], *lp)
    y_prompt = rmsnorm(h_ctx, g_final)
    y_sample = rmsnorm(h_lat, g_final)
    new_state_gla_fwd = jnp.stack(sf_list, axis=1)
    new_state_gla_bwd = jnp.stack(sb_list, axis=1)
    new_cache_k = jnp.stack(k_list, axis=1)
    new_cache_v = jnp.stack(v_list, axis=1)
    return (y_prompt, y_sample, new_state_gla_fwd, new_state_gla_bwd, new_cache_k, new_cache_v)


_drawn_inputs = setup_inputs


def setup_inputs(seed=0):
    import zlib

    import numpy as np

    out = dict(_drawn_inputs(seed))
    spreads = {}
    factors = {'state_gla_fwd': 8.0,
     'state_gla_bwd': 8.0,
     'cache_k': 6.69,
     'cache_v': 5.542,
     'g_gla': 8.0,
     'attn_sink': 22.49,
     'g_norm2': 8.0,
     'g_final': 8.294}
    for name, (base, spread) in spreads.items():
        noise = np.random.default_rng([zlib.crc32(name.encode()), seed]).standard_normal(out[name].shape)
        drawn = base * np.exp(spread * noise) if base else spread * noise
        out[name] = __import__('jax').numpy.asarray(drawn.astype(out[name].dtype))
    for name, factor in factors.items():
        out[name] = (out[name] * factor).astype(out[name].dtype)
    return out
```

```python
from contextlib import ExitStack

import numpy as np

import concourse.bass as bass
from concourse import mybir

F32 = mybir.dt.float32
F32R = mybir.dt.float32r
I32 = mybir.dt.int32
U32 = mybir.dt.uint32
ALU = mybir.AluOpType
ACT = mybir.ActivationFunctionType
AX = mybir.AxisListType
ds = bass.ds

P = 128
D = 2048
KT = D // P
LAT, CTX = 512, 128
TOK = LAT + CTX
NT = TOK // P
EPS = 1e-6
BANK = 512

GH, GK, GV, RANK = 4, 128, 256, 16
TAU = 16.0
CH = 64
NCH = TOK // CH
LCH = LAT // CH

SH, SKV, HD = 16, 4, 64
GRP = SH // SKV

NE, FF = 16, 1024
FT = FF // P
CAP_L = 2 * LAT // NE
CAP_C = 2 * CTX // NE
CAP = CAP_L + CAP_C

COL_GV = 2 * GH * GK
COL_GR = COL_GV + GH * GV
COL_GA = COL_GR + GH * GV
COL_SQ = COL_GA + 2 * RANK
COL_SKV = COL_SQ + SH * HD
COL_GATE_A = COL_SKV + 2 * SKV * HD
COL_GATE_B = COL_GATE_A + D

SLOTS = 4
SLOT = 2048

G_MOD = 0
G_A = G_MOD + 6 * KT
G_GATE = G_A + 9 * 4
G_OUT = G_GATE + 4 * 12
G_EXP = G_OUT + 4 * 4
EXP_G = 3 * 8

SP = 4
AHEAD = 3
P_A = 0
P_GATE = P_A + 9 * KT
P_OUT = P_GATE + 4 * 48
GATE_PIECES = ((0, KT), (KT, 8), (KT + 8, KT), (2 * KT + 8, 8))
P_EXP = P_OUT + 4 * KT
P_END = P_EXP + NE * EXP_G

C_ID, C_MF, C_MB, C_RST, C_SW, C_SW3, C_COS, C_SIN, C_PERM = np.cumsum(
    [0, 128, 128, 128, 640, 512, 384, 512, 512]).tolist()
C_END = C_PERM + 128


def constants():
    c = np.zeros((P, C_END), np.float32)
    i = np.arange(P)
    c[:, C_ID:C_ID + P] = np.eye(P)
    same = i[:, None] // CH == i[None, :] // CH
    c[:, C_MF:C_MF + P] = same & (i[:, None] <= i[None, :])
    c[:, C_MB:C_MB + P] = same & (i[:, None] >= i[None, :])
    c[:, C_RST:C_RST + TOK] = (np.arange(TOK) % CH != 0)[None, :]
    before = np.where(i[None, :] >= i[:, None], 0.0, -1e30)
    after = np.where(i[None, :] <= i[:, None], 0.0, -1e30)
    c[:, C_SW:C_SW + P] = before
    c[:, C_SW + 2 * P:C_SW + 3 * P] = after
    c[:, C_SW3:C_SW3 + P] = before
    npair = HD // 4
    inv = (np.float32(10000.0) ** (-np.arange(npair, dtype=np.float32) / np.float32(npair))).astype(np.float32)
    tok = np.arange(LAT)
    d = i % HD
    pos = np.where((d < HD // 2)[:, None], (tok // 64)[None, :], (tok % 64)[None, :]).astype(np.float32)
    ang = pos * inv[d % npair][:, None]
    c[:, C_COS:C_COS + LAT] = np.cos(ang)
    c[:, C_SIN:C_SIN + LAT] = np.sin(ang)
    for m in range(P):
        if m % (2 * npair) < npair:
            c[m + npair, C_PERM + m] = -1.0
        else:
            c[m - npair, C_PERM + m] = 1.0
    return c


U_PLACE = [(5, 0, 3, 0), (6, 0, 4, 0), (5, 1, 3, 0), (6, 1, 4, 0), (7, 0, 7, 0), (5, 0, 8, 3), (7, 1, 7, 0),
           (5, 1, 8, 3), (6, 0, 9, 4)]


class Chain:

    def __init__(self, eng, sem):
        self.eng, self.sem, self.base, self.n = eng, sem, 0, 0

    def step(self, ins):
        ins.then_inc(self.sem, 1)
        self.n += 1
        self.eng.wait_ge(self.sem, self.base + self.n)

    def enter(self, i, per):
        self.start = self.n
        self.base = i * per
        self.per = per

    def leave(self, count):
        assert self.n - self.start == self.per, (self.n - self.start, self.per)
        self.n = self.start + count * self.per
        self.base = 0


def build(nc, T):
    w_mod = T["w_mod"][0].rearrange("(k p) n -> p k n", p=P)
    w_in = T["w_in"][0].rearrange("(k p) n -> p k n", p=P)
    w_a = T["w_branch_a"][0].rearrange("(k p) n -> p k n", p=P)
    w_b = T["w_branch_b"][0].rearrange("(k p) n -> p k n", p=P)
    w_out = T["w_out"][0].rearrange("(k p) n -> p k n", p=P)
    w_eg = T["w_exp_gate"][0].rearrange("e (p k) n -> e p k n", p=P)
    w_eu = T["w_exp_up"][0].rearrange("e (p k) n -> e p k n", p=P)
    w_ed = T["w_exp_down"][0].rearrange("e (p k) n -> e p k n", p=P)
    x_lat, x_ctx = T["x_sample"][0], T["x_prompt"][0]
    x_of = [x_lat[t * P:(t + 1) * P, :] for t in range(4)] + [x_ctx]
    y_of = [T["y_sample"][0][t * P:(t + 1) * P, :] for t in range(4)] + [T["y_prompt"][0]]
    mod_dram = nc.dram_tensor("mod_rows", [2, 6 * D], F32, kind="Internal").ap()
    h2_dram = nc.dram_tensor("h2_rows", [TOK, D], F32, kind="Internal").ap()
    mT_dram = nc.dram_tensor("merged_T", [P, KT, TOK], F32, kind="Internal").ap()
    y_dram = nc.dram_tensor("y_rows", [TOK, D], F32, kind="Internal").ap()

    def row_bcast(row, n=P):
        return row.partition_broadcast(n)

    with ExitStack() as ctx:
        def sb(name, shape, dt=F32):
            return ctx.enter_context(nc.sbuf_tensor(name, shape, dt))

        def sem(name):
            return ctx.enter_context(nc.semaphore(name))

        ps = ctx.enter_context(nc.psum_tensor("ps", [P, 8, BANK], F32))
        cst = sb("cst", [P, C_END])
        ring = sb("ring", [P, SLOTS, SLOT])
        hT = sb("hT", [P, KT, TOK])
        ar_at = nc.sbuf_base
        ar = sb("ar", [P, 30400])
        condT = sb("condT", [P, KT, 2])
        stat = sb("stat", [P, 2 * NT])
        decay = sb("decay", [P, NCH])
        rs_gla = sb("rs_gla", [P, NT * GH])
        sink = sb("sink", [P, SH])
        soft = sb("soft", [P, 2, 5, GRP])
        aff = sb("aff", [P, 2, NT, 16])
        idxT = sb("idxT", [P, NE + 2], U32)
        gateT = sb("gateT", [P, NE])
        epsb = sb("epsb", [P, 1])
        gidx = sb("gidx", [CAP, 1], U32)
        sidx = sb("sidx", [CAP, 1], U32)

        ident = cst[:, C_ID:C_ID + P]

        def area(at, *dims):
            n = int(np.prod(dims))
            v = ar[:, at:at + n]
            if len(dims) == 2:
                v = v.rearrange("p (a b) -> p a b", a=dims[0])
            if len(dims) == 3:
                v = v.rearrange("p (a b c) -> p a b c", a=dims[0], b=dims[1])
            return v

        def split_area(name, at, *dims):
            return nc.alloc_sbuf_tensor_at(name, [P, *dims], F32R, offset=ar_at + 4 * at)

        def hT_area(at, n):
            return hT[:, :, :].rearrange("p k t -> p (k t)")[:, at:at + n]

        bmod = area(0, 6 * D)
        modrow = area(6 * D, 6 * D)
        cond = area(28800, P)
        Ah, Bh = area(0, 2, D), area(2 * D, 2, D)
        g1 = area(4 * D, D)
        hrow = area(5 * D, 2, D)
        junk = area(7 * D, D)
        xrow = area(12 * D, 2, D)
        gqT, gkT = area(0, GH, TOK), area(2560, GH, TOK)
        gv = area(5120, NT, GH * GV)
        og = area(10240, NT, GH * GV)
        gaT = area(15360, TOK)
        wdec = area(16000, 2, GH * GK)
        st = area(17024, 2, 10, GV)
        tz, tg, tc, tB, tD, xq, xk, ks = [area(22144 + 640 * i, TOK) for i in range(8)]
        aTm = area(27264, 2, TOK)
        glag = area(28544, GH * GV)
        oT = area(0, 8, TOK)
        sil, onr = area(5120, 2, BANK), area(6144, 2, BANK)
        swT = area(5120, 8, TOK)
        skT = area(10240, SKV, TOK + P)
        svr = area(13312, NT + 1, SKV * HD)
        skr = area(14848, NT + 1, SKV * 2 * HD)
        Sbuf = area(17920, 2, GRP * BANK)
        pT = area(22016, 2, 4 * BANK)
        rp = area(27264, 2, BANK)
        krow_out = area(28544, SKV * HD)
        spW = split_area("split_weights", 18000, SP, 2, BANK)
        spX = split_area("split_tokens", 18000 + SP * 2 * BANK, SP, 2, TOK)
        mTc = area(10240, 4, TOK)
        sg = area(15360, NT, BANK)
        mrow = area(27216, NT, BANK)
        mtmp = area(29776, BANK)
        x1 = area(0, NT, D)
        gt1 = area(10240, 2, D)
        wtmp = area(14336, 2, BANK)
        junkx = area(15360, D)
        A2 = hT_area(0, 2 * D).rearrange("p (a b) -> p a b", a=2)
        B2 = hT_area(2 * D, 2 * D).rearrange("p (a b) -> p a b", a=2)
        g2 = hT_area(4 * D, D)
        gt2 = area(27300, D)
        h2row = area(18000, D)
        h2T = area(20048, KT, P)
        wrt = area(22096, KT, NE)
        affT = area(22352, TOK)
        vals, idxf = area(22992, CAP), area(23072, CAP)
        idxu = area(23152, CAP).bitcast(U32)
        xs = area(0, D)
        xsT = split_area("split_xsT", 2048, 2, KT, CAP)
        hidT = split_area("split_hidT", 4608, 2, FT, CAP)
        hid = area(5888, FF)
        silx = area(6912, FF)
        ye = area(7936, D)
        spE = split_area("split_experts", 10240, SP, 2, SLOT)
        gfin = hT_area(0, D)
        yrow = hT_area(D, 2 * D).rearrange("p (a b) -> p a b", a=2)
        junk2 = hT_area(3 * D, D)

        s_cst = sem("consts_loaded")
        slot_ready = [sem(f"slot_ready{s}") for s in range(SLOTS)]
        slot_used = sem("slots_used")
        piece_high, piece_ready, piece_used = sem("pieces_high"), sem("pieces_ready"), sem("pieces_used")
        mT_st, mT_free, mT_ld, xs_h, xs_l, hd_h = (sem("merged_stored"), sem("merged_free"), sem("merged_loaded"),
                                                   sem("xs_high"), sem("xs_low"), sem("hidden_high"))
        s_condT, s_condS = sem("cond_transposed"), sem("cond_silu")
        mod_ev, mod_st = sem("mod_evacuated"), sem("mod_stored")
        mod_ab, x_ld, h_sq, h_row, h_tr, h_cp = (sem("mod_rows_loaded"), [sem("x_loaded0"), sem("x_loaded1")],
                                                 sem("x_squared"), sem("h_rows"), sem("h_transposed"), sem("h_copied"))
        pj_pe, pj_ev = sem("projected"), sem("projection_evacuated")
        ga_w, s_wdec, ga_pe, ga_ev = sem("decay_in_loaded"), sem("decay_w_loaded"), sem("ga_product"), sem("ga_ready")
        wdec0 = sem("wdec_cleared")
        z_pe, z_ab, z_ln, g_b, g_e, g_m = (sem("z_product"), sem("z_abs_read"), sem("z_log"), sem("gla_cumsum"),
                                           sem("gla_exp"), sem("gla_scaled"))
        kt_pe, kt_cp, at_pe, at_cp = sem("kst_transposed"), sem("kst_copied"), sem("aT_product"), sem("aT_masked")
        u_pe, s_up, o_pe, o_ev = sem("U_product"), sem("state_updated"), sem("o_product"), sem("o_evacuated")
        st_ld, st_out, o_sq = [sem("state0_loaded"), sem("state1_loaded")], sem("state_stored"), sem("o_squared")
        gr_s, gr_o, gr_tr, gr_cp = sem("gr_silu"), sem("gr_gated"), sem("gr_transposed"), sem("gr_copied")
        sq_pm, sq_rp, kv_ld = sem("rope_permuted"), sem("roped"), sem("cache_loaded")
        k_dup, k_tr, k_cp, k_pm, k_rp, kv_st = (sem("k_doubled"), sem("k_transposed"), sem("k_copied"),
                                                sem("k_permuted"), sem("k_roped"), sem("cache_stored"))
        sc_pe, sc_m, sc_mx, sc_e, sc_n = sem("scores"), sem("scores_masked"), sem("scores_max"), sem("probs_exp"), sem("probs")
        pt_pe, pt_cp, pv_pe, pv_cp = sem("p_transposed"), sem("pT_copied"), sem("pv_product"), sem("pv_copied")
        gt_pe, gt_act, gt_dve = sem("gate_products"), sem("gate_sigmoid"), sem("gate_merged")
        mt_pe, mt_cp = sem("merged_transposed"), sem("merged_copied")
        wo_ld, xr_ld, wo_pe, wo_ev = sem("mod2_loaded"), sem("x_again_loaded"), sem("out_products"), sem("x1_ready")
        n2_sq, n2_h, n2_tr, n2_cp, n2_st, lg_pe = (sem("x1_squared"), sem("h2_row"), sem("h2_transposed"),
                                                   sem("h2_copied"), sem("h2_stored"), sem("logits"))
        af_e, af_r, af_tr, af_cp, tk_d, tk_tr, tk_cp = (sem("aff_exp"), sem("aff_rows"), sem("aff_transposed"),
                                                        sem("aff_copied"), sem("topk"), sem("topk_transposed"), sem("topk_ready"))
        gi_cp, xs_ld, xs_tr, xs_cp = sem("gather_index"), sem("xs_gathered"), sem("xs_transposed"), sem("xs_copied")
        hd_s, hd_r, hd_tr, hd_cp, ye_r, ye_st = (
            sem("gate_silu"), sem("hidden"), sem("hidden_transposed"), sem("hidden_copied"),
            sem("expert_out"), sem("expert_added"))
        y_ld, y_sq, y_r, y_st = [sem("y_loaded0"), sem("y_loaded1")], sem("y_squared"), sem("y_ready"), sem("y_stored")
        gf_ld, y_sto = sem("gfinal_loaded"), [sem("y_out0"), sem("y_out1")]
        act_step, dve_step, dve2_step, pool_step = sem("act_step"), sem("dve_step"), sem("dve_loop_step"), sem("pool_step")
        loads_issued, rows_issued = sem("loads_issued"), sem("rows_issued")
        ye_free, x1_st = sem("ye_free"), sem("x1_stored")

        def gate_split(sp, n, q, lo, hi):
            first = GATE_PIECES[q][0]
            sp.pieces(P_GATE + first, n * 48, G_GATE + first // 4, n * 3, (hT, oT, hT, swT)[q], lo, hi)

        units = [(t, g) for t in range(NT) for g in range(SKV)]

        def unit_keys(t):
            if t == NT - 1:
                return [(LAT, P)], [NT - 1]
            lo, hi = max(t - 1, 0), min(t + 1, LAT // P - 1)
            return [(lo * P, (hi - lo + 1) * P), (TOK, P)], [*range(lo, hi + 1), NT]

        def copy_pT(act, u, n):
            for i, _ in enumerate(unit_keys(units[u][0])[1]):
                act.wait_ge(pt_pe, n + 1)
                if u >= 2:
                    act.wait_ge(pv_pe, u - 1)
                act.activation(pT[:, u % 2, i * BANK:(i + 1) * BANK], ps[:, 4 + n % 3, :], ACT.Copy).then_inc(pt_cp, 1)
                n += 1
            return n

        def copy_o(act, u):
            t, g = units[u]
            act.wait_ge(pv_pe, u + 1)
            act.activation(swT[:, 2 * g:2 * g + 2, t * P:(t + 1) * P],
                           ps[:, 7, 0:2 * P].rearrange("p (c q) -> p c q", c=2), ACT.Copy).then_inc(pv_cp, 1)

        def parts(*places):
            return [(k, ps[:, b, at * CAP:(at + n) * CAP].rearrange("p (k t) -> p k t", k=n)) for k, b, at, n in places]

        xs_parts = parts((0, 2, 0, 6), (6, 3, 0, 6), (12, 1, 2, 4))
        hid_parts = parts((0, 0, 0, 6), (6, 1, 0, 2))

        def bank_done(eng, done, before, b, last):
            if b < 4:
                eng.wait_ge(done, before * 4 + (b + 1))
            else:
                eng.wait_ge(piece_used, last + (SP + 1))

        class Split:

            def __init__(self, eng, high):
                self.eng, self.high = eng, high

            def pieces(self, first, turn, granule, gturn, src, lo, hi):
                for k in range(lo, hi):
                    s, g = (first + k) % SP, granule + k // 4
                    raw = ring[:, g % SLOTS, :].rearrange("p (k n) -> p k n", k=4)[:, k % 4, :]
                    if self.high:
                        if k % 4 == 0:
                            self.eng.wait_ge(slot_ready[g % SLOTS], gturn * 16 + 16 * (g // SLOTS + 1))
                        self.eng.wait_ge(piece_used, turn + (first + k + 1))
                        self.eng.activation(spW[:, s, 0, :], raw, ACT.Copy)
                        self.eng.activation(spX[:, s, 0, :], src[:, k, :], ACT.Copy).then_inc(piece_high, 1)
                    else:
                        self.eng.wait_ge(piece_high, turn + (first + k + 1))
                        a = self.eng.tensor_tensor(spW[:, s, 1, :], raw, spW[:, s, 0, :].bitcast(F32), ALU.subtract)
                        if k % 4 == 3:
                            a.then_inc(slot_used, 1)
                        self.eng.tensor_tensor(spX[:, s, 1, :], src[:, k, :], spX[:, s, 0, :].bitcast(F32),
                                               ALU.subtract).then_inc(piece_ready, 1)

            def chunk(self, i, lo=0, hi=KT):
                self.pieces(P_A + KT * i, 0, G_A + 4 * i, 0, hT, lo, hi)

        block = ctx.enter_context(nc.Block())

        @block.sync
        def _(sync):
            def load(g, src, dst=None, freed=None):
                first, turn = g
                s = first % SLOTS
                if freed is None:
                    sync.wait_ge(slot_used, first + turn + 1)
                else:
                    sync.wait_ge(piece_ready, freed)
                sync.sem_inc(loads_issued, 1)
                out = ring[:, s, :] if dst is None else dst(ring[:, s, :])
                sync.dma_start(out, src).then_inc(slot_ready[s], 16)

            def k4(v):
                return v.rearrange("p (k n) -> p k n", k=4)

            def k2(v):
                return v.rearrange("p (k n) -> p k n", k=2)

            with sync.Fori(0, 6) as m:
                for j in range(KT):
                    load((G_MOD + j, m * KT), w_mod[:, j, ds(m * D, D)])
            with sync.Fori(0, 6) as c:
                for j in range(4):
                    load((G_A + j, c * 4), w_in[:, 4 * j:4 * j + 4, ds(c * BANK, BANK)], k4)
            with sync.Fori(0, 3) as c:
                for j in range(4):
                    load((G_A + 24 + j, c * 4), w_in[:, 4 * j:4 * j + 4, ds(c * BANK + COL_SQ, BANK)], k4)
            with sync.Fori(0, 4) as n:
                for half, (col, w) in enumerate(((COL_GATE_A, w_a), (COL_GATE_B, w_b))):
                    for j in range(4):
                        load((G_GATE + 6 * half + j, n * 12), w_in[:, 4 * j:4 * j + 4, ds(n * BANK + col, BANK)], k4)
                    for j in range(2):
                        load((G_GATE + 6 * half + 4 + j, n * 12), w[:, 4 * j:4 * j + 4, ds(n * BANK, BANK)], k4)
            with sync.Fori(0, 4) as n:
                for j in range(4):
                    load((G_OUT + j, n * 4), w_out[:, 4 * j:4 * j + 4, ds(n * BANK, BANK)], k4)
            with sync.Fori(0, NE) as e:
                def expert(j, src, dst=None):
                    load((G_EXP + j, e * EXP_G), src, dst, e * EXP_G + (P_EXP + j + 1 - SLOTS))

                for j in range(8):
                    expert(2 * j, w_eg[ds(e, 1), :, 2 * j:2 * j + 2, :].squeeze(0), k2)
                    expert(2 * j + 1, w_eu[ds(e, 1), :, 2 * j:2 * j + 2, :].squeeze(0), k2)
                for j in range(8):
                    expert(16 + j, w_ed[ds(e, 1), :, j, :].squeeze(0))

        @block.gpsimd
        def _(pool):
            pool.dma_start(cst[:, :], T["consts"]).then_inc(s_cst, 16)
            pool.dma_start(cond[0:KT, :], T["c"][0].rearrange("(k p) -> k p", p=P)).then_inc(s_cst, 16)
            pool.dma_start(cond[KT:2 * KT, :], T["c_ctx"].rearrange("(k p) -> k p", p=P)).then_inc(s_cst, 16)
            pool.dma_start(bmod[0:2, :], row_bcast(T["b_mod"][0], 2)).then_inc(s_cst, 16)
            pool.dma_start(sink[:, :], row_bcast(T["attn_sink"][0])).then_inc(s_cst, 16)
            for t in range(2):
                pool.dma_start(xrow[:, t, :], x_of[t]).then_inc(x_ld[t], 16)
            pool.wait_ge(mod_ev, 7)
            pool.dma_start(mod_dram, modrow[0:2, :]).then_inc(mod_st, 16)
            pool.wait_ge(mod_st, 16)

            def mod_load(dst, who, part, s, n=P):
                pool.dma_start(dst, row_bcast(mod_dram[who, part * D:(part + 1) * D], n)).then_inc(s, 16)

            for who in range(2):
                mod_load(Ah[:, who, :], who, 1, mod_ab)
                mod_load(Bh[:, who, :], who, 0, mod_ab)
            pool.dma_start(g1, row_bcast(T["g_norm1"][0])).then_inc(mod_ab, 16)
            for t in range(2, NT):
                pool.wait_ge(h_row, t - 1)
                pool.dma_start(xrow[:, t % 2, :], x_of[t]).then_inc(x_ld[t % 2], 16)
            pool.wait_ge(h_row, NT)
            pool.wait_ge(wdec0, 1)
            for dr, (w, b) in enumerate((("w_dec_f", "b_dec_f"), ("w_dec_b", "b_dec_b"))):
                pool.dma_start(wdec[RANK * dr:RANK * dr + RANK, dr, :], T[w][0]).then_inc(s_wdec, 16)
                pool.dma_start(wdec[2 * RANK:2 * RANK + 1, dr, :], T[b]).then_inc(s_wdec, 16)
            pool.dma_start(glag, row_bcast(T["g_gla"][0])).then_inc(s_wdec, 16)
            pool.wait_ge(piece_used, SP + 4 * KT)
            for s in range(2 * GH):
                h, dr = s // 2, s % 2
                src = T["state_gla_bwd" if dr else "state_gla_fwd"][0, 0, h]
                if s >= 2:
                    pool.wait_ge(o_pe, NT * (s - 1))
                    pool.wait_ge(s_up, 9 * (s - 1))
                    final = T["ns_bwd" if (s - 2) % 2 else "ns_fwd"][0, 0, (s - 2) // 2]
                    pool.dma_start(final, st[:, s % 2, 9, :]).then_inc(st_out, 16)
                pool.dma_start(st[:, s % 2, 0, :], src).then_inc(st_ld[s % 2], 16)
            for s in range(2 * GH, 2 * GH + 2):
                pool.wait_ge(s_up, 9 * (s - 1))
                final = T["ns_bwd" if (s - 2) % 2 else "ns_fwd"][0, 0, (s - 2) // 2]
                pool.dma_start(final, st[:, s % 2, 9, :]).then_inc(st_out, 16)
            pool.wait_ge(st_out, 16 * 2 * GH)
            pool.wait_ge(gr_tr, 10)
            kc = T["cache_k"][0, 0].rearrange("s h d -> s h d")
            skr_c = skr[:, NT, :].rearrange("p (h e d) -> p h e d", h=SKV, e=2)
            for e in range(2):
                pool.dma_start(skr_c[:, :, e, :], kc).then_inc(kv_ld, 16)
            pool.dma_start(svr[:, NT, :], T["cache_v"][0, 0].rearrange("s h d -> s (h d)")).then_inc(kv_ld, 16)
            pool.wait_ge(k_dup, 3 * NT + 1)
            pool.dma_start(T["nk"][0, 0].rearrange("s h d -> s (h d)"), krow_out).then_inc(kv_st, 16)
            pool.dma_start(T["nv"][0, 0].rearrange("s h d -> s (h d)"), svr[:, NT - 1, :]).then_inc(kv_st, 16)
            for n in range(4):
                pool.wait_ge(mt_cp, NT * (n + 1) + 1)
                pool.dma_start(mT_dram[:, 4 * n:4 * n + 4, :], mTc).then_inc(mT_st, 16)
                pool.wait_ge(mT_st, 16 * (n + 1))
                pool.sem_inc(mT_free, 1)
            pool.dma_start(hT[:, :, :], mT_dram).then_inc(mT_ld, 16)
            for who in range(2):
                mod_load(gt1[:, who, :], who, 2, wo_ld)
            for t in range(NT):
                pool.dma_start(x1[:, t, :], x_of[t]).then_inc(xr_ld, 16)
            pool.wait_ge(piece_used, SP + P_EXP)
            for who in range(2):
                mod_load(A2[:, who, :], who, 4, wo_ld)
                mod_load(B2[:, who, :], who, 3, wo_ld)
            pool.dma_start(g2, row_bcast(T["g_norm2"][0])).then_inc(wo_ld, 16)
            mod_load(gt2[0:CAP_L, :], 0, 5, wo_ld, CAP_L)
            mod_load(gt2[CAP_L:CAP, :], 1, 5, wo_ld, CAP_C)
            pool.dma_start(wrt, T["w_router"][0].rearrange("(k p) e -> p k e", p=P)).then_inc(wo_ld, 16)
            for t in range(NT):
                pool.wait_ge(n2_sq, t + 1)
                pool.dma_start(y_dram[t * P:(t + 1) * P, :], x1[:, t, :]).then_inc(x1_st, 16)
                pool.wait_ge(n2_h, t + 1)
                pool.dma_start(h2_dram[t * P:(t + 1) * P, :], h2row).then_inc(n2_st, 16)
            pool.wait_ge(tk_cp, 3)
            pool.wait_ge(n2_st, 16 * NT)
            pool.wait_ge(x1_st, 16 * NT)

            def gather(col):
                pool.tensor_copy(gidx[:, :], col).then_inc(gi_cp, 1)

            def gather_rows():
                pool.indirect_dma_start(xs[0:CAP, :], None, h2_dram, bass.IndirectOffsetOnAxis(ap=gidx[:, :], axis=0))\
                    .then_inc(xs_ld, 16)

            gather(idxT[0:CAP, 0:1])
            pool.wait_ge(gi_cp, 1)
            gather_rows()
            pool.wait_ge(xs_tr, 1)
            gather(idxT[0:CAP, 1:2])
            pool.wait_ge(gi_cp, 2)
            gather_rows()
            with pool.Fori(0, NE) as e:
                pool.wait_ge(xs_tr, e + 2)
                pool.wait_ge(xs_ld, e * 16 + 32)
                gather(idxT[0:CAP, ds(e + 2, 1)])
                pool.wait_ge(gi_cp, e + 3)
                pool.sem_inc(rows_issued, 1)
                gather_rows()
                pool.tensor_copy(sidx[:, :], idxT[0:CAP, ds(e, 1)]).then_inc(pool_step, 1)
                pool.wait_ge(pool_step, e + 1)
                pool.wait_ge(ye_r, e + 2)
                pool.sem_inc(rows_issued, 1)
                pool.indirect_dma_start(y_dram, bass.IndirectOffsetOnAxis(ap=sidx[:, :], axis=0), ye[0:CAP, :], None,
                                        compute_op=ALU.add).then_inc(ye_st, 16)
                pool.wait_ge(ye_st, e * 16 + 16)
                pool.sem_inc(ye_free, 1)
            pool.wait_ge(xs_ld, 16 * (NE + 2))
            pool.wait_ge(ye_st, 16 * NE)
            pool.dma_start(gfin, row_bcast(T["g_final"])).then_inc(gf_ld, 16)
            for t in range(NT):
                if t >= 2:
                    pool.wait_ge(y_sto[t % 2], 16 * (t // 2))
                pool.dma_start(yrow[:, t % 2, :], y_dram[t * P:(t + 1) * P, :]).then_inc(y_ld[t % 2], 16)
                if t >= 1:
                    pool.wait_ge(y_r, t)
                    pool.dma_start(y_of[t - 1], yrow[:, (t - 1) % 2, :]).then_inc(y_sto[(t - 1) % 2], 16)
            pool.wait_ge(y_r, NT)
            pool.dma_start(y_of[NT - 1], yrow[:, (NT - 1) % 2, :]).then_inc(y_sto[(NT - 1) % 2], 16)
            pool.wait_ge(y_sto[0], 48)
            pool.wait_ge(y_sto[1], 32)
            pool.wait_ge(kv_st, 32)
            pool.wait_ge(st_out, 16 * 2 * GH)

        @block.tensor
        def _(pe):
            def slot(first, turn):
                s = first % SLOTS
                pe.wait_ge(slot_ready[s], turn * 16 + 16 * (first // SLOTS + 1))
                return ring[:, s, :]

            pe.sem_inc(slot_used, SLOTS)
            pe.sem_inc(piece_used, SP)
            pe.wait_ge(s_cst, 80)
            pe.transpose(ps[:, 0, 0:2 * KT], cond[0:2 * KT, :], ident[0:2 * KT, 0:2 * KT]).then_inc(s_condT, 1)
            pe.wait_ge(s_condS, 2)
            with pe.Fori(0, 6) as m:
                pe.wait_ge(mod_ev, m + 1)
                for k in range(KT):
                    w = slot(G_MOD + k, m * 4)
                    for n in range(4):
                        mm = pe.matmul(ps[0:2, n, :], condT[:, k, :], w[:, n * BANK:(n + 1) * BANK],
                                       start=(k == 0), stop=(k == KT - 1))
                    mm.then_inc(slot_used, 1)
            for t in range(NT):
                pe.wait_ge(h_row, t + 1)
                if t:
                    pe.wait_ge(h_cp, 4 * t)
                else:
                    pe.wait_ge(mod_ev, 7)
                for k in range(KT):
                    mm = pe.transpose(ps[:, k // 4, (k % 4) * P:(k % 4 + 1) * P],
                                      hrow[:, t % 2, k * P:(k + 1) * P], ident)
                    if k % 4 == 3:
                        mm.then_inc(h_tr, 1)

            def product(first, turn, n_k, bank_free, done):
                for k in range(n_k):
                    s = (first + k) % SP
                    pe.wait_ge(piece_ready, turn + (first + k + 1))
                    for b in range(NT):
                        if k == 0:
                            bank_free(b)
                        for x, w in ((0, 0), (0, 1), (1, 0)):
                            mm = pe.matmul(ps[:, b, :], spX[:, s, x, b * P:(b + 1) * P], spW[:, s, w, :],
                                           start=(k == 0 and x == w), stop=(k == n_k - 1 and x == 1))
                        if k == n_k - 1 and b < 4:
                            mm.then_inc(done, 1)
                    mm.then_inc(piece_used, 1)

            def product_T(first, turn, bank_free, done):
                for k in range(KT):
                    s = (first + k) % SP
                    pe.wait_ge(piece_ready, turn + (first + k + 1))
                    for c in range(4):
                        if k == 0:
                            bank_free(c)
                        for x, w in ((0, 0), (1, 0), (0, 1)):
                            mm = pe.matmul(ps[:, c, :], spW[:, s, w, c * P:(c + 1) * P], spX[:, s, x, 0:LAT],
                                           start=(k == 0 and x == w), stop=(k == KT - 1 and w == 1))
                        if k == KT - 1:
                            mm.then_inc(done, 1)
                        if k == 0 and c == 0:
                            bank_free(4)
                        for x, w in ((0, 0), (1, 0), (0, 1)):
                            mm = pe.matmul(ps[:, 4, c * P:(c + 1) * P], spW[:, s, w, c * P:(c + 1) * P],
                                           spX[:, s, x, LAT:TOK], start=(k == 0 and c == 0 and x == w),
                                           stop=(k == KT - 1 and w == 1), skip_group_check=True)
                    mm.then_inc(piece_used, 1)

            def chunks(first, count, rows):
                with pe.Fori(0, count) as c:
                    def bank_free(b):
                        pe.wait_ge(pj_ev, c * NT + (NT * first + b + 1))
                    if rows:
                        product(P_A + KT * first, c * KT, KT, bank_free, pj_pe)
                    else:
                        product_T(P_A + KT * first, c * KT, bank_free, pj_pe)

            pe.wait_ge(h_cp, 4 * NT)
            chunks(0, 2, False)
            chunks(2, 2, True)
            pe.wait_ge(ga_w, 16)
            gaw = ar[:, 27264:27264 + KT * 2 * RANK].rearrange("p (k n) -> p k n", k=KT)
            for k in range(KT):
                pe.matmul(ps[0:2 * RANK, 5, :], gaw[:, k, :], hT[:, k, 0:LAT], start=(k == 0), stop=(k == KT - 1))
                mm = pe.matmul(ps[0:2 * RANK, 6, 0:CTX], gaw[:, k, :], hT[:, k, LAT:TOK],
                               start=(k == 0), stop=(k == KT - 1))
            mm.then_inc(ga_pe, 1)
            pe.wait_ge(ga_ev, 2)
            pe.wait_ge(s_wdec, 80)
            pe.wait_ge(pj_ev, NT * 5)
            for s in range(2 * GH):
                h, dr = s // 2, s % 2
                if s:
                    pe.wait_ge(o_ev, NT * s)
                w = wdec[0:2 * RANK + 1, dr, h * GK:(h + 1) * GK]
                pe.matmul(ps[:, 0, :], w, gaT[0:2 * RANK + 1, 0:LAT], start=True, stop=True)
                pe.matmul(ps[:, 1, 0:CTX], w, gaT[0:2 * RANK + 1, LAT:TOK], start=True, stop=True).then_inc(z_pe, 1)
                pe.wait_ge(g_m, s + 1)
                for t in range(NT):
                    mm = pe.transpose(ps[:, 2 + t // 4, (t % 4) * P:(t % 4 + 1) * P], tD[:, t * P:(t + 1) * P], ident)
                mm.then_inc(kt_pe, 1)
                for t in range(NT):
                    o = ps[:, 4, t * P:(t + 1) * P] if t < 4 else ps[:, 1, P:2 * P]
                    mm = pe.matmul(o, xk[:, t * P:(t + 1) * P], xq[:, t * P:(t + 1) * P], start=True, stop=True,
                                   skip_group_check=True)
                mm.then_inc(at_pe, 1)
                order = ([9, 8] if dr else [8, 9]) + (list(range(7, 0, -1)) if dr else list(range(7)))
                pe.wait_ge(kt_cp, s + 1)
                for u, c in enumerate(order):
                    lo, t = (c % 2) * CH, c // 2
                    bank, half, _, freed = U_PLACE[u]
                    if s or freed:
                        pe.wait_ge(s_up, 9 * s + freed)
                    pe.matmul(ps[:, bank, half * GV:(half + 1) * GV],
                              ks[lo:lo + CH, t * P:(t + 1) * P], gv[lo:lo + CH, t, h * GV:(h + 1) * GV],
                              start=True, stop=True, skip_group_check=True).then_inc(u_pe, 1)
                pe.wait_ge(at_cp, s + 1)
                for t in ([4, 3, 2, 1, 0] if dr else [4, 0, 1, 2, 3]):
                    o = ps[:, t, 0:GV]
                    mm = pe.matmul(o, aTm[:, dr, t * P:(t + 1) * P], gv[:, t, h * GV:(h + 1) * GV],
                                   start=True, stop=False, skip_group_check=True)
                    for c in ([2 * t + 1, 2 * t] if dr else [2 * t, 2 * t + 1]):
                        lo = (c % 2) * CH
                        if c >= LCH:
                            if c == order[0]:
                                continue
                            state = st[:, dr, 8, :]
                            pe.wait_ge(s_up, 9 * s + 1)
                        else:
                            i = 7 - c if dr else c
                            state = st[:, dr, i, :]
                            if i:
                                pe.wait_ge(s_up, 9 * s + 2 + i)
                            else:
                                pe.wait_ge(st_ld[dr], 16 * (h + 1))
                        mm = pe.matmul(o[lo:lo + CH, :], xq[:, c * CH:(c + 1) * CH], state,
                                       start=False, stop=True, skip_group_check=True)
                    mm.then_inc(o_pe, 1)
            pe.wait_ge(o_ev, 2 * GH * NT)
            with pe.Fori(0, 2) as c:
                def bank_free(b):
                    pe.wait_ge(pj_ev, c * NT + (NT * 4 + b + 1))
                product(P_A + KT * 4, c * KT, KT, bank_free, pj_pe)
                for b in range(NT):
                    pe.wait_ge(gr_o, c * NT + (b + 1))
                    pe.wait_ge(gr_cp, c * NT + (b + 1 + (b == 0)))
                    for q in range(4):
                        mm = pe.transpose(ps[:, 5 + b % 2, q * P:(q + 1) * P], onr[:, b % 2, q * P:(q + 1) * P], ident)
                    mm.then_inc(gr_tr, 1)
            chunks(6, 2, False)
            chunks(8, 1, True)
            for i in range(8):
                pe.wait_ge(pj_ev, NT * (7 + i // 4) + i % 4 + 1)
                if i >= 2:
                    pe.wait_ge(sq_rp, i - 1)
                pe.matmul(ps[:, 5 + i % 2, :], cst[:, C_PERM:C_PERM + P], swT[:, i, 0:LAT],
                          start=True, stop=True).then_inc(sq_pm, 1)
            pe.wait_ge(k_dup, 3 * NT + 1)
            pe.wait_ge(kv_ld, 48)
            pe.wait_ge(sq_rp, 8)
            for g in range(SKV):
                if g:
                    pe.wait_ge(k_cp, 2 * g)
                for t in range(NT + 1):
                    mm = pe.transpose(ps[:, t // 4, (t % 4) * P:(t % 4 + 1) * P],
                                      skr[:, t, g * 2 * HD:(g + 1) * 2 * HD], ident)
                mm.then_inc(k_tr, 1)
                pe.wait_ge(k_cp, 2 * g + 2)
                if g >= 2:
                    pe.wait_ge(k_rp, g - 1)
                pe.matmul(ps[:, 2 + g % 2, :], cst[:, C_PERM:C_PERM + P], skT[:, g, 0:LAT],
                          start=True, stop=True).then_inc(k_pm, 1)
            pe.wait_ge(k_rp, SKV)

            def scores(u):
                t, g = units[u]
                keys, _ = unit_keys(t)
                if u:
                    pe.wait_ge(sc_m, u)
                for j in range(GRP):
                    lo, ch = (j % 2) * HD, 2 * g + j // 2
                    at = 0
                    for a, n in keys:
                        mm = pe.matmul(ps[:, j, at:at + n], swT[lo:lo + HD, ch, t * P:(t + 1) * P],
                                       skT[lo:lo + HD, g, a:a + n], start=True, stop=True, skip_group_check=True)
                        at += n
                mm.then_inc(sc_pe, 1)

            n_pt = 0
            scores(0)
            for u, (t, g) in enumerate(units):
                if u + 1 < len(units):
                    scores(u + 1)
                _, blocks = unit_keys(t)
                pe.wait_ge(sc_n, u + 1)
                for i, _ in enumerate(blocks):
                    if n_pt >= 3:
                        pe.wait_ge(pt_cp, n_pt - 2)
                    for j in range(GRP):
                        mm = pe.transpose(ps[:, 4 + n_pt % 3, j * P:(j + 1) * P],
                                          Sbuf[:, u % 2, j * BANK + i * P:j * BANK + (i + 1) * P], ident)
                    mm.then_inc(pt_pe, 1)
                    n_pt += 1
                if u:
                    pe.wait_ge(pv_cp, u)
                for half in range(2):
                    lo = half * HD
                    for i, vt in enumerate(blocks):
                        pe.wait_ge(pt_cp, n_pt - len(blocks) + i + 1)
                        mm = pe.matmul(ps[lo:lo + HD, 7, 0:2 * P], svr[:, vt, g * HD:(g + 1) * HD],
                                       pT[:, u % 2, i * BANK:(i + 1) * BANK].rearrange(
                                           "p (c e q) -> p c e q", c=2, e=2)[:, :, half, :],
                                       start=(i == 0), stop=(i == len(blocks) - 1), skip_group_check=True)
                mm.then_inc(pv_pe, 1)
            pe.wait_ge(pv_cp, len(units))
            with pe.Fori(0, 4) as n:
                for q, (first, n_k) in enumerate(GATE_PIECES):
                    def bank_free(b):
                        if q == 0:
                            pe.wait_ge(gt_dve, n * 10 + (b + 1))
                        elif q == 2:
                            pe.wait_ge(gt_dve, n * 10 + (NT + b + 1))
                        else:
                            pe.wait_ge(gt_act, n * 10 + (5 * (q // 2) + b + 1))
                    product(P_GATE + first, n * 48, n_k, bank_free, gt_pe)
                for b in range(NT):
                    pe.wait_ge(gt_dve, n * 10 + (2 * NT + b + 1))
                    pe.wait_ge(mt_cp, n * NT + (1 if b < 3 else b - 1))
                    for q in range(4):
                        mm = pe.transpose(ps[:, 5 + b % 3, q * P:(q + 1) * P], mrow[:, b, q * P:(q + 1) * P], ident)
                    mm.then_inc(mt_pe, 1)
            pe.wait_ge(mt_cp, 4 * NT + 1)
            pe.wait_ge(gt_dve, 9 * NT)
            with pe.Fori(0, 4) as n:
                def bank_free(b):
                    pe.wait_ge(wo_ev, n * NT + (b + 1))
                product(P_OUT, n * KT, KT, bank_free, wo_pe)
            pe.wait_ge(wo_ev, 5 * NT)
            for t in range(NT):
                pe.wait_ge(n2_h, t + 1)
                if t:
                    pe.wait_ge(n2_cp, t)
                for k in range(KT):
                    mm = pe.transpose(ps[:, k // 4, (k % 4) * P:(k % 4 + 1) * P], h2row[:, k * P:(k + 1) * P], ident)
                mm.then_inc(n2_tr, 1)
                if t == 0:
                    pe.wait_ge(wo_ld, 16 * 10)
                pe.wait_ge(n2_cp, t + 1)
                for k in range(KT):
                    mm = pe.matmul(ps[:, 4, t * NE:(t + 1) * NE], h2T[:, k, :], wrt[:, k, :],
                                   start=(k == 0), stop=(k == KT - 1), skip_group_check=True)
                mm.then_inc(lg_pe, 1)
            pe.wait_ge(af_r, 1)
            for t in range(NT):
                mm = pe.transpose(ps[0:NE, 5 + t // 4, (t % 4) * P:(t % 4 + 1) * P], aff[:, 0, t, :], ident)
            mm.then_inc(af_tr, 1)
            pe.wait_ge(tk_d, 1)
            pe.transpose(ps[0:CAP, 7, 0:NE], idxf[0:NE, :], ident[0:NE, 0:NE])
            pe.transpose(ps[0:CAP, 7, NE:2 * NE], vals[0:NE, :], ident[0:NE, 0:NE]).then_inc(tk_tr, 1)

            def xs_transposes(bank1_free=None):
                v = xs[0:CAP, :].rearrange("r (p k) -> r k p", k=KT)
                for k in range(KT):
                    o = xs_bank(k)
                    if k == 12 and bank1_free is not None:
                        pe.wait_ge(hd_cp, bank1_free)
                    mm = pe.transpose(o, v[:, k, :], ident[0:CAP, 0:CAP])
                mm.then_inc(xs_tr, 1)

            def xs_bank(k):
                b, i = ((2, k) if k < 6 else (3, k - 6)) if k < 12 else (1, k - 12 + 2)
                return ps[:, b, i * CAP:(i + 1) * CAP]

            pe.wait_ge(xs_ld, 16)
            pe.wait_ge(af_cp, 1)
            xs_transposes()
            with pe.Fori(0, NE) as e:
                pe.wait_ge(xs_l, e + 1)
                for j in range(16):
                    g, up = j // 2, j % 2
                    s = j % SP
                    pe.wait_ge(piece_ready, e * EXP_G + (P_EXP + j + 1))
                    for kk in range(2):
                        k = 2 * g + kk
                        for x, w in ((0, 0), (0, 1), (1, 0)):
                            for n in range(2):
                                col = kk * FF + n * BANK
                                mm = pe.matmul(ps[0:CAP, 2 * up + n, :], xsT[:, x, k, :], spE[:, s, w, col:col + BANK],
                                               start=(k == 0 and x == w), stop=(k == KT - 1 and x == 1))
                    mm.then_inc(piece_used, 1)
                pe.wait_ge(hd_r, e + 1)
                v = hid[0:CAP, :].rearrange("r (p k) -> r k p", k=FT)
                for k in range(FT):
                    mm = pe.transpose(ps[:, k // 6, (k % 6) * CAP:(k % 6 + 1) * CAP], v[:, k, :], ident[0:CAP, 0:CAP])
                mm.then_inc(hd_tr, 1)
                pe.wait_ge(xs_ld, e * 16 + 32)
                xs_transposes(e + 1)
                pe.wait_ge(hd_cp, e + 1)
                pe.wait_ge(ye_r, e + 1)
                for k in range(FT):
                    s = (16 + k) % SP
                    pe.wait_ge(piece_ready, e * EXP_G + (P_EXP + 16 + k + 1))
                    for x, w in ((0, 0), (0, 1), (1, 0)):
                        for n in range(4):
                            mm = pe.matmul(ps[0:CAP, 4 + n, :], hidT[:, x, k, :], spE[:, s, w, n * BANK:(n + 1) * BANK],
                                           start=(k == 0 and x == w), stop=(k == FT - 1 and x == 1))
                    mm.then_inc(piece_used, 1)

        @block.scalar
        def _(act):
            ch = Chain(act, act_step)
            act.wait_ge(s_condT, 1)
            act.activation(condT[:, :, :].rearrange("p k w -> p w k"),
                           ps[:, 0, 0:2 * KT].rearrange("p (w k) -> p w k", w=2), ACT.Silu).then_inc(s_condS, 1)
            act.wait_ge(mod_st, 16)
            for t in range(NT):
                act.wait_ge(x_ld[t % 2], 16 * (t // 2 + 1))
                act.activation(junk, xrow[:, t % 2, :], ACT.Square, accum_out=stat[:, t:t + 1]).then_inc(act_step, 1)
                ch.n += 1
                act.wait_ge(act_step, ch.n)
                act.activation(stat[:, NT + t:NT + t + 1], stat[:, t:t + 1], ACT.Sqrt, scale=1.0 / D,
                               bias=epsb[:, :]).then_inc(h_sq, 1)
                for q in range(4):
                    act.wait_ge(h_tr, 4 * t + q + 1)
                    act.activation(hT[:, 4 * q:4 * q + 4, t * P:(t + 1) * P],
                                   ps[:, q, :].rearrange("p (k t) -> p k t", k=4), ACT.Copy).then_inc(h_cp, 1)
            gaw = ar[:, 27264:27264 + KT * 2 * RANK].rearrange("p (k n) -> p k n", k=KT)
            act.dma_start(gaw, w_in[:, :, COL_GA:COL_SQ]).then_inc(ga_w, 16)

            sp = Split(act, True)
            act.wait_ge(h_cp, 4 * NT)
            sp.chunk(0, 0, AHEAD)
            for i, dst in enumerate((gqT, gkT)):
                sp.chunk(i, AHEAD)
                sp.chunk(i + 1, 0, AHEAD)
                for b in range(4):
                    bank_done(act, pj_pe, i, b, P_A + KT * i + KT - 1)
                    act.activation(dst[:, b, 0:LAT], ps[:, b, :], ACT.Copy).then_inc(pj_ev, 1)
                bank_done(act, pj_pe, i, 4, P_A + KT * i + KT - 1)
                act.activation(dst[:, :, LAT:TOK], ps[:, 4, :].rearrange("p (c t) -> p c t", c=4), ACT.Copy)\
                    .then_inc(pj_ev, 1)
            for i in range(2):
                sp.chunk(2 + i, AHEAD)
                if i == 0:
                    sp.chunk(3, 0, AHEAD)
                for b in range(NT):
                    bank_done(act, pj_pe, 2 + i, b, P_A + KT * (2 + i) + KT - 1)
                    act.activation(gv[:, b, i * BANK:(i + 1) * BANK], ps[:, b, :], ACT.Copy).then_inc(pj_ev, 1)
            act.wait_ge(ga_pe, 1)
            act.wait_ge(wdec0, 1)
            act.activation(gaT[0:2 * RANK, 0:LAT], ps[0:2 * RANK, 5, :], ACT.Copy).then_inc(ga_ev, 1)
            act.activation(gaT[0:2 * RANK, LAT:TOK], ps[0:2 * RANK, 6, 0:CTX], ACT.Copy).then_inc(ga_ev, 1)
            for s in range(2 * GH):
                dr = s % 2
                act.wait_ge(z_pe, s + 1)
                if s:
                    act.wait_ge(g_b, s)
                act.activation(tz[:, 0:LAT], ps[:, 0, :], ACT.Abs)
                act.activation(tz[:, LAT:TOK], ps[:, 1, 0:CTX], ACT.Abs).then_inc(z_ab, 1)
                act.wait_ge(z_ab, s + 1)
                ch.step(act.activation(tz, tz, ACT.Exp, scale=-1.0))
                act.activation(tz, tz, ACT.Ln, bias=1.0).then_inc(z_ln, 1)
                act.wait_ge(g_b, s + 1)
                if s:
                    act.wait_ge(o_pe, NT * s)
                act.activation(xq, tB, ACT.Exp, scale=1.0 / TAU)
                act.activation(xk, tB, ACT.Exp, scale=-1.0 / TAU)
                act.activation(tD, tD, ACT.Exp, scale=1.0 / TAU)
                act.activation(decay[:, :], tc.rearrange("p (c t) -> p c t", t=CH)[:, :, CH - 1], ACT.Exp,
                               scale=1.0 / TAU).then_inc(g_e, 1)
                act.wait_ge(kt_pe, s + 1)
                if s:
                    act.wait_ge(u_pe, 9 * s)
                act.activation(ks[:, 0:LAT], ps[:, 2, :], ACT.Copy)
                act.activation(ks[:, LAT:TOK], ps[:, 3, 0:P], ACT.Copy).then_inc(kt_cp, 1)
                if dr:
                    h = s // 2
                    act.wait_ge(o_ev, NT * (s + 1))
                    for t in range(NT):
                        if h or t:
                            pass
                        ch.step(act.activation(tz[:, 0:GV], og[:, t, h * GV:(h + 1) * GV], ACT.Square,
                                               accum_out=rs_gla[:, t * GH + h:t * GH + h + 1]))
            act.activation(rs_gla[:, :], rs_gla[:, :], ACT.Sqrt, scale=1.0 / GV, bias=epsb[:, :]).then_inc(o_sq, 1)
            act.wait_ge(st_out, 16 * 2 * GH)
            sp.chunk(4, 0, AHEAD)
            for c in range(2):
                sp.chunk(4 + c, AHEAD)
                sp.chunk(5 + c, 0, AHEAD)
                for b in range(NT):
                    n = c * NT + b
                    bank_done(act, pj_pe, 4 + c, b, P_A + KT * (4 + c) + KT - 1)
                    if n >= 2:
                        act.wait_ge(gr_o, n - 1)
                    act.activation(sil[:, n % 2, :], ps[:, b, :], ACT.Silu).then_inc(pj_ev, 1)
                for b in range(NT):
                    n = c * NT + b
                    act.wait_ge(gr_tr, n + 1)
                    act.activation(oT[:, 4 * c:4 * c + 4, b * P:(b + 1) * P],
                                   ps[:, 5 + b % 2, :].rearrange("p (k t) -> p k t", k=4), ACT.Copy).then_inc(gr_cp, 1)
            for i in range(2):
                sp.chunk(6 + i, AHEAD)
                sp.chunk(7 + i, 0, AHEAD)
                for b in range(4):
                    bank_done(act, pj_pe, 6 + i, b, P_A + KT * (6 + i) + KT - 1)
                    act.activation(swT[:, 4 * i + b, 0:LAT], ps[:, b, :], ACT.Copy).then_inc(pj_ev, 1)
                bank_done(act, pj_pe, 6 + i, 4, P_A + KT * (6 + i) + KT - 1)
                act.activation(swT[:, 4 * i:4 * i + 4, LAT:TOK], ps[:, 4, :].rearrange("p (c t) -> p c t", c=4),
                               ACT.Copy).then_inc(pj_ev, 1)
            sp.chunk(8, AHEAD)
            for b in range(NT):
                bank_done(act, pj_pe, 8, b, P_A + KT * 8 + KT - 1)
                kd = skr[:, b, :].rearrange("p (h e d) -> p h e d", h=SKV, e=2)
                kp = ps[:, b, 0:SKV * HD].rearrange("p (h d) -> p h d", h=SKV)
                act.activation(kd[:, :, 0, :], kp, ACT.Copy).then_inc(k_dup, 1)
                act.activation(kd[:, :, 1, :], kp, ACT.Copy).then_inc(k_dup, 1)
                if b == NT - 1:
                    act.activation(krow_out, ps[:, b, 0:SKV * HD], ACT.Copy).then_inc(k_dup, 1)
                act.activation(svr[:, b, :], ps[:, b, SKV * HD:2 * SKV * HD], ACT.Copy).then_inc(k_dup, 1)
            for g in range(SKV):
                act.wait_ge(k_tr, g + 1)
                act.activation(skT[:, g, 0:LAT], ps[:, 0, :], ACT.Copy).then_inc(k_cp, 1)
                act.activation(skT[:, g, LAT:TOK + P], ps[:, 1, 0:2 * P], ACT.Copy).then_inc(k_cp, 1)
            n_pt = 0
            for u, (t, g) in enumerate(units):
                keys, blocks = unit_keys(t)
                act.wait_ge(sc_mx, u + 1)
                sf = soft[:, u % 2]
                act.activation(sf[:, 3, :], sf[:, 3, :], ACT.Exp)
                for j in range(GRP):
                    s = Sbuf[:, u % 2, j * BANK:j * BANK + len(blocks) * P]
                    a = act.activation(s, s, ACT.Exp, bias=sf[:, 1, j:j + 1], accum_out=sf[:, 2, j:j + 1])
                a.then_inc(sc_e, 1)
                if u:
                    n_pt = copy_pT(act, u - 1, n_pt)
                    copy_o(act, u - 1)
            n_pt = copy_pT(act, len(units) - 1, n_pt)
            copy_o(act, len(units) - 1)
            with act.Fori(0, 4) as n:
                gate_split(sp, n, 0, 0, KT)
                for q in (0, 2):
                    gate_split(sp, n, q + 1, 0, AHEAD)
                    for b in range(NT):
                        bank_done(act, gt_pe, n * 4 + q, b, n * 48 + (P_GATE + sum(GATE_PIECES[q]) - 1))
                        act.activation(sg[:, b, :], ps[:, b, :], ACT.Sigmoid).then_inc(gt_act, 1)
                    gate_split(sp, n, q + 1, AHEAD, 8)
                    if q == 0:
                        gate_split(sp, n, 2, 0, KT)
                act.wait_ge(mT_free, n + 1)
                for b in range(NT):
                    act.wait_ge(mt_pe, n * NT + (b + 1))
                    act.activation(mTc[:, :, b * P:(b + 1) * P],
                                   ps[:, 5 + b % 3, :].rearrange("p (k t) -> p k t", k=4), ACT.Copy).then_inc(mt_cp, 1)
            act.wait_ge(mT_ld, 16)
            with act.Fori(0, 4) as n:
                sp.pieces(P_OUT, n * KT, G_OUT, n, hT, 0, KT)
            for t in range(NT):
                act.wait_ge(wo_ev, 4 * NT + t + 1)
                ch.step(act.activation(junkx, x1[:, t, :], ACT.Square, accum_out=stat[:, t:t + 1]))
                act.activation(stat[:, NT + t:NT + t + 1], stat[:, t:t + 1], ACT.Sqrt, scale=1.0 / D,
                               bias=epsb[:, :]).then_inc(n2_sq, 1)
                act.wait_ge(n2_tr, t + 1)
                if t:
                    act.wait_ge(lg_pe, t)
                act.activation(h2T, ps[:, 0:4, :].rearrange("p b (k t) -> p (b k) t", k=4), ACT.Copy).then_inc(n2_cp, 1)
            act.wait_ge(af_e, 1)
            act.activation(aff[:, 0], aff[:, 0], ACT.Exp).then_inc(af_e, 1)

            def copy_xs():
                for dst, src in xs_parts:
                    a = act.activation(xsT[:, 0, dst:dst + src.shape[1], :], src, ACT.Copy)
                a.then_inc(xs_h, 1)

            def split_expert(e, lo, hi):
                for j in range(lo, hi):
                    s = j % SP
                    act.wait_ge(slot_ready[s], e * 96 + 16 * ((G_EXP + j) // SLOTS + 1))
                    act.wait_ge(piece_used, e * EXP_G + (P_EXP + j + 1))
                    act.activation(spE[:, s, 0, :], ring[:, s, :], ACT.Copy).then_inc(piece_high, 1)

            act.wait_ge(xs_tr, 1)
            copy_xs()
            split_expert(0, 0, AHEAD)

            def expert_act(e, last):
                split_expert(e, AHEAD, 19)
                act.wait_ge(piece_used, e * EXP_G + (SP + P_EXP + 16))
                act.activation(silx[0:CAP, :], ps[0:CAP, 0:2, :].rearrange("p b n -> p (b n)"), ACT.Silu).then_inc(hd_s, 1)
                act.wait_ge(hd_tr, e + 1)
                for dst, src in hid_parts:
                    a = act.activation(hidT[:, 0, dst:dst + src.shape[1], :], src, ACT.Copy)
                a.then_inc(hd_h, 1)
                act.wait_ge(xs_tr, e + 2)
                copy_xs()
                split_expert(e, 19, EXP_G)
                if not last:
                    split_expert(e + 1, 0, AHEAD)

            with act.Fori(0, NE - 1) as e:
                expert_act(e, False)
            expert_act(NE - 1, True)
            for t in range(NT):
                act.wait_ge(y_ld[t % 2], 16 * (t // 2 + 1))
                ch.step(act.activation(junk2, yrow[:, t % 2, :], ACT.Square, accum_out=stat[:, t:t + 1]))
                act.activation(stat[:, NT + t:NT + t + 1], stat[:, t:t + 1], ACT.Sqrt, scale=1.0 / D,
                               bias=epsb[:, :]).then_inc(y_sq, 1)

        @block.vector
        def _(dve):
            ch = Chain(dve, dve_step)
            dve.memset(epsb[:, :], EPS).then_inc(s_condS, 1)
            dve.sem_inc(mod_ev, 1)
            dve.sem_inc(pj_ev, NT)
            dve.sem_inc(gt_dve, NT)
            dve.sem_inc(wo_ev, NT)
            dve.sem_inc(gr_cp, 2)
            dve.sem_inc(mt_cp, 1)
            dve.sem_inc(mT_free, 1)
            dve.sem_inc(ye_free, 1)
            dve.sem_inc(ye_r, 1)
            dve.wait_ge(s_cst, 80)
            with dve.Fori(0, 6) as m:
                dve.wait_ge(slot_used, m * KT + (SLOTS + G_MOD + KT))
                dve.tensor_tensor(modrow[0:2, ds(m * D, D)], ps[0:2, 0:4, :].rearrange("p b n -> p (b n)"),
                                  bmod[0:2, ds(m * D, D)], ALU.add).then_inc(mod_ev, 1)
            dve.wait_ge(mod_ab, 80)
            for who in range(2):
                a = dve.scalar_tensor_tensor(Ah[:, who, :], Ah[:, who, :], 1.0, g1, ALU.add, ALU.mult)
            ch.step(a)
            for t in range(NT):
                who = t // 4
                dve.wait_ge(h_sq, t + 1)
                if t >= 2:
                    dve.wait_ge(h_tr, 4 * (t - 1))
                ch.step(dve.reciprocal(stat[:, NT + t:NT + t + 1], stat[:, NT + t:NT + t + 1]))
                ch.step(dve.scalar_tensor_tensor(hrow[:, t % 2, :], xrow[:, t % 2, :], stat[:, NT + t:NT + t + 1],
                                                 Ah[:, who, :], ALU.mult, ALU.mult))
                dve.tensor_tensor(hrow[:, t % 2, :], hrow[:, t % 2, :], Bh[:, who, :], ALU.add).then_inc(h_row, 1)
            sp = Split(dve, False)
            dve.wait_ge(h_tr, 4 * NT)
            dve.memset(gaT[2 * RANK:2 * RANK + 1, :], 1.0)
            dve.memset(wdec[0:2 * RANK + 1, :, :], 0.0).then_inc(wdec0, 1)
            for i in range(4):
                sp.chunk(i)
            dve.wait_ge(ga_pe, 1)
            ch.step(dve.memset(aTm, 0.0))
            for s in range(2 * GH):
                h, dr = s // 2, s % 2
                dve.wait_ge(z_ab, s + 1)
                dve.tensor_scalar(tg[:, 0:LAT], ps[:, 0, :], 0.0, None, ALU.min)
                ch.step(dve.tensor_scalar(tg[:, LAT:TOK], ps[:, 1, 0:CTX], 0.0, None, ALU.min))
                dve.wait_ge(z_ln, s + 1)
                ch.step(dve.tensor_tensor(tg, tg, tz, ALU.subtract))
                if s:
                    dve.wait_ge(g_e, s)
                ch.step(dve.tensor_tensor_scan(tc, cst[:, C_RST:C_RST + TOK], tg, 0.0, ALU.mult, ALU.add))
                c3 = tc.rearrange("p (c t) -> p c t", t=CH)
                total = c3[:, :, CH - 1:CH].to_broadcast([P, NCH, CH])
                if s:
                    dve.wait_ge(kt_pe, s)
                if dr:
                    dve.tensor_tensor(tD, tc, tg, ALU.subtract)
                    ch.step(dve.tensor_tensor(tB.rearrange("p (c t) -> p c t", t=CH), total, c3, ALU.subtract))
                    dve.tensor_tensor(tB, tB, tg, ALU.add).then_inc(g_b, 1)
                else:
                    dve.tensor_tensor(tD.rearrange("p (c t) -> p c t", t=CH), total, c3, ALU.subtract)
                    dve.tensor_copy(tB, tc).then_inc(g_b, 1)
                dve.wait_ge(g_e, s + 1)
                dve.scalar_tensor_tensor(xq, gqT[:, h, :], float(GK) ** -0.5, xq, ALU.mult, ALU.mult)
                dve.tensor_tensor(xk, gkT[:, h, :], xk, ALU.mult)
                dve.tensor_tensor(tD, gkT[:, h, :], tD, ALU.mult).then_inc(g_m, 1)
                dve.wait_ge(at_pe, s + 1)
                mask = cst[:, C_MB if dr else C_MF:][:, 0:P].bitcast(I32)
                if s >= 2:
                    dve.wait_ge(o_pe, NT * (s - 1))
                for t in range(NT):
                    src = ps[:, 4, t * P:(t + 1) * P] if t < 4 else ps[:, 1, P:2 * P]
                    a = dve.copy_predicated(aTm[:, dr, t * P:(t + 1) * P], mask, src)
                a.then_inc(at_cp, 1)
                order = ([9, 8] if dr else [8, 9]) + (list(range(7, 0, -1)) if dr else list(range(7)))
                if s >= 2:
                    dve.wait_ge(st_out, 16 * (s - 1))
                    dve.wait_ge(o_pe, NT * (s - 1))
                dve.wait_ge(st_ld[dr], 16 * (h + 1))
                for u, c in enumerate(order):
                    bank, half, made, _ = U_PLACE[u]
                    U = ps[:, bank, half * GV:(half + 1) * GV]
                    dve.wait_ge(u_pe, 9 * s + made)
                    if u == 0:
                        dve.tensor_copy(st[:, dr, 8, :], U).then_inc(s_up, 1)
                        dve.wait_ge(s_up, 9 * s + 1)
                        continue
                    src, dst = (8, 9) if u == 1 else (u - 2, u - 1)
                    dve.scalar_tensor_tensor(st[:, dr, dst, :], st[:, dr, src, :], decay[:, c:c + 1], U,
                                             ALU.mult, ALU.add).then_inc(s_up, 1)
                    dve.wait_ge(s_up, 9 * s + u + 1)
                for i, t in enumerate([4, 3, 2, 1, 0] if dr else [4, 0, 1, 2, 3]):
                    src = ps[:, t, 0:GV]
                    dst = og[:, t, h * GV:(h + 1) * GV]
                    dve.wait_ge(o_pe, NT * s + i + 1)
                    if dr:
                        dve.tensor_tensor(dst, dst, src, ALU.add).then_inc(o_ev, 1)
                    else:
                        dve.tensor_copy(dst, src).then_inc(o_ev, 1)
                if dr == 0:
                    dve.wait_ge(o_ev, NT * (s + 1))
            dve.wait_ge(o_sq, 1)
            ch.step(dve.reciprocal(rs_gla[:, :], rs_gla[:, :]))
            sp.chunk(4, 0, AHEAD)
            for c in range(2):
                sp.chunk(4 + c, AHEAD)
                sp.chunk(5 + c, 0, AHEAD)
                for b in range(NT):
                    n = c * NT + b
                    dve.wait_ge(pj_ev, NT * (5 + c) + b + 1)
                    if n >= 2:
                        dve.wait_ge(gr_tr, n - 1 + (b == 0))
                    o = onr[:, b % 2, :]
                    for hh in range(2):
                        h = 2 * c + hh
                        a = dve.scalar_tensor_tensor(o[:, hh * GV:(hh + 1) * GV], og[:, b, h * GV:(h + 1) * GV],
                                                     rs_gla[:, b * GH + h:b * GH + h + 1],
                                                     glag[:, h * GV:(h + 1) * GV], ALU.mult, ALU.mult)
                    ch.step(a)
                    dve.tensor_tensor(o, o, sil[:, n % 2, :], ALU.mult).then_inc(gr_o, 1)
            sp.chunk(6, AHEAD)
            sp.chunk(7)
            sp.chunk(8)
            for i in range(8):
                dve.wait_ge(pj_ev, NT * (7 + i // 4) + i % 4 + 1)
                if i >= 1:
                    dve.wait_ge(sq_rp, i)
                ch.step(dve.tensor_tensor(rp[:, 0, :], swT[:, i, 0:LAT], cst[:, C_COS:C_COS + LAT], ALU.mult))
                dve.wait_ge(sq_pm, i + 1)
                ch.step(dve.tensor_tensor(rp[:, 1, :], ps[:, 5 + i % 2, :], cst[:, C_SIN:C_SIN + LAT], ALU.mult))
                dve.tensor_tensor(swT[:, i, 0:LAT], rp[:, 0, :], rp[:, 1, :], ALU.add).then_inc(sq_rp, 1)
            for g in range(SKV):
                dve.wait_ge(k_cp, 2 * g + 2)
                if g:
                    dve.wait_ge(k_rp, g)
                else:
                    dve.wait_ge(sq_rp, 8)
                ch.step(dve.tensor_tensor(rp[:, 0, :], skT[:, g, 0:LAT], cst[:, C_COS:C_COS + LAT], ALU.mult))
                dve.wait_ge(k_pm, g + 1)
                ch.step(dve.tensor_tensor(rp[:, 1, :], ps[:, 2 + g % 2, :], cst[:, C_SIN:C_SIN + LAT], ALU.mult))
                dve.tensor_tensor(skT[:, g, 0:LAT], rp[:, 0, :], rp[:, 1, :], ALU.add).then_inc(k_rp, 1)

            def softmax_front(u):
                t, g = units[u]
                _, blocks = unit_keys(t)
                nk = len(blocks) * P
                S = Sbuf[:, u % 2, :].rearrange("p (j n) -> p j n", j=GRP)[:, :, 0:nk]
                sf = soft[:, u % 2]
                dve.wait_ge(sc_pe, u + 1)
                if u >= 2:
                    dve.wait_ge(pt_pe, sum(len(unit_keys(units[v][0])[1]) for v in range(u - 1)))
                src = ps[:, 0:GRP, 0:nk]
                if t == 4:
                    dve.tensor_scalar(S, src, HD ** -0.5, None, ALU.mult).then_inc(sc_m, 1)
                else:
                    lo = {0: C_SW + P, 3: C_SW3}.get(t, C_SW)
                    m = cst[:, lo:lo + nk].unsqueeze(1).to_broadcast([P, GRP, nk])
                    dve.scalar_tensor_tensor(S, src, HD ** -0.5, m, ALU.mult, ALU.add).then_inc(sc_m, 1)
                dve.wait_ge(sc_m, u + 1)
                ch.step(dve.tensor_reduce(sf[:, 0, :], S, AX.X, ALU.max))
                ch.step(dve.tensor_tensor(sf[:, 0, :], sf[:, 0, :], sink[:, GRP * g:GRP * g + GRP], ALU.max))
                dve.tensor_tensor(sf[:, 3, :], sink[:, GRP * g:GRP * g + GRP], sf[:, 0, :], ALU.subtract)
                dve.tensor_scalar(sf[:, 1, :], sf[:, 0, :], -1.0, None, ALU.mult).then_inc(sc_mx, 1)

            def softmax_back(u):
                t, g = units[u]
                nk = len(unit_keys(t)[1]) * P
                sf = soft[:, u % 2]
                dve.wait_ge(sc_e, u + 1)
                ch.step(dve.tensor_tensor(sf[:, 2, :], sf[:, 2, :], sf[:, 3, :], ALU.add))
                ch.step(dve.reciprocal(sf[:, 4, :], sf[:, 2, :]))
                for j in range(GRP):
                    s = Sbuf[:, u % 2, j * BANK:j * BANK + nk]
                    a = dve.tensor_scalar(s, s, sf[:, 4, j:j + 1], None, ALU.mult)
                a.then_inc(sc_n, 1)

            softmax_front(0)
            for u in range(len(units)):
                if u + 1 < len(units):
                    softmax_front(u + 1)
                softmax_back(u)
            dve.wait_ge(kv_st, 32)
            ch2 = Chain(dve, dve2_step)
            with dve.Fori(0, 4) as n:
                ch2.enter(n, NT)
                gate_split(sp, n, 0, 0, KT)
                gate_split(sp, n, 1, 0, 8)
                gate_split(sp, n, 2, 0, AHEAD)
                for b in range(NT):
                    bank_done(dve, gt_pe, n * 4 + 1, b, n * 48 + (P_GATE + sum(GATE_PIECES[1]) - 1))
                    dve.wait_ge(gt_act, n * 10 + (b + 1))
                    dve.tensor_tensor(mrow[:, b, :], ps[:, b, :], sg[:, b, :], ALU.mult).then_inc(gt_dve, 1)
                gate_split(sp, n, 2, AHEAD, KT)
                gate_split(sp, n, 3, 0, 8)
                for b in range(NT):
                    bank_done(dve, gt_pe, n * 4 + 3, b, n * 48 + (P_GATE + sum(GATE_PIECES[3]) - 1))
                    dve.wait_ge(gt_act, n * 10 + (NT + b + 1))
                    dve.wait_ge(gt_dve, n * 10 + (2 * NT + b))
                    ch2.step(dve.tensor_tensor(mtmp, ps[:, b, :], sg[:, b, :], ALU.mult))
                    dve.tensor_tensor(mrow[:, b, :], mrow[:, b, :], mtmp, ALU.add).then_inc(gt_dve, 1)
                ch2.leave(4)
            with dve.Fori(0, 4) as n:
                ch2.enter(n, NT)
                sp.pieces(P_OUT, n * KT, G_OUT, n, hT, 0, KT)
                dve.wait_ge(wo_ld, 16 * 2)
                dve.wait_ge(xr_ld, 16 * NT)
                for b in range(NT):
                    who = b // 4
                    bank_done(dve, wo_pe, n, b, n * KT + (P_OUT + KT - 1))
                    dve.wait_ge(wo_ev, n * NT + (NT + b))
                    ch2.step(dve.tensor_tensor(wtmp[:, b % 2, :], ps[:, b, :], gt1[:, who, ds(n * BANK, BANK)], ALU.mult))
                    xv = x1[:, b, ds(n * BANK, BANK)]
                    dve.tensor_tensor(xv, xv, wtmp[:, b % 2, :], ALU.add).then_inc(wo_ev, 1)
                ch2.leave(4)
            dve.wait_ge(wo_ld, 16 * 10)
            for who in range(2):
                a = dve.scalar_tensor_tensor(A2[:, who, :], A2[:, who, :], 1.0, g2, ALU.add, ALU.mult)
            ch.step(a)
            for t in range(NT):
                who = t // 4
                dve.wait_ge(n2_sq, t + 1)
                ch.step(dve.reciprocal(stat[:, NT + t:NT + t + 1], stat[:, NT + t:NT + t + 1]))
                if t:
                    dve.wait_ge(n2_tr, t)
                    dve.wait_ge(n2_st, 16 * t)
                ch.step(dve.scalar_tensor_tensor(h2row, x1[:, t, :], stat[:, NT + t:NT + t + 1], A2[:, who, :],
                                                 ALU.mult, ALU.mult))
                dve.tensor_tensor(h2row, h2row, B2[:, who, :], ALU.add).then_inc(n2_h, 1)
            a0, a1 = aff[:, 0], aff[:, 1]
            dve.wait_ge(lg_pe, NT)
            lg = ps[:, 4, 0:NT * NE].rearrange("p (t e) -> p t e", t=NT)
            ch.step(dve.tensor_reduce(a1[:, :, 0], lg, AX.X, ALU.max))
            dve.tensor_tensor(a0, lg, a1[:, :, 0:1].to_broadcast([P, NT, NE]), ALU.subtract).then_inc(af_e, 1)
            dve.wait_ge(af_e, 2)
            ch.step(dve.tensor_reduce(a1[:, :, 1], a0, AX.X, ALU.add))
            ch.step(dve.reciprocal(a1[:, :, 2], a1[:, :, 1]))
            dve.tensor_tensor(a0, a0, a1[:, :, 2:3].to_broadcast([P, NT, NE]), ALU.mult).then_inc(af_r, 1)
            dve.wait_ge(af_tr, 1)
            dve.tensor_copy(affT[0:NE, 0:LAT], ps[0:NE, 5, :])
            dve.tensor_copy(affT[0:NE, LAT:TOK], ps[0:NE, 6, 0:CTX]).then_inc(af_cp, 1)
            dve.wait_ge(af_cp, 1)
            for lo, n, at, cap in ((0, LAT, 0, CAP_L), (LAT, CTX, CAP_L, CAP_C)):
                a = affT[0:NE, lo:lo + n]
                for r in range(cap // 8):
                    v = vals[0:NE, at + 8 * r:at + 8 * r + 8]
                    ch.step(dve.max(v, a))
                    dve.max_index(idxu[0:NE, at + 8 * r:at + 8 * r + 8], v, a)
                    ch.step(dve.match_replace(a, v, a, -1.0))
            dve.tensor_copy(idxf[0:NE, 0:CAP_L], idxu[0:NE, 0:CAP_L])
            dve.tensor_scalar(idxf[0:NE, CAP_L:CAP], idxu[0:NE, CAP_L:CAP], float(LAT), None, ALU.add).then_inc(tk_d, 1)
            dve.wait_ge(tk_tr, 1)
            dve.tensor_copy(idxT[0:CAP, 0:NE], ps[0:CAP, 7, 0:NE]).then_inc(tk_cp, 1)
            dve.tensor_copy(idxT[0:CAP, NE:NE + 2], ps[0:CAP, 7, 0:2]).then_inc(tk_cp, 1)
            dve.tensor_copy(gateT[0:CAP, :], ps[0:CAP, 7, NE:2 * NE]).then_inc(tk_cp, 1)
            def low_xs():
                for dst, src in xs_parts:
                    n = src.shape[1]
                    a = dve.tensor_tensor(xsT[:, 1, dst:dst + n, :], src, xsT[:, 0, dst:dst + n, :].bitcast(F32),
                                          ALU.subtract)
                a.then_inc(xs_l, 1)

            def low_expert(e, lo, hi):
                for j in range(lo, hi):
                    s = j % SP
                    dve.wait_ge(piece_high, e * EXP_G + (P_EXP + j + 1))
                    dve.tensor_tensor(spE[:, s, 1, :], ring[:, s, :], spE[:, s, 0, :].bitcast(F32), ALU.subtract)\
                       .then_inc(piece_ready, 1)

            dve.wait_ge(xs_h, 1)
            low_xs()
            low_expert(0, 0, AHEAD)

            def expert_dve(e, last):
                low_expert(e, AHEAD, 19)
                dve.wait_ge(hd_s, e + 1)
                dve.tensor_tensor(hid[0:CAP, :], silx[0:CAP, :], ps[0:CAP, 2:4, :].rearrange("p b n -> p (b n)"),
                                  ALU.mult).then_inc(hd_r, 1)
                dve.wait_ge(hd_h, e + 1)
                for dst, src in hid_parts:
                    n = src.shape[1]
                    a = dve.tensor_tensor(hidT[:, 1, dst:dst + n, :], src, hidT[:, 0, dst:dst + n, :].bitcast(F32),
                                          ALU.subtract)
                a.then_inc(hd_cp, 1)
                dve.wait_ge(xs_h, e + 2)
                low_xs()
                low_expert(e, 19, EXP_G)
                if not last:
                    low_expert(e + 1, 0, AHEAD)
                dve.wait_ge(piece_used, e * EXP_G + (SP + P_EXP + EXP_G))
                dve.wait_ge(ye_free, e + 1)
                dve.scalar_tensor_tensor(ye[0:CAP, :], ps[0:CAP, 4:8, :].rearrange("p b n -> p (b n)"),
                                         gateT[0:CAP, ds(e, 1)], gt2[0:CAP, :], ALU.mult, ALU.mult).then_inc(ye_r, 1)

            with dve.Fori(0, NE - 1) as e:
                expert_dve(e, False)
            expert_dve(NE - 1, True)
            dve.wait_ge(gf_ld, 16)
            for t in range(NT):
                dve.wait_ge(y_sq, t + 1)
                ch.step(dve.reciprocal(stat[:, NT + t:NT + t + 1], stat[:, NT + t:NT + t + 1]))
                y = yrow[:, t % 2, :]
                dve.scalar_tensor_tensor(y, y, stat[:, NT + t:NT + t + 1], gfin, ALU.mult, ALU.mult).then_inc(y_r, 1)


INS = ["x_prompt", "x_sample", "state_gla_fwd", "state_gla_bwd", "cache_k", "cache_v", "c", "c_ctx", "w_mod", "b_mod",
       "g_norm1", "w_in", "w_dec_f", "b_dec_f", "w_dec_b", "b_dec_b", "g_gla", "attn_sink", "w_branch_a",
       "w_branch_b", "w_out", "g_norm2", "w_router", "w_exp_gate", "w_exp_up", "w_exp_down", "g_final"]
OUTS = [("y_prompt", (1, CTX, D)), ("y_sample", (1, LAT, D)), ("ns_fwd", (1, 1, GH, GK, GV)),
        ("ns_bwd", (1, 1, GH, GK, GV)), ("nk", (1, 1, CTX, SKV, HD)), ("nv", (1, 1, CTX, SKV, HD))]


def kernel(**inputs):
    import concourse.bacc as bacc
    from concourse.bass_utils import run_bass_kernel_spmd

    nc = bacc.Bacc("TRN2", target_bir_lowering=False, num_devices=1)
    arrays = {name: np.ascontiguousarray(inputs[name]) for name in INS}
    arrays["consts"] = constants()
    T = {name: nc.dram_tensor(name, a.shape, F32, kind="ExternalInput").ap() for name, a in arrays.items()}
    for name, shape in OUTS:
        T[name] = nc.dram_tensor(name, shape, F32, kind="ExternalOutput").ap()
    build(nc, T)
    r = run_bass_kernel_spmd(nc, [arrays], core_ids=[0])
    return tuple(r.results[0][name] for name, _ in OUTS)
```

```python
from contextlib import ExitStack

import numpy as np

import concourse.bass as bass
from concourse import mybir

F32 = mybir.dt.float32
F32R = mybir.dt.float32r
I32 = mybir.dt.int32
U32 = mybir.dt.uint32
ALU = mybir.AluOpType
ACT = mybir.ActivationFunctionType
AX = mybir.AxisListType
ds = bass.ds

P = 128
D = 2048
KT = D // P
LAT, CTX = 512, 128
TOK = LAT + CTX
NT = TOK // P
EPS = 1e-6
BANK = 512

GH, GK, GV, RANK = 4, 128, 256, 16
TAU = 16.0
CH = 64
NCH = TOK // CH
LCH = LAT // CH

SH, SKV, HD = 16, 4, 64
GRP = SH // SKV

NE, FF = 16, 1024
FT = FF // P
CAP_L = 2 * LAT // NE
CAP_C = 2 * CTX // NE
CAP = CAP_L + CAP_C

COL_GV = 2 * GH * GK
COL_GR = COL_GV + GH * GV
COL_GA = COL_GR + GH * GV
COL_SQ = COL_GA + 2 * RANK
COL_SKV = COL_SQ + SH * HD
COL_GATE_A = COL_SKV + 2 * SKV * HD
COL_GATE_B = COL_GATE_A + D

SLOTS = 4
SLOT = 2048

G_MOD = 0
G_A = G_MOD + 2 * KT
G_M2 = G_A + 4 * 4
G_A2 = G_M2 + 8 * 4
G_M3 = G_A2 + 5 * 4
G_GATE = G_M3 + 8 * 4
G_OUT = G_GATE + 4 * 12
G_EXP = G_OUT + 4 * 4
EXP_G = 3 * 8
ESLOTS = 8

TA, TB = 3 * P, TOK - 3 * P

SP = 4
AHEAD = 3
P_A = 0
P_GATE = P_A + 9 * KT
P_OUT = P_GATE + 4 * 48
GATE_PIECES = ((0, KT), (KT, 8), (KT + 8, KT), (2 * KT + 8, 8))
P_EXP = P_OUT + 4 * KT
P_END = P_EXP + NE * EXP_G

C_ID, C_MF, C_MB, C_RST, C_SW, C_SW3, C_COS, C_SIN, C_PERM = np.cumsum(
    [0, 128, 128, 128, 640, 512, 384, 512, 512]).tolist()
C_END = C_PERM + 128


def constants():
    c = np.zeros((P, C_END), np.float32)
    i = np.arange(P)
    c[:, C_ID:C_ID + P] = np.eye(P)
    same = i[:, None] // CH == i[None, :] // CH
    c[:, C_MF:C_MF + P] = same & (i[:, None] <= i[None, :])
    c[:, C_MB:C_MB + P] = same & (i[:, None] >= i[None, :])
    c[:, C_RST:C_RST + TOK] = (np.arange(TOK) % CH != 0)[None, :]
    before = np.where(i[None, :] >= i[:, None], 0.0, -1e30)
    after = np.where(i[None, :] <= i[:, None], 0.0, -1e30)
    c[:, C_SW:C_SW + P] = before
    c[:, C_SW + 2 * P:C_SW + 3 * P] = after
    c[:, C_SW3:C_SW3 + P] = before
    npair = HD // 4
    inv = (np.float32(10000.0) ** (-np.arange(npair, dtype=np.float32) / np.float32(npair))).astype(np.float32)
    tok = np.arange(LAT)
    d = i % HD
    pos = np.where((d < HD // 2)[:, None], (tok // 64)[None, :], (tok % 64)[None, :]).astype(np.float32)
    ang = pos * inv[d % npair][:, None]
    c[:, C_COS:C_COS + LAT] = np.cos(ang)
    c[:, C_SIN:C_SIN + LAT] = np.sin(ang)
    for m in range(P):
        if m % (2 * npair) < npair:
            c[m + npair, C_PERM + m] = -1.0
        else:
            c[m - npair, C_PERM + m] = 1.0
    return c


U_PLACE = [(5, 0, 3, 0), (6, 0, 4, 0), (5, 1, 3, 0), (6, 1, 4, 0), (5, 0, 7, 3), (6, 0, 8, 4), (5, 1, 7, 3),
           (6, 1, 8, 4), (5, 0, 9, 7)]


class Chain:

    def __init__(self, eng, sem):
        self.eng, self.sem, self.base, self.n = eng, sem, 0, 0

    def step(self, ins):
        ins.then_inc(self.sem, 1)
        self.n += 1
        self.eng.wait_ge(self.sem, self.base + self.n)

    def enter(self, i, per):
        self.start = self.n
        self.base = i * per
        self.per = per

    def leave(self, count):
        assert self.n - self.start == self.per, (self.n - self.start, self.per)
        self.n = self.start + count * self.per
        self.base = 0


def build(nc, T):
    w_mod = T["w_mod"][0].rearrange("(k p) n -> p k n", p=P)
    w_in = T["w_in"][0].rearrange("(k p) n -> p k n", p=P)
    w_a = T["w_branch_a"][0].rearrange("(k p) n -> p k n", p=P)
    w_b = T["w_branch_b"][0].rearrange("(k p) n -> p k n", p=P)
    w_out = T["w_out"][0].rearrange("(k p) n -> p k n", p=P)
    w_eg = T["w_exp_gate"][0].rearrange("e (p k) n -> e p k n", p=P)
    w_eu = T["w_exp_up"][0].rearrange("e (p k) n -> e p k n", p=P)
    w_ed = T["w_exp_down"][0].rearrange("e (p k) n -> e p k n", p=P)
    x_lat, x_ctx = T["x_sample"][0], T["x_prompt"][0]
    x_of = [x_lat[t * P:(t + 1) * P, :] for t in range(4)] + [x_ctx]
    y_of = [T["y_sample"][0][t * P:(t + 1) * P, :] for t in range(4)] + [T["y_prompt"][0]]
    mod_dram = nc.dram_tensor("mod_rows", [2, 6 * D], F32, kind="Internal").ap()
    h2_dram = nc.dram_tensor("h2_rows", [TOK, D], F32, kind="Internal").ap()
    mT_dram = nc.dram_tensor("merged_T", [P, KT, TOK], F32, kind="Internal").ap()
    y_dram = nc.dram_tensor("y_rows", [TOK, D], F32, kind="Internal").ap()

    def row_bcast(row, n=P):
        return row.partition_broadcast(n)

    with ExitStack() as ctx:
        def sb(name, shape, dt=F32):
            return ctx.enter_context(nc.sbuf_tensor(name, shape, dt))

        def sem(name):
            return ctx.enter_context(nc.semaphore(name))

        ps = ctx.enter_context(nc.psum_tensor("ps", [P, 8, BANK], F32))
        cst = sb("cst", [P, C_END])
        ring = sb("ring", [P, SLOTS, SLOT])
        hT = sb("hT", [P, KT, TOK])
        ar_at = nc.sbuf_base
        ar = sb("ar", [P, 30288])
        modc = sb("modc", [P, 2, BANK])
        condT = sb("condT", [P, KT, 2])
        stat = sb("stat", [P, 2 * NT])
        decay = sb("decay", [P, 2, NCH])
        rs_gla = sb("rs_gla", [P, NT * GH])
        sink = sb("sink", [P, SH])
        soft = sb("soft", [P, 2, 5, GRP])
        aff = sb("aff", [P, 2, NT, 16])
        idxT = sb("idxT", [P, NE + 2], U32)
        gateT = sb("gateT", [P, NE])
        epsb = sb("epsb", [P, 1])
        gidx = sb("gidx", [CAP, 1], U32)
        sidx = sb("sidx", [CAP, 1], U32)

        ident = cst[:, C_ID:C_ID + P]

        def area(at, *dims):
            n = int(np.prod(dims))
            v = ar[:, at:at + n]
            if len(dims) == 2:
                v = v.rearrange("p (a b) -> p a b", a=dims[0])
            if len(dims) == 3:
                v = v.rearrange("p (a b c) -> p a b c", a=dims[0], b=dims[1])
            return v

        def split_area(name, at, *dims):
            return nc.alloc_sbuf_tensor_at(name, [P, *dims], F32R, offset=ar_at + 4 * at)

        def hT_area(at, n):
            return hT[:, :, :].rearrange("p k t -> p (k t)")[:, at:at + n]

        bmod = area(0, 2 * D)
        modrow = area(2 * D, 2 * D)
        g1 = area(4 * D, D)
        cond = area(5 * D, P)
        Ah, Bh = area(0, 2, D), area(2 * D, 2, D)
        hrow = area(6 * D, 2, D)
        junk = area(8 * D, D)
        xrow = area(18432, NT, D)
        gqT, gkT = area(0, GH, TOK), area(2560, GH, TOK)
        gv = area(5120, NT, GH * GV)
        og = area(10240, NT, GH * GV)
        gaT = area(15360, TOK)
        wdec = area(16000, 2, GH * GK)
        st = area(17024, 2, 10, GV)
        tz, tg, tc, tB, tD, xq0, xk, ks = [area(22144 + TOK * i, TOK) for i in range(8)]
        xq2 = (xq0, area(29568, TOK))
        aTm = area(27264, 2, TOK)
        glag = area(28544, GH * GV)
        oT = area(0, 8, TOK)
        sil, onr = area(5120, 2, BANK), area(6144, 2, BANK)
        swT = area(5120, 8, TOK)
        skT = area(10240, SKV, TOK + P)
        svr = area(13312, NT + 1, SKV * HD)
        skr = area(14848, NT + 1, SKV * 2 * HD)
        Sbuf = area(17920, 2, GRP * BANK)
        pT = area(22016, 2, 4 * BANK)
        rp = area(27264, 2, BANK)
        krow_out = area(28544, SKV * HD)
        spW = split_area("split_weights", 18000, SP, 2, BANK)
        spX = split_area("split_tokens", 18000 + SP * 2 * BANK, SP, 2, TOK)
        mTc = area(10240, 4, TOK)
        mT_last = {12 + k: mTc[:, k, :] for k in range(4)}
        sg = area(15424, NT, BANK)
        mrow = area(27216, NT, BANK)
        mtmp = area(29776, BANK)
        x1 = area(0, NT, D)
        gt1 = area(13312, 2, D)
        wtmp = area(27216, 2, BANK)
        junkx = area(10240, D)
        A2 = hT_area(0, 2 * D).rearrange("p (a b) -> p a b", a=2)
        B2 = hT_area(2 * D, 2 * D).rearrange("p (a b) -> p a b", a=2)
        g2 = hT_area(4 * D, D)
        gt2 = area(28240, D)
        h2row = area(17408, 2, D)
        h2T = area(21504, 2, KT, P)
        wrt = area(25600, KT, NE)
        affT = area(25856, TOK)
        vals, idxf = area(26496, CAP), area(26576, CAP)
        idxu = area(26656, CAP).bitcast(U32)
        xs = area(0, D)
        xsT = split_area("split_xsT", 2048, 2, KT, CAP)
        hidT = split_area("split_hidT", 4608, 2, FT, CAP)
        hid = area(5888, FF)
        ye = area(6912, D)
        spE = split_area("split_experts", 8960, SP, 2, SLOT)
        exp_slot = [ring[:, s, :] for s in range(SLOTS)] + [hT_area((2 + i) * SLOT, SLOT) for i in range(3)] + [area(25344, SLOT)]
        gfin = hT_area(0, D)
        yrow = area(0, NT, D)
        junk2 = area(NT * D, D)

        s_cst = sem("consts_loaded")
        slot_ready = [sem(f"slot_ready{s}") for s in range(SLOTS)]
        slot_used = sem("slots_used")
        exp_ready = [sem(f"expert_slot_ready{s}") for s in range(ESLOTS)]
        piece_high, piece_ready, piece_used = sem("pieces_high"), sem("pieces_ready"), sem("pieces_used")
        mT_st, mT_free, mT_ld, xs_h, xs_l, hd_h = (sem("merged_stored"), sem("merged_free"), sem("merged_loaded"),
                                                   sem("xs_high"), sem("xs_low"), sem("hidden_high"))
        s_condT, s_condS, s_eps = sem("cond_transposed"), sem("cond_silu"), sem("eps_set")
        mod_ev, mod_st, mod_a, mb_ld = sem("mod_evacuated"), sem("mod_stored"), sem("mod_scale"), sem("mod_bias")
        mc_pe, mc_ev, mc_st = sem("mod_column"), sem("mod_column_evacuated"), [sem("mod_column_added0"), sem("mod_column_added1")]
        mod_ab, x_ld, h_sq, h_row, h_tr, h_cp = ([sem("mod_rows_latent"), sem("mod_rows_context")],
                                                 [sem(f"x_loaded{t}") for t in range(NT)],
                                                 sem("x_squared"), sem("h_rows"), sem("h_transposed"), sem("h_copied"))
        pj_pe, pj_ev = sem("projected"), sem("projection_evacuated")
        ga_w, s_wdec, ga_pe, ga_ev = sem("decay_in_loaded"), sem("decay_w_loaded"), sem("ga_product"), sem("ga_ready")
        wdec0 = sem("wdec_cleared")
        z_pe, z_ab, z_mn, z_ln, g_b, g_e, g_m = (
            sem("z_product"), sem("z_abs_read"), sem("z_min_read"), sem("z_log"), sem("gla_cumsum"),
                                           sem("gla_exp"), sem("gla_scaled"))
        kt_pe, kt_cp, at_pe, at_cp = sem("kst_transposed"), sem("kst_copied"), sem("aT_product"), sem("aT_masked")
        u_pe, s_up, o_pe, o_ev = sem("U_product"), sem("state_updated"), sem("o_product"), sem("o_evacuated")
        st_ld, st_out, o_sq = [sem("state0_loaded"), sem("state1_loaded")], sem("state_stored"), sem("o_squared")
        gr_s, gr_o, gr_tr, gr_cp = sem("gr_silu"), sem("gr_gated"), sem("gr_transposed"), sem("gr_copied")
        sq_pm, sq_rp, kv_ld = sem("rope_permuted"), sem("roped"), sem("cache_loaded")
        k_dup, k_tr, k_cp, k_pm, k_rp, kv_st = (sem("k_doubled"), sem("k_transposed"), sem("k_copied"),
                                                sem("k_permuted"), sem("k_roped"), sem("cache_stored"))
        sc_pe, sc_m, sc_mx, sc_e, sc_n = sem("scores"), sem("scores_masked"), sem("scores_max"), sem("probs_exp"), sem("probs")
        pt_pe, pt_cp, pv_pe, pv_cp = sem("p_transposed"), sem("pT_copied"), sem("pv_product"), sem("pv_copied")
        gt_pe, gt_act, gt_dve = sem("gate_products"), sem("gate_sigmoid"), sem("gate_merged")
        mt_pe, mt_cp = sem("merged_transposed"), sem("merged_copied")
        wo_ld, xr_ld, wo_pe, wo_ev = sem("mod2_loaded"), sem("x_again_loaded"), sem("out_products"), sem("x1_ready")
        n2_sq, n2_h, n2_tr, n2_cp, n2_st, lg_pe = (sem("x1_squared"), sem("h2_row"), sem("h2_transposed"),
                                                   sem("h2_copied"), [sem("h2_stored0"), sem("h2_stored1")],
                                                   sem("logits"))
        af_e, af_r, af_tr, af_cp, tk_d, tk_tr, tk_cp = (sem("aff_exp"), sem("aff_rows"), sem("aff_transposed"),
                                                        sem("aff_copied"), sem("topk"), sem("topk_transposed"), sem("topk_ready"))
        gi_cp, xs_ld, xs_tr, xs_cp = sem("gather_index"), sem("xs_gathered"), sem("xs_transposed"), sem("xs_copied")
        hd_s, hd_r, hd_tr, hd_cp, ye_r, ye_st = (
            sem("gate_silu"), sem("hidden"), sem("hidden_transposed"), sem("hidden_copied"),
            sem("expert_out"), sem("expert_added"))
        y_ld, y_sq, y_r, y_st = [sem(f"y_loaded{t}") for t in range(NT)], sem("y_squared"), sem("y_ready"), sem("y_stored")
        gf_ld, y_sto = sem("gfinal_loaded"), sem("y_out")
        act_step, dve_step, dve2_step, pool_step = sem("act_step"), sem("dve_step"), sem("dve_loop_step"), sem("pool_step")
        loads_issued, rows_issued = sem("loads_issued"), sem("rows_issued")
        ye_free, x1_st = sem("ye_free"), sem("x1_stored")

        def gate_split(sp, n, q, lo, hi):
            first = GATE_PIECES[q][0]
            sp.pieces(P_GATE + first, n * 48, G_GATE + first // 4, n * 3, (hT, oT, hT, swT)[q], lo, hi)

        def out_pieces(sp, eng, n, lo, hi):
            if lo == 0:
                eng.wait_ge(mT_ld, 16 * 3)
            sp.pieces(P_OUT, n * KT, G_OUT, n, hT, lo, min(hi, 12))
            sp.pieces(P_OUT, n * KT, G_OUT, n, mT_last, max(lo, 12), hi)

        units = [(t, g) for t in range(NT) for g in range(SKV)]

        def unit_keys(t):
            if t == NT - 1:
                return [(LAT, P)], [NT - 1]
            lo, hi = max(t - 1, 0), min(t + 1, LAT // P - 1)
            return [(lo * P, (hi - lo + 1) * P), (TOK, P)], [*range(lo, hi + 1), NT]

        def copy_pT(act, u, n):
            for i, _ in enumerate(unit_keys(units[u][0])[1]):
                act.wait_ge(pt_pe, n + 1)
                if u >= 2:
                    act.wait_ge(pv_pe, u - 1)
                act.activation(pT[:, u % 2, i * BANK:(i + 1) * BANK], ps[:, 4 + n % 2, :], ACT.Copy).then_inc(pt_cp, 1)
                n += 1
            return n

        def copy_o(act, u):
            t, g = units[u]
            act.wait_ge(pv_pe, u + 1)
            act.activation(swT[:, 2 * g:2 * g + 2, t * P:(t + 1) * P],
                           ps[:, 6, 0:2 * P].rearrange("p (c q) -> p c q", c=2), ACT.Copy).then_inc(pv_cp, 1)

        def parts(*places):
            return [(k, ps[:, b, at * CAP:(at + n) * CAP].rearrange("p (k t) -> p k t", k=n)) for k, b, at, n in places]

        xs_parts = parts((0, 2, 0, 6), (6, 3, 0, 6), (12, 1, 2, 4))
        hid_parts = parts((0, 0, 0, 6), (6, 1, 0, 2))

        def bank_done(eng, done, before, b, last):
            if b < 4:
                eng.wait_ge(done, before * 4 + (b + 1))
            else:
                eng.wait_ge(piece_used, last + (SP + 1))

        class Split:

            def __init__(self, eng, high):
                self.eng, self.high = eng, high

            def pieces(self, first, turn, granule, gturn, src, lo, hi):
                for k in range(lo, hi):
                    s, g = (first + k) % SP, granule + k // 4
                    raw = ring[:, g % SLOTS, :].rearrange("p (k n) -> p k n", k=4)[:, k % 4, :]
                    if self.high:
                        if k % 4 == 0:
                            self.eng.wait_ge(slot_ready[g % SLOTS], gturn * 16 + 16 * (g // SLOTS + 1))
                        self.eng.wait_ge(piece_used, turn + (first + k + 1))
                        self.eng.activation(spW[:, s, 0, :], raw, ACT.Copy)
                        self.eng.activation(spX[:, s, 0, :], (src[k] if type(src) is dict else src[:, k, :]), ACT.Copy).then_inc(piece_high, 1)
                    else:
                        self.eng.wait_ge(piece_high, turn + (first + k + 1))
                        a = self.eng.tensor_tensor(spW[:, s, 1, :], raw, spW[:, s, 0, :].bitcast(F32), ALU.subtract)
                        if k % 4 == 3:
                            a.then_inc(slot_used, 1)
                        self.eng.tensor_tensor(spX[:, s, 1, :], (src[k] if type(src) is dict else src[:, k, :]), spX[:, s, 0, :].bitcast(F32),
                                               ALU.subtract).then_inc(piece_ready, 1)

            def chunk(self, i, lo=0, hi=KT):
                self.pieces(P_A + KT * i, 0, G_A + 4 * i if i < 4 else G_A2 + 4 * (i - 4), 0, hT, lo, hi)

        block = ctx.enter_context(nc.Block())

        @block.sync
        def _(sync):
            def load(g, src, dst=None):
                first, turn = g
                s = first % SLOTS
                sync.wait_ge(slot_used, first + turn + 1)
                sync.sem_inc(loads_issued, 1)
                out = ring[:, s, :] if dst is None else dst(ring[:, s, :])
                sync.dma_start(out, src).then_inc(slot_ready[s], 16)

            def k4(v):
                return v.rearrange("p (k n) -> p k n", k=4)

            def k2(v):
                return v.rearrange("p (k n) -> p k n", k=2)

            def modulation(first, col):
                with sync.Fori(0, 8) as c:
                    for j in range(4):
                        load((first + j, c * 4), w_mod[:, 4 * j:4 * j + 4, ds(c * BANK + col, BANK)], k4)

            def projection(first, count, col):
                with sync.Fori(0, count) as c:
                    for j in range(4):
                        load((first + j, c * 4), w_in[:, 4 * j:4 * j + 4, ds(c * BANK + col, BANK)], k4)

            with sync.Fori(0, 2) as m:
                for j in range(KT):
                    load((G_MOD + j, m * KT), w_mod[:, j, ds(m * D, D)])
            projection(G_A, 4, 0)
            modulation(G_M2, 2 * D)
            projection(G_A2, 2, COL_GR)
            projection(G_A2 + 8, 3, COL_SQ)
            modulation(G_M3, 4 * D)
            with sync.Fori(0, 4) as n:
                for half, (col, w) in enumerate(((COL_GATE_A, w_a), (COL_GATE_B, w_b))):
                    for j in range(4):
                        load((G_GATE + 6 * half + j, n * 12), w_in[:, 4 * j:4 * j + 4, ds(n * BANK + col, BANK)], k4)
                    for j in range(2):
                        load((G_GATE + 6 * half + 4 + j, n * 12), w[:, 4 * j:4 * j + 4, ds(n * BANK, BANK)], k4)
            with sync.Fori(0, 4) as n:
                for j in range(4):
                    load((G_OUT + j, n * 4), w_out[:, 4 * j:4 * j + 4, ds(n * BANK, BANK)], k4)
            sync.wait_ge(piece_ready, P_EXP)
            with sync.Fori(0, NE) as e:
                def expert(j, src, dst=None):
                    sync.wait_ge(piece_ready, e * EXP_G + (P_EXP + j + 1 - ESLOTS))
                    if j == SLOTS:
                        sync.wait_ge(n2_h, NT)
                    if j == ESLOTS - 1:
                        sync.wait_ge(tk_cp, 3)
                    sync.sem_inc(loads_issued, 1)
                    out = exp_slot[j % ESLOTS]
                    sync.dma_start(out if dst is None else dst(out), src).then_inc(exp_ready[j % ESLOTS], 16)

                for j in range(8):
                    expert(2 * j, w_eg[ds(e, 1), :, 2 * j:2 * j + 2, :].squeeze(0), k2)
                    expert(2 * j + 1, w_eu[ds(e, 1), :, 2 * j:2 * j + 2, :].squeeze(0), k2)
                for j in range(8):
                    expert(16 + j, w_ed[ds(e, 1), :, j, :].squeeze(0))

        @block.gpsimd
        def _(pool):
            pool.dma_start(cst[:, :], T["consts"]).then_inc(s_cst, 16)
            pool.dma_start(cond[0:KT, :], T["c"][0].rearrange("(k p) -> k p", p=P)).then_inc(s_cst, 16)
            pool.dma_start(cond[KT:2 * KT, :], T["c_ctx"].rearrange("(k p) -> k p", p=P)).then_inc(s_cst, 16)
            pool.dma_start(bmod[0:2, :], row_bcast(T["b_mod"][0, 0:2 * D], 2)).then_inc(s_cst, 16)
            pool.dma_start(g1[0:2, :], row_bcast(T["g_norm1"][0], 2)).then_inc(s_cst, 16)
            pool.dma_start(sink[:, :], row_bcast(T["attn_sink"][0])).then_inc(s_cst, 16)
            for t in range(NT):
                pool.dma_start(xrow[:, t, :], x_of[t]).then_inc(x_ld[t], 16)
            for who in range(2):
                pool.dma_start(mod_dram[who:who + 1, 2 * D:6 * D], T["b_mod"][0:1, 2 * D:6 * D]).then_inc(mb_ld, 16)
            pool.wait_ge(mod_ev, 3)
            pool.dma_start(mod_dram[:, 0:D], modrow[0:2, 0:D]).then_inc(mod_st, 16)
            pool.wait_ge(mod_a, 1)
            pool.dma_start(mod_dram[:, D:2 * D], modrow[0:2, D:2 * D]).then_inc(mod_st, 16)
            pool.wait_ge(mod_st, 32)

            def mod_load(dst, who, part, s, n=P):
                pool.dma_start(dst, row_bcast(mod_dram[who, part * D:(part + 1) * D], n)).then_inc(s, 16)

            for who in range(2):
                mod_load(Ah[:, who, :], who, 1, mod_ab[who])
                mod_load(Bh[:, who, :], who, 0, mod_ab[who])

            def mod_columns(first, count):
                for i in range(first, first + count):
                    pool.wait_ge(mc_ev, i + 1)
                    pool.dma_start(mod_dram[:, 2 * D + i * BANK:2 * D + (i + 1) * BANK], modc[0:2, i % 2, :],
                                   accum_op=ALU.add).then_inc(mc_st[i % 2], 16)

            pool.wait_ge(mb_ld, 32)
            pool.wait_ge(h_row, NT)
            pool.wait_ge(wdec0, 1)
            for dr, (w, b) in enumerate((("w_dec_f", "b_dec_f"), ("w_dec_b", "b_dec_b"))):
                pool.dma_start(wdec[RANK * dr:RANK * dr + RANK, dr, :], T[w][0]).then_inc(s_wdec, 16)
                pool.dma_start(wdec[2 * RANK:2 * RANK + 1, dr, :], T[b]).then_inc(s_wdec, 16)
            pool.dma_start(glag, row_bcast(T["g_gla"][0])).then_inc(s_wdec, 16)
            pool.wait_ge(piece_used, SP + 4 * KT)
            for s in range(2 * GH):
                h, dr = s // 2, s % 2
                src = T["state_gla_bwd" if dr else "state_gla_fwd"][0, 0, h]
                if s >= 2:
                    pool.wait_ge(o_pe, 3 * (s - 1))
                    pool.wait_ge(s_up, 9 * (s - 1))
                    final = T["ns_bwd" if (s - 2) % 2 else "ns_fwd"][0, 0, (s - 2) // 2]
                    pool.dma_start(final, st[:, s % 2, 9, :]).then_inc(st_out, 16)
                pool.dma_start(st[:, s % 2, 0, :], src).then_inc(st_ld[s % 2], 16)
                if s >= 2:
                    mod_columns(s - 2, 1)
            for s in range(2 * GH, 2 * GH + 2):
                pool.wait_ge(s_up, 9 * (s - 1))
                final = T["ns_bwd" if (s - 2) % 2 else "ns_fwd"][0, 0, (s - 2) // 2]
                pool.dma_start(final, st[:, s % 2, 9, :]).then_inc(st_out, 16)
            mod_columns(2 * GH - 2, 2)
            pool.wait_ge(st_out, 16 * 2 * GH)
            pool.wait_ge(gr_tr, 10)
            kc = T["cache_k"][0, 0].rearrange("s h d -> s h d")
            skr_c = skr[:, NT, :].rearrange("p (h e d) -> p h e d", h=SKV, e=2)
            for e in range(2):
                pool.dma_start(skr_c[:, :, e, :], kc).then_inc(kv_ld, 16)
            pool.dma_start(svr[:, NT, :], T["cache_v"][0, 0].rearrange("s h d -> s (h d)")).then_inc(kv_ld, 16)
            pool.wait_ge(k_dup, 3 * NT + 1)
            pool.dma_start(T["nk"][0, 0].rearrange("s h d -> s (h d)"), krow_out).then_inc(kv_st, 16)
            pool.dma_start(T["nv"][0, 0].rearrange("s h d -> s (h d)"), svr[:, NT - 1, :]).then_inc(kv_st, 16)
            mod_columns(8, 8)
            for n in range(3):
                pool.wait_ge(mt_cp, NT * (n + 1) + 1)
                pool.dma_start(mT_dram[:, 4 * n:4 * n + 4, :], mTc).then_inc(mT_st, 16)
                pool.wait_ge(mT_st, 16 * (n + 1))
                pool.sem_inc(mT_free, 1)
            pool.wait_ge(piece_ready, P_GATE + 3 * 48 + GATE_PIECES[3][0])
            for n in range(3):
                pool.dma_start(hT[:, 4 * n:4 * n + 4, :], mT_dram[:, 4 * n:4 * n + 4, :]).then_inc(mT_ld, 16)
            pool.wait_ge(piece_used, SP + P_OUT)
            for t in range(NT):
                pool.dma_start(x1[:, t, :], x_of[t]).then_inc(xr_ld, 16)
            pool.wait_ge(gt_dve, 9 * NT)
            for who in range(2):
                mod_load(gt1[:, who, :], who, 2, wo_ld)
            pool.wait_ge(piece_used, SP + P_EXP)
            for who in range(2):
                mod_load(A2[:, who, :], who, 4, wo_ld)
                mod_load(B2[:, who, :], who, 3, wo_ld)
            pool.dma_start(g2, row_bcast(T["g_norm2"][0])).then_inc(wo_ld, 16)
            mod_load(gt2[0:CAP_L, :], 0, 5, wo_ld, CAP_L)
            mod_load(gt2[CAP_L:CAP, :], 1, 5, wo_ld, CAP_C)
            pool.dma_start(wrt, T["w_router"][0].rearrange("(k p) e -> p k e", p=P)).then_inc(wo_ld, 16)
            for t in range(NT):
                pool.wait_ge(n2_sq, t + 1)
                pool.dma_start(y_dram[t * P:(t + 1) * P, :], x1[:, t, :]).then_inc(x1_st, 16)
                pool.wait_ge(n2_h, t + 1)
                pool.dma_start(h2_dram[t * P:(t + 1) * P, :], h2row[:, t % 2]).then_inc(n2_st[t % 2], 16)
            pool.wait_ge(tk_cp, 3)
            pool.wait_ge(n2_st[0], 48)
            pool.wait_ge(n2_st[1], 32)
            pool.wait_ge(x1_st, 16 * NT)

            def gather(col):
                pool.tensor_copy(gidx[:, :], col).then_inc(gi_cp, 1)

            def gather_rows():
                pool.indirect_dma_start(xs[0:CAP, :], None, h2_dram, bass.IndirectOffsetOnAxis(ap=gidx[:, :], axis=0))\
                    .then_inc(xs_ld, 16)

            pool.dma_start(gfin, row_bcast(T["g_final"])).then_inc(gf_ld, 16)
            gather(idxT[0:CAP, 0:1])
            pool.wait_ge(gi_cp, 1)
            gather_rows()
            pool.wait_ge(xs_tr, 1)
            gather(idxT[0:CAP, 1:2])
            pool.wait_ge(gi_cp, 2)
            gather_rows()
            with pool.Fori(0, NE) as e:
                pool.wait_ge(xs_tr, e + 2)
                pool.wait_ge(xs_ld, e * 16 + 32)
                gather(idxT[0:CAP, ds(e + 2, 1)])
                pool.wait_ge(gi_cp, e + 3)
                pool.sem_inc(rows_issued, 1)
                gather_rows()
                pool.tensor_copy(sidx[:, :], idxT[0:CAP, ds(e, 1)]).then_inc(pool_step, 1)
                pool.wait_ge(pool_step, e + 1)
                pool.wait_ge(ye_r, e + 2)
                pool.sem_inc(rows_issued, 1)
                pool.indirect_dma_start(y_dram, bass.IndirectOffsetOnAxis(ap=sidx[:, :], axis=0), ye[0:CAP, :], None,
                                        compute_op=ALU.add).then_inc(ye_st, 16)
                pool.wait_ge(ye_st, e * 16 + 16)
                pool.sem_inc(ye_free, 1)
            pool.wait_ge(xs_ld, 16 * (NE + 2))
            for t in range(NT):
                pool.dma_start(yrow[:, t, :], y_dram[t * P:(t + 1) * P, :]).then_inc(y_ld[t], 16)
            for t in range(NT):
                pool.wait_ge(y_r, t + 1)
                pool.dma_start(y_of[t], yrow[:, t, :]).then_inc(y_sto, 16)
            pool.wait_ge(y_sto, 16 * NT)
            pool.wait_ge(kv_st, 32)
            pool.wait_ge(st_out, 16 * 2 * GH)

        @block.tensor
        def _(pe):
            def slot(first, turn):
                s = first % SLOTS
                pe.wait_ge(slot_ready[s], turn * 16 + 16 * (first // SLOTS + 1))
                return ring[:, s, :]

            pe.sem_inc(slot_used, SLOTS)
            pe.sem_inc(piece_used, SP)
            pe.wait_ge(s_cst, 96)
            pe.transpose(ps[:, 0, 0:2 * KT], cond[0:2 * KT, :], ident[0:2 * KT, 0:2 * KT]).then_inc(s_condT, 1)
            pe.wait_ge(s_condS, 1)
            with pe.Fori(0, 2) as m:
                pe.wait_ge(mod_ev, m + 1)
                for k in range(KT):
                    w = slot(G_MOD + k, m * 4)
                    for n in range(4):
                        mm = pe.matmul(ps[0:2, n, :], condT[:, k, :], w[:, n * BANK:(n + 1) * BANK],
                                       start=(k == 0), stop=(k == KT - 1))
                    mm.then_inc(slot_used, 1)
            n_mod = 0

            def mod_granules(count):
                nonlocal n_mod
                for _ in range(count):
                    c, j = n_mod // 4, n_mod % 4
                    w = slot((G_M2 if c < 8 else G_M3 - 32) + n_mod, 0).rearrange("p (k n) -> p k n", k=4)
                    if j == 0 and c:
                        pe.wait_ge(mc_ev, c)
                    for kk in range(4):
                        mm = pe.matmul(ps[0:2, 7, :], condT[:, 4 * j + kk, :], w[:, kk, :],
                                       start=(j == 0 and kk == 0), stop=(j == 3 and kk == 3))
                    mm.then_inc(slot_used, 1)
                    n_mod += 1

            for t in range(NT):
                pe.wait_ge(h_row, t + 1)
                if t >= 2:
                    pe.wait_ge(h_cp, 4 * (t - 1))
                else:
                    pe.wait_ge(mod_ev, 3)
                for k in range(KT):
                    mm = pe.transpose(ps[:, 4 * (t % 2) + k // 4, (k % 4) * P:(k % 4 + 1) * P],
                                      hrow[:, t % 2, k * P:(k + 1) * P], ident)
                    if k % 4 == 3:
                        mm.then_inc(h_tr, 1)

            def product(first, turn, n_k, bank_free, done):
                for k in range(n_k):
                    s = (first + k) % SP
                    pe.wait_ge(piece_ready, turn + (first + k + 1))
                    for b in range(NT):
                        if k == 0:
                            bank_free(b)
                        for x, w in ((0, 0), (0, 1), (1, 0)):
                            mm = pe.matmul(ps[:, b, :], spX[:, s, x, b * P:(b + 1) * P], spW[:, s, w, :],
                                           start=(k == 0 and x == w), stop=(k == n_k - 1 and x == 1))
                        if k == n_k - 1 and b < 4:
                            mm.then_inc(done, 1)
                    mm.then_inc(piece_used, 1)

            def product_T(first, turn, bank_free, done):
                for k in range(KT):
                    s = (first + k) % SP
                    pe.wait_ge(piece_ready, turn + (first + k + 1))
                    for c in range(4):
                        if k == 0:
                            bank_free(c)
                        for x, w in ((0, 0), (1, 0), (0, 1)):
                            mm = pe.matmul(ps[:, c, 0:TA], spW[:, s, w, c * P:(c + 1) * P], spX[:, s, x, 0:TA],
                                           start=(k == 0 and x == w), stop=(k == KT - 1 and w == 1))
                        if k == KT - 1:
                            mm.then_inc(done, 1)
                        if k == 0 and c == 0:
                            bank_free(4)
                        for x, w in ((0, 0), (1, 0), (0, 1)):
                            mm = pe.matmul(ps[:, 4 + c // 2, (c % 2) * TB:(c % 2 + 1) * TB],
                                           spW[:, s, w, c * P:(c + 1) * P],
                                           spX[:, s, x, TA:TOK], start=(k == 0 and c % 2 == 0 and x == w),
                                           stop=(k == KT - 1 and w == 1), skip_group_check=True)
                    mm.then_inc(piece_used, 1)

            def chunks(first, count, rows):
                with pe.Fori(0, count) as c:
                    def bank_free(b):
                        pe.wait_ge(pj_ev, c * NT + (NT * first + b + 1))
                    if rows:
                        product(P_A + KT * first, c * KT, KT, bank_free, pj_pe)
                    else:
                        product_T(P_A + KT * first, c * KT, bank_free, pj_pe)

            pe.wait_ge(h_cp, 4 * NT)
            chunks(0, 2, False)
            chunks(2, 2, True)
            pe.wait_ge(ga_w, 16)
            gaw = ar[:, 27264:27264 + KT * 2 * RANK].rearrange("p (k n) -> p k n", k=KT)
            for k in range(KT):
                pe.matmul(ps[0:2 * RANK, 5, :], gaw[:, k, :], hT[:, k, 0:LAT], start=(k == 0), stop=(k == KT - 1))
                mm = pe.matmul(ps[0:2 * RANK, 6, 0:CTX], gaw[:, k, :], hT[:, k, LAT:TOK],
                               start=(k == 0), stop=(k == KT - 1))
            mm.then_inc(ga_pe, 1)
            pe.wait_ge(ga_ev, 2)
            pe.wait_ge(s_wdec, 80)
            pe.wait_ge(pj_ev, NT * 5)

            def z_product(s, part):
                w = wdec[0:2 * RANK + 1, s % 2, s // 2 * GK:(s // 2 + 1) * GK]
                lo, n = ((0, LAT), (LAT, CTX))[part]
                if s or part:
                    pe.wait_ge(z_mn, 2 * s + part)
                pe.matmul(ps[:, 4, 0:n], w, gaT[0:2 * RANK + 1, lo:lo + n], start=True, stop=True).then_inc(z_pe, 1)

            z_product(0, 0)
            mod_granules(1)
            z_product(0, 1)
            for s in range(2 * GH):
                h, dr = s // 2, s % 2
                xq = xq2[dr]
                pe.wait_ge(g_m, s + 1)
                if s:
                    pe.wait_ge(s_up, 9 * s)
                for t in range(NT):
                    mm = pe.transpose(ps[:, 5 + t // 4, (t % 4) * P:(t % 4 + 1) * P], tD[:, t * P:(t + 1) * P], ident)
                mm.then_inc(kt_pe, 1)
                if s:
                    pe.wait_ge(o_ev, 3 * s)
                for t in range(NT):
                    o = ps[:, 3, t * P:(t + 1) * P] if t < 4 else ps[:, 2, 2 * GV - P:2 * GV]
                    mm = pe.matmul(o, xk[:, t * P:(t + 1) * P], xq[:, t * P:(t + 1) * P], start=True, stop=True,
                                   skip_group_check=True)
                mm.then_inc(at_pe, 1)
                if s + 1 < 2 * GH:
                    z_product(s + 1, 0)
                mod_granules(1)
                order = ([9, 8] if dr else [8, 9]) + (list(range(7, 0, -1)) if dr else list(range(7)))
                pe.wait_ge(kt_cp, s + 1)
                for u, c in enumerate(order):
                    lo, t = (c % 2) * CH, c // 2
                    bank, half, _, freed = U_PLACE[u]
                    if freed:
                        pe.wait_ge(s_up, 9 * s + freed)
                    pe.matmul(ps[:, bank, half * GV:(half + 1) * GV],
                              ks[lo:lo + CH, t * P:(t + 1) * P], gv[lo:lo + CH, t, h * GV:(h + 1) * GV],
                              start=True, stop=True, skip_group_check=True).then_inc(u_pe, 1)
                if s + 1 < 2 * GH:
                    z_product(s + 1, 1)
                    mod_granules(3)
                else:
                    mod_granules(2)
                pe.wait_ge(at_cp, s + 1)
                for i, t in enumerate([4, 3, 2, 1, 0] if dr else [4, 0, 1, 2, 3]):
                    o = ps[:, t // 2, (t % 2) * GV:(t % 2 + 1) * GV]
                    mm = pe.matmul(o, aTm[:, dr, t * P:(t + 1) * P], gv[:, t, h * GV:(h + 1) * GV],
                                   start=True, stop=False, skip_group_check=True)
                    for c in ([2 * t + 1, 2 * t] if dr else [2 * t, 2 * t + 1]):
                        lo = (c % 2) * CH
                        if c >= LCH:
                            if c == order[0]:
                                continue
                            state = st[:, dr, 8, :]
                            pe.wait_ge(s_up, 9 * s + 1)
                        else:
                            n = 7 - c if dr else c
                            state = st[:, dr, n, :]
                            if n:
                                pe.wait_ge(s_up, 9 * s + 2 + n)
                            else:
                                pe.wait_ge(st_ld[dr], 16 * (h + 1))
                        mm = pe.matmul(o[lo:lo + CH, :], xq[:, c * CH:(c + 1) * CH], state,
                                       start=False, stop=True, skip_group_check=True)
                    if i % 2 == 0:
                        mm.then_inc(o_pe, 1)
            pe.wait_ge(o_ev, 2 * GH * 3)
            with pe.Fori(0, 2) as c:
                def bank_free(b):
                    pe.wait_ge(pj_ev, c * NT + (NT * 4 + b + 1))
                product(P_A + KT * 4, c * KT, KT, bank_free, pj_pe)
                for b in range(NT):
                    pe.wait_ge(gr_o, c * NT + (b + 1))
                    pe.wait_ge(gr_cp, c * NT + (b + 1 + (b == 0)))
                    for q in range(4):
                        mm = pe.transpose(ps[:, 5 + b % 2, q * P:(q + 1) * P], onr[:, b % 2, q * P:(q + 1) * P], ident)
                    mm.then_inc(gr_tr, 1)
            pe.wait_ge(gr_cp, 2 + 2 * NT)
            chunks(6, 2, False)
            chunks(8, 1, True)
            for i in range(8):
                pe.wait_ge(pj_ev, NT * (8 + i // 4))
                if i >= 2:
                    pe.wait_ge(sq_rp, i - 1)
                pe.matmul(ps[:, 5 + i % 2, :], cst[:, C_PERM:C_PERM + P], swT[:, i, 0:LAT],
                          start=True, stop=True).then_inc(sq_pm, 1)
            pe.wait_ge(k_dup, 3 * NT + 1)
            pe.wait_ge(kv_ld, 48)
            pe.wait_ge(sq_rp, 8)
            for g in range(SKV):
                if g:
                    pe.wait_ge(k_cp, 2 * g)
                for t in range(NT + 1):
                    mm = pe.transpose(ps[:, t // 4, (t % 4) * P:(t % 4 + 1) * P],
                                      skr[:, t, g * 2 * HD:(g + 1) * 2 * HD], ident)
                mm.then_inc(k_tr, 1)
                pe.wait_ge(k_cp, 2 * g + 2)
                if g >= 2:
                    pe.wait_ge(k_rp, g - 1)
                pe.matmul(ps[:, 2 + g % 2, :], cst[:, C_PERM:C_PERM + P], skT[:, g, 0:LAT],
                          start=True, stop=True).then_inc(k_pm, 1)
            pe.wait_ge(k_rp, SKV)

            def scores(u):
                t, g = units[u]
                keys, _ = unit_keys(t)
                if u:
                    pe.wait_ge(sc_m, u)
                for j in range(GRP):
                    lo, ch = (j % 2) * HD, 2 * g + j // 2
                    at = 0
                    for a, n in keys:
                        mm = pe.matmul(ps[:, j, at:at + n], swT[lo:lo + HD, ch, t * P:(t + 1) * P],
                                       skT[lo:lo + HD, g, a:a + n], start=True, stop=True, skip_group_check=True)
                        at += n
                mm.then_inc(sc_pe, 1)

            n_pt = 0
            scores(0)
            for u, (t, g) in enumerate(units):
                if u + 1 < len(units):
                    scores(u + 1)
                _, blocks = unit_keys(t)
                mod_granules(2 if u % 5 < 3 else 1)
                pe.wait_ge(sc_n, u + 1)
                for i, _ in enumerate(blocks):
                    if n_pt >= 2:
                        pe.wait_ge(pt_cp, n_pt - 1)
                    for j in range(GRP):
                        mm = pe.transpose(ps[:, 4 + n_pt % 2, j * P:(j + 1) * P],
                                          Sbuf[:, u % 2, j * BANK + i * P:j * BANK + (i + 1) * P], ident)
                    mm.then_inc(pt_pe, 1)
                    n_pt += 1
                if u:
                    pe.wait_ge(pv_cp, u)
                for half in range(2):
                    lo = half * HD
                    for i, vt in enumerate(blocks):
                        pe.wait_ge(pt_cp, n_pt - len(blocks) + i + 1)
                        mm = pe.matmul(ps[lo:lo + HD, 6, 0:2 * P], svr[:, vt, g * HD:(g + 1) * HD],
                                       pT[:, u % 2, i * BANK:(i + 1) * BANK].rearrange(
                                           "p (c e q) -> p c e q", c=2, e=2)[:, :, half, :],
                                       start=(i == 0), stop=(i == len(blocks) - 1), skip_group_check=True)
                mm.then_inc(pv_pe, 1)
            pe.wait_ge(pv_cp, len(units))

            def merged_transposes(n):
                for b in range(NT):
                    pe.wait_ge(gt_dve, n * 10 + (2 * NT + b + 1))
                    pe.wait_ge(mt_cp, n * NT + (1 if b < 3 else b - 1))
                    for q in range(4):
                        mm = pe.transpose(ps[:, 5 + b % 3, q * P:(q + 1) * P], mrow[:, b, q * P:(q + 1) * P], ident)
                    mm.then_inc(mt_pe, 1)

            def gate_products(n, before):
                for q, (first, n_k) in enumerate(GATE_PIECES):
                    def bank_free(b):
                        if q == 0:
                            pe.wait_ge(gt_dve, n * 10 + (b + 1))
                        elif q == 2:
                            pe.wait_ge(gt_dve, n * 10 + (NT + b + 1))
                        else:
                            pe.wait_ge(gt_act, n * 10 + (5 * (q // 2) + b + 1))
                    product(P_GATE + first, n * 48, n_k, bank_free, gt_pe)
                    if q == 0 and before is not None:
                        merged_transposes(before)

            gate_products(0, None)
            with pe.Fori(1, 4) as n:
                gate_products(n, n - 1)
            merged_transposes(3)
            pe.wait_ge(mt_cp, 4 * NT + 1)
            pe.wait_ge(gt_dve, 9 * NT)
            with pe.Fori(0, 4) as n:
                def bank_free(b):
                    pe.wait_ge(wo_ev, n * NT + (b + 1))
                product(P_OUT, n * KT, KT, bank_free, wo_pe)
            pe.wait_ge(wo_ev, 5 * NT)
            for t in range(NT):
                pe.wait_ge(n2_h, t + 1)
                for k in range(KT):
                    mm = pe.transpose(ps[:, k // 4, (k % 4) * P:(k % 4 + 1) * P],
                                      h2row[:, t % 2, k * P:(k + 1) * P], ident)
                mm.then_inc(n2_tr, 1)
                if t == 0:
                    pe.wait_ge(wo_ld, 16 * 10)
                pe.wait_ge(n2_cp, t + 1)
                for k in range(KT):
                    mm = pe.matmul(ps[:, 4, t * NE:(t + 1) * NE], h2T[:, t % 2, k, :], wrt[:, k, :],
                                   start=(k == 0), stop=(k == KT - 1), skip_group_check=True)
                mm.then_inc(lg_pe, 1)
            pe.wait_ge(af_r, 1)
            for t in range(NT):
                mm = pe.transpose(ps[0:NE, 5 + t // 4, (t % 4) * P:(t % 4 + 1) * P], aff[:, 0, t, :], ident)
            mm.then_inc(af_tr, 1)
            pe.wait_ge(tk_d, 1)
            pe.transpose(ps[0:CAP, 7, 0:NE], idxf[0:NE, :], ident[0:NE, 0:NE])
            pe.transpose(ps[0:CAP, 7, NE:2 * NE], vals[0:NE, :], ident[0:NE, 0:NE]).then_inc(tk_tr, 1)

            def xs_transposes(bank1_free=None):
                v = xs[0:CAP, :].rearrange("r (p k) -> r k p", k=KT)
                for k in range(KT):
                    o = xs_bank(k)
                    if k == 12 and bank1_free is not None:
                        pe.wait_ge(hd_cp, bank1_free)
                    mm = pe.transpose(o, v[:, k, :], ident[0:CAP, 0:CAP])
                mm.then_inc(xs_tr, 1)

            def xs_bank(k):
                b, i = ((2, k) if k < 6 else (3, k - 6)) if k < 12 else (1, k - 12 + 2)
                return ps[:, b, i * CAP:(i + 1) * CAP]

            pe.wait_ge(xs_ld, 16)
            pe.wait_ge(af_cp, 1)
            xs_transposes()
            with pe.Fori(0, NE) as e:
                pe.wait_ge(xs_l, e + 1)
                for j in range(16):
                    g, up = j // 2, j % 2
                    s = j % SP
                    pe.wait_ge(piece_ready, e * EXP_G + (P_EXP + j + 1))
                    for kk in range(2):
                        k = 2 * g + kk
                        for x, w in ((0, 0), (0, 1), (1, 0)):
                            for n in range(2):
                                col = kk * FF + n * BANK
                                mm = pe.matmul(ps[0:CAP, 2 * up + n, :], xsT[:, x, k, :], spE[:, s, w, col:col + BANK],
                                               start=(k == 0 and x == w), stop=(k == KT - 1 and x == 1))
                    mm.then_inc(piece_used, 1)
                pe.wait_ge(hd_r, e + 1)
                v = hid[0:CAP, :].rearrange("r (p k) -> r k p", k=FT)
                for k in range(FT):
                    mm = pe.transpose(ps[:, k // 6, (k % 6) * CAP:(k % 6 + 1) * CAP], v[:, k, :], ident[0:CAP, 0:CAP])
                mm.then_inc(hd_tr, 1)
                pe.wait_ge(xs_ld, e * 16 + 32)
                xs_transposes(e + 1)
                pe.wait_ge(hd_cp, e + 1)
                pe.wait_ge(ye_r, e + 1)
                for k in range(FT):
                    s = (16 + k) % SP
                    pe.wait_ge(piece_ready, e * EXP_G + (P_EXP + 16 + k + 1))
                    for x, w in ((0, 0), (0, 1), (1, 0)):
                        for n in range(4):
                            mm = pe.matmul(ps[0:CAP, 4 + n, :], hidT[:, x, k, :], spE[:, s, w, n * BANK:(n + 1) * BANK],
                                           start=(k == 0 and x == w), stop=(k == FT - 1 and x == 1))
                    mm.then_inc(piece_used, 1)

        @block.scalar
        def _(act):
            ch = Chain(act, act_step)
            act.wait_ge(s_condT, 1)
            act.activation(condT[:, :, :].rearrange("p k w -> p w k"),
                           ps[:, 0, 0:2 * KT].rearrange("p (w k) -> p w k", w=2), ACT.Silu).then_inc(s_condS, 1)
            act.wait_ge(s_eps, 1)
            for t in range(NT):
                act.wait_ge(x_ld[t], 16)
                ch.step(act.activation(junk, xrow[:, t, :], ACT.Square, accum_out=stat[:, t:t + 1]))
                act.activation(stat[:, NT + t:NT + t + 1], stat[:, t:t + 1], ACT.Sqrt, scale=1.0 / D,
                               bias=epsb[:, :]).then_inc(h_sq, 1)
            for t in range(NT):
                for q in range(4):
                    act.wait_ge(h_tr, 4 * t + q + 1)
                    act.activation(hT[:, 4 * q:4 * q + 4, t * P:(t + 1) * P],
                                   ps[:, 4 * (t % 2) + q, :].rearrange("p (k t) -> p k t", k=4), ACT.Copy).then_inc(h_cp, 1)
            gaw = ar[:, 27264:27264 + KT * 2 * RANK].rearrange("p (k n) -> p k n", k=KT)
            act.dma_start(gaw, w_in[:, :, COL_GA:COL_SQ]).then_inc(ga_w, 16)

            n_col = 0

            def mod_column():
                nonlocal n_col
                act.wait_ge(slot_used, SLOTS + (G_M2 if n_col < 8 else G_M3 - 32) + 4 * n_col + 4)
                if n_col >= 2:
                    act.wait_ge(mc_st[n_col % 2], 16 * (n_col // 2))
                act.activation(modc[0:2, n_col % 2, :], ps[0:2, 7, :], ACT.Copy).then_inc(mc_ev, 1)
                n_col += 1

            sp = Split(act, True)
            act.wait_ge(h_cp, 4 * NT)
            sp.chunk(0, 0, AHEAD)
            for i, dst in enumerate((gqT, gkT)):
                sp.chunk(i, AHEAD)
                sp.chunk(i + 1, 0, AHEAD)
                for b in range(4):
                    bank_done(act, pj_pe, i, b, P_A + KT * i + KT - 1)
                    act.activation(dst[:, b, 0:TA], ps[:, b, 0:TA], ACT.Copy).then_inc(pj_ev, 1)
                bank_done(act, pj_pe, i, 4, P_A + KT * i + KT - 1)
                act.activation(dst[:, :, TA:TOK], ps[:, 4:6, :].rearrange("p b (c t) -> p (b c) t", c=2), ACT.Copy)\
                    .then_inc(pj_ev, 1)
            for i in range(2):
                sp.chunk(2 + i, AHEAD)
                if i == 0:
                    sp.chunk(3, 0, AHEAD)
                for b in range(NT):
                    bank_done(act, pj_pe, 2 + i, b, P_A + KT * (2 + i) + KT - 1)
                    act.activation(gv[:, b, i * BANK:(i + 1) * BANK], ps[:, b, :], ACT.Copy).then_inc(pj_ev, 1)
            act.wait_ge(ga_pe, 1)
            act.wait_ge(wdec0, 1)
            act.activation(gaT[0:2 * RANK, 0:LAT], ps[0:2 * RANK, 5, :], ACT.Copy).then_inc(ga_ev, 1)
            act.activation(gaT[0:2 * RANK, LAT:TOK], ps[0:2 * RANK, 6, 0:CTX], ACT.Copy).then_inc(ga_ev, 1)

            def gla_logs(s):
                if s:
                    act.wait_ge(g_b, s)
                act.wait_ge(z_pe, 2 * s + 1)
                act.activation(tz[:, 0:LAT], ps[:, 4, :], ACT.Abs).then_inc(z_ab, 1)
                act.wait_ge(z_pe, 2 * s + 2)
                act.activation(tz[:, LAT:TOK], ps[:, 4, 0:CTX], ACT.Abs).then_inc(z_ab, 1)
                act.wait_ge(z_ab, 2 * s + 2)
                ch.step(act.activation(tz, tz, ACT.Exp, scale=-1.0))
                act.activation(tz, tz, ACT.Ln, bias=1.0).then_inc(z_ln, 1)

            def gla_exps(s):
                act.wait_ge(g_b, s + 1)
                if s >= 2:
                    act.wait_ge(o_pe, 3 * (s - 1))
                    act.wait_ge(s_up, 9 * (s - 1))
                act.activation(xq2[s % 2], tB, ACT.Exp, scale=1.0 / TAU)
                if s:
                    act.wait_ge(at_pe, s)
                act.activation(xk, tB, ACT.Exp, scale=-1.0 / TAU)
                act.activation(tD, tD, ACT.Exp, scale=1.0 / TAU)
                act.activation(decay[:, s % 2, :], tc.rearrange("p (c t) -> p c t", t=CH)[:, :, CH - 1], ACT.Exp,
                               scale=1.0 / TAU).then_inc(g_e, 1)

            gla_logs(0)
            gla_exps(0)
            for s in range(2 * GH):
                act.wait_ge(kt_pe, s + 1)
                if s:
                    act.wait_ge(u_pe, 9 * s)
                act.activation(ks[:, 0:LAT], ps[:, 5, :], ACT.Copy)
                act.activation(ks[:, LAT:TOK], ps[:, 6, 0:P], ACT.Copy).then_inc(kt_cp, 1)
                if s + 1 < 2 * GH:
                    gla_logs(s + 1)
                    gla_exps(s + 1)
                mod_column()
                if s % 2:
                    h = s // 2
                    act.wait_ge(o_ev, 3 * (s + 1))
                    for t in range(NT):
                        ch.step(act.activation(tz[:, 0:GV], og[:, t, h * GV:(h + 1) * GV], ACT.Square,
                                               accum_out=rs_gla[:, t * GH + h:t * GH + h + 1]))
            act.activation(rs_gla[:, :], rs_gla[:, :], ACT.Sqrt, scale=1.0 / GV, bias=epsb[:, :]).then_inc(o_sq, 1)
            act.wait_ge(st_out, 16 * 2 * GH)
            sp.chunk(4, 0, AHEAD)
            for c in range(2):
                sp.chunk(4 + c, AHEAD)
                sp.chunk(5 + c, 0, AHEAD)
                for b in range(NT):
                    n = c * NT + b
                    bank_done(act, pj_pe, 4 + c, b, P_A + KT * (4 + c) + KT - 1)
                    if n >= 2:
                        act.wait_ge(gr_o, n - 1)
                    act.activation(sil[:, n % 2, :], ps[:, b, :], ACT.Silu).then_inc(pj_ev, 1)
                for b in range(NT):
                    n = c * NT + b
                    act.wait_ge(gr_tr, n + 1)
                    act.activation(oT[:, 4 * c:4 * c + 4, b * P:(b + 1) * P],
                                   ps[:, 5 + b % 2, :].rearrange("p (k t) -> p k t", k=4), ACT.Copy).then_inc(gr_cp, 1)
            for i in range(2):
                sp.chunk(6 + i, AHEAD)
                sp.chunk(7 + i, 0, AHEAD)
                for b in range(4):
                    bank_done(act, pj_pe, 6 + i, b, P_A + KT * (6 + i) + KT - 1)
                    act.activation(swT[:, 4 * i + b, 0:TA], ps[:, b, 0:TA], ACT.Copy).then_inc(pj_ev, 1)
                bank_done(act, pj_pe, 6 + i, 4, P_A + KT * (6 + i) + KT - 1)
                act.activation(swT[:, 4 * i:4 * i + 4, TA:TOK], ps[:, 4:6, :].rearrange("p b (c t) -> p (b c) t", c=2),
                               ACT.Copy).then_inc(pj_ev, 1)
            sp.chunk(8, AHEAD)
            for b in range(NT):
                bank_done(act, pj_pe, 8, b, P_A + KT * 8 + KT - 1)
                kd = skr[:, b, :].rearrange("p (h e d) -> p h e d", h=SKV, e=2)
                kp = ps[:, b, 0:SKV * HD].rearrange("p (h d) -> p h d", h=SKV)
                act.activation(kd[:, :, 0, :], kp, ACT.Copy).then_inc(k_dup, 1)
                act.activation(kd[:, :, 1, :], kp, ACT.Copy).then_inc(k_dup, 1)
                if b == NT - 1:
                    act.activation(krow_out, ps[:, b, 0:SKV * HD], ACT.Copy).then_inc(k_dup, 1)
                act.activation(svr[:, b, :], ps[:, b, SKV * HD:2 * SKV * HD], ACT.Copy).then_inc(k_dup, 1)
            for g in range(SKV):
                act.wait_ge(k_tr, g + 1)
                act.activation(skT[:, g, 0:LAT], ps[:, 0, :], ACT.Copy).then_inc(k_cp, 1)
                act.activation(skT[:, g, LAT:TOK + P], ps[:, 1, 0:2 * P], ACT.Copy).then_inc(k_cp, 1)
            n_pt = 0
            for u, (t, g) in enumerate(units):
                keys, blocks = unit_keys(t)
                act.wait_ge(sc_mx, u + 1)
                sf = soft[:, u % 2]
                act.activation(sf[:, 3, :], sf[:, 3, :], ACT.Exp)
                for j in range(GRP):
                    s = Sbuf[:, u % 2, j * BANK:j * BANK + len(blocks) * P]
                    a = act.activation(s, s, ACT.Exp, bias=sf[:, 1, j:j + 1], accum_out=sf[:, 2, j:j + 1])
                a.then_inc(sc_e, 1)
                if u:
                    n_pt = copy_pT(act, u - 1, n_pt)
                    copy_o(act, u - 1)
                while n_col < 8 + sum(2 if v % 5 < 3 else 1 for v in range(u + 1)) // 4:
                    mod_column()
            n_pt = copy_pT(act, len(units) - 1, n_pt)
            copy_o(act, len(units) - 1)

            def merged_copies(n):
                act.wait_ge(mT_free, n + 1)
                for b in range(NT):
                    act.wait_ge(mt_pe, n * NT + (b + 1))
                    act.activation(mTc[:, :, b * P:(b + 1) * P],
                                   ps[:, 5 + b % 3, :].rearrange("p (k t) -> p k t", k=4), ACT.Copy).then_inc(mt_cp, 1)

            def gates_act(n, first, last):
                gate_split(sp, n, 0, AHEAD, KT)
                for q in (0, 2):
                    gate_split(sp, n, q + 1, 0, AHEAD)
                    for b in range(NT):
                        bank_done(act, gt_pe, n * 4 + q, b, n * 48 + (P_GATE + sum(GATE_PIECES[q]) - 1))
                        act.activation(sg[:, b, :], ps[:, b, :], ACT.Sigmoid).then_inc(gt_act, 1)
                    if q == 0 and not first:
                        merged_copies(n - 1)
                    gate_split(sp, n, q + 1, AHEAD, 8)
                    if q == 0:
                        gate_split(sp, n, 2, 0, KT)
                if not last:
                    gate_split(sp, n + 1, 0, 0, AHEAD)

            gate_split(sp, 0, 0, 0, AHEAD)
            gates_act(0, True, False)
            with act.Fori(1, 3) as n:
                gates_act(n, False, False)
            gates_act(3, False, True)
            merged_copies(3)
            out_pieces(sp, act, 0, 0, AHEAD)
            with act.Fori(0, 3) as n:
                out_pieces(sp, act, n, AHEAD, KT)
                out_pieces(sp, act, n + 1, 0, AHEAD)
            out_pieces(sp, act, 3, AHEAD, KT)
            for t in range(NT):
                act.wait_ge(wo_ev, 4 * NT + t + 1)
                ch.step(act.activation(junkx, x1[:, t, :], ACT.Square, accum_out=stat[:, t:t + 1]))
                act.activation(stat[:, NT + t:NT + t + 1], stat[:, t:t + 1], ACT.Sqrt, scale=1.0 / D,
                               bias=epsb[:, :]).then_inc(n2_sq, 1)
                act.wait_ge(n2_tr, t + 1)
                if t >= 2:
                    act.wait_ge(lg_pe, t - 1)
                act.activation(h2T[:, t % 2], ps[:, 0:4, :].rearrange("p b (k t) -> p (b k) t", k=4), ACT.Copy).then_inc(n2_cp, 1)
            act.wait_ge(af_e, 1)
            act.activation(aff[:, 0], aff[:, 0], ACT.Exp).then_inc(af_e, 1)

            def copy_xs():
                for dst, src in xs_parts:
                    a = act.activation(xsT[:, 0, dst:dst + src.shape[1], :], src, ACT.Copy)
                a.then_inc(xs_h, 1)

            def split_expert(e, lo, hi):
                for j in range(lo, hi):
                    s = j % SP
                    act.wait_ge(exp_ready[j % ESLOTS], e * (16 * EXP_G // ESLOTS) + 16 * (j // ESLOTS + 1))
                    act.wait_ge(piece_used, e * EXP_G + (P_EXP + j + 1))
                    act.activation(spE[:, s, 0, :], exp_slot[j % ESLOTS], ACT.Copy).then_inc(piece_high, 1)

            act.wait_ge(xs_tr, 1)
            copy_xs()
            split_expert(0, 0, AHEAD)

            def expert_act(e, last):
                split_expert(e, AHEAD, 19)
                act.wait_ge(piece_used, e * EXP_G + (SP + P_EXP + 16))
                act.activation(hid[0:CAP, :], ps[0:CAP, 0:2, :].rearrange("p b n -> p (b n)"), ACT.Silu).then_inc(hd_s, 1)
                act.wait_ge(hd_tr, e + 1)
                for dst, src in hid_parts:
                    a = act.activation(hidT[:, 0, dst:dst + src.shape[1], :], src, ACT.Copy)
                a.then_inc(hd_h, 1)
                act.wait_ge(xs_tr, e + 2)
                copy_xs()
                split_expert(e, 19, EXP_G)
                if not last:
                    split_expert(e + 1, 0, AHEAD)

            with act.Fori(0, NE - 1) as e:
                expert_act(e, False)
            expert_act(NE - 1, True)
            for t in range(NT):
                act.wait_ge(y_ld[t], 16)
                ch.step(act.activation(junk2, yrow[:, t, :], ACT.Square, accum_out=stat[:, t:t + 1]))
                act.activation(stat[:, NT + t:NT + t + 1], stat[:, t:t + 1], ACT.Sqrt, scale=1.0 / D,
                               bias=epsb[:, :]).then_inc(y_sq, 1)

        @block.vector
        def _(dve):
            ch = Chain(dve, dve_step)
            dve.memset(epsb[:, :], EPS).then_inc(s_eps, 1)
            dve.sem_inc(mod_ev, 1)
            dve.sem_inc(pj_ev, NT)
            dve.sem_inc(gt_dve, NT)
            dve.sem_inc(wo_ev, NT)
            dve.sem_inc(gr_cp, 2)
            dve.sem_inc(mt_cp, 1)
            dve.sem_inc(mT_free, 1)
            dve.sem_inc(ye_free, 1)
            dve.sem_inc(ye_r, 1)
            dve.wait_ge(s_cst, 96)
            with dve.Fori(0, 2) as m:
                dve.wait_ge(slot_used, m * KT + (SLOTS + G_MOD + KT))
                dve.tensor_tensor(modrow[0:2, ds(m * D, D)], ps[0:2, 0:4, :].rearrange("p b n -> p (b n)"),
                                  bmod[0:2, ds(m * D, D)], ALU.add).then_inc(mod_ev, 1)
            dve.wait_ge(mod_ev, 3)
            sc = modrow[0:2, D:2 * D]
            dve.scalar_tensor_tensor(sc, sc, 1.0, g1[0:2, :], ALU.add, ALU.mult).then_inc(mod_a, 1)
            dve.wait_ge(h_sq, NT)
            ch.step(dve.reciprocal(stat[:, NT:2 * NT], stat[:, NT:2 * NT]))
            for t in range(NT):
                who = t // 4
                dve.wait_ge(mod_ab[who], 32)
                if t >= 2:
                    dve.wait_ge(h_tr, 4 * (t - 1))
                ch.step(dve.scalar_tensor_tensor(hrow[:, t % 2, :], xrow[:, t, :], stat[:, NT + t:NT + t + 1],
                                                 Ah[:, who, :], ALU.mult, ALU.mult))
                dve.tensor_tensor(hrow[:, t % 2, :], hrow[:, t % 2, :], Bh[:, who, :], ALU.add).then_inc(h_row, 1)
            sp = Split(dve, False)
            dve.wait_ge(h_tr, 4 * NT)
            dve.memset(gaT[2 * RANK:2 * RANK + 1, :], 1.0)
            dve.memset(wdec[0:2 * RANK + 1, :, :], 0.0).then_inc(wdec0, 1)
            for i in range(4):
                sp.chunk(i)
            dve.wait_ge(ga_pe, 1)
            ch.step(dve.memset(aTm, 0.0))

            def z_min(s, part):
                lo, n = ((0, LAT), (LAT, CTX))[part]
                dve.wait_ge(z_ab, 2 * s + part + 1)
                dve.tensor_scalar(tg[:, lo:lo + n], ps[:, 4, 0:n], 0.0, None, ALU.min).then_inc(z_mn, 1)

            def gla_decays(s):
                dr = s % 2
                dve.wait_ge(z_mn, 2 * s + 2)
                dve.wait_ge(z_ln, s + 1)
                ch.step(dve.tensor_tensor(tg, tg, tz, ALU.subtract))
                if s:
                    dve.wait_ge(g_e, s)
                ch.step(dve.tensor_tensor_scan(tc, cst[:, C_RST:C_RST + TOK], tg, 0.0, ALU.mult, ALU.add))
                c3 = tc.rearrange("p (c t) -> p c t", t=CH)
                total = c3[:, :, CH - 1:CH].to_broadcast([P, NCH, CH])
                if s:
                    dve.wait_ge(kt_pe, s)
                if dr:
                    dve.tensor_tensor(tD, tc, tg, ALU.subtract)
                    ch.step(dve.tensor_tensor(tB.rearrange("p (c t) -> p c t", t=CH), total, c3, ALU.subtract))
                    dve.tensor_tensor(tB, tB, tg, ALU.add).then_inc(g_b, 1)
                else:
                    dve.tensor_tensor(tD.rearrange("p (c t) -> p c t", t=CH), total, c3, ALU.subtract)
                    dve.tensor_copy(tB, tc).then_inc(g_b, 1)

            def gla_scaled(s):
                h, xq = s // 2, xq2[s % 2]
                dve.wait_ge(g_e, s + 1)
                dve.tensor_tensor(tD, gkT[:, h, :], tD, ALU.mult)
                dve.scalar_tensor_tensor(xq, gqT[:, h, :], float(GK) ** -0.5, xq, ALU.mult, ALU.mult)
                dve.tensor_tensor(xk, gkT[:, h, :], xk, ALU.mult).then_inc(g_m, 1)

            z_min(0, 0)
            z_min(0, 1)
            gla_decays(0)
            gla_scaled(0)
            for s in range(2 * GH):
                h, dr = s // 2, s % 2
                dve.wait_ge(at_pe, s + 1)
                mask = cst[:, C_MB if dr else C_MF:][:, 0:P].bitcast(I32)
                if s >= 2:
                    dve.wait_ge(o_pe, 3 * (s - 1))
                for t in range(NT):
                    src = ps[:, 3, t * P:(t + 1) * P] if t < 4 else ps[:, 2, 2 * GV - P:2 * GV]
                    a = dve.copy_predicated(aTm[:, dr, t * P:(t + 1) * P], mask, src)
                a.then_inc(at_cp, 1)
                if s + 1 < 2 * GH:
                    z_min(s + 1, 0)
                order = ([9, 8] if dr else [8, 9]) + (list(range(7, 0, -1)) if dr else list(range(7)))
                if s >= 2:
                    dve.wait_ge(st_out, 16 * (s - 1))
                dve.wait_ge(st_ld[dr], 16 * (h + 1))
                for u, c in enumerate(order):
                    bank, half, made, _ = U_PLACE[u]
                    U = ps[:, bank, half * GV:(half + 1) * GV]
                    dve.wait_ge(u_pe, 9 * s + made)
                    if u == 0:
                        dve.tensor_copy(st[:, dr, 8, :], U).then_inc(s_up, 1)
                        dve.wait_ge(s_up, 9 * s + 1)
                        continue
                    src, dst = (8, 9) if u == 1 else (u - 2, u - 1)
                    dve.scalar_tensor_tensor(st[:, dr, dst, :], st[:, dr, src, :], decay[:, dr, c:c + 1], U,
                                             ALU.mult, ALU.add).then_inc(s_up, 1)
                    dve.wait_ge(s_up, 9 * s + u + 1)
                if s + 1 < 2 * GH:
                    z_min(s + 1, 1)
                    gla_decays(s + 1)
                    gla_scaled(s + 1)
                for i, b in enumerate((2, 1, 0) if dr else (2, 0, 1)):
                    n = 1 if b == 2 else 2
                    src = ps[:, b, 0:n * GV].rearrange("p (t v) -> p t v", t=n)
                    dst = og[:, 2 * b:2 * b + n, h * GV:(h + 1) * GV]
                    dve.wait_ge(o_pe, 3 * s + i + 1)
                    if dr:
                        dve.tensor_tensor(dst, dst, src, ALU.add).then_inc(o_ev, 1)
                    else:
                        dve.tensor_copy(dst, src).then_inc(o_ev, 1)
                if dr == 0:
                    dve.wait_ge(o_ev, 3 * (s + 1))
            dve.wait_ge(o_sq, 1)
            ch.step(dve.reciprocal(rs_gla[:, :], rs_gla[:, :]))
            sp.chunk(4, 0, AHEAD)
            for c in range(2):
                sp.chunk(4 + c, AHEAD)
                sp.chunk(5 + c, 0, AHEAD)
                for b in range(NT):
                    n = c * NT + b
                    dve.wait_ge(pj_ev, NT * (5 + c) + b + 1)
                    if n >= 2:
                        dve.wait_ge(gr_tr, n - 1 + (b == 0))
                    o = onr[:, b % 2, :]
                    for hh in range(2):
                        h = 2 * c + hh
                        a = dve.scalar_tensor_tensor(o[:, hh * GV:(hh + 1) * GV], og[:, b, h * GV:(h + 1) * GV],
                                                     rs_gla[:, b * GH + h:b * GH + h + 1],
                                                     glag[:, h * GV:(h + 1) * GV], ALU.mult, ALU.mult)
                    ch.step(a)
                    dve.tensor_tensor(o, o, sil[:, n % 2, :], ALU.mult).then_inc(gr_o, 1)
            sp.chunk(6, AHEAD)
            sp.chunk(7)
            sp.chunk(8)
            for i in range(8):
                dve.wait_ge(pj_ev, NT * (8 + i // 4))
                if i >= 1:
                    dve.wait_ge(sq_rp, i)
                ch.step(dve.tensor_tensor(rp[:, 0, :], swT[:, i, 0:LAT], cst[:, C_COS:C_COS + LAT], ALU.mult))
                dve.wait_ge(sq_pm, i + 1)
                ch.step(dve.tensor_tensor(rp[:, 1, :], ps[:, 5 + i % 2, :], cst[:, C_SIN:C_SIN + LAT], ALU.mult))
                dve.tensor_tensor(swT[:, i, 0:LAT], rp[:, 0, :], rp[:, 1, :], ALU.add).then_inc(sq_rp, 1)
            for g in range(SKV):
                dve.wait_ge(k_cp, 2 * g + 2)
                if g:
                    dve.wait_ge(k_rp, g)
                else:
                    dve.wait_ge(sq_rp, 8)
                ch.step(dve.tensor_tensor(rp[:, 0, :], skT[:, g, 0:LAT], cst[:, C_COS:C_COS + LAT], ALU.mult))
                dve.wait_ge(k_pm, g + 1)
                ch.step(dve.tensor_tensor(rp[:, 1, :], ps[:, 2 + g % 2, :], cst[:, C_SIN:C_SIN + LAT], ALU.mult))
                dve.tensor_tensor(skT[:, g, 0:LAT], rp[:, 0, :], rp[:, 1, :], ALU.add).then_inc(k_rp, 1)

            def softmax_front(u):
                t, g = units[u]
                _, blocks = unit_keys(t)
                nk = len(blocks) * P
                S = Sbuf[:, u % 2, :].rearrange("p (j n) -> p j n", j=GRP)[:, :, 0:nk]
                sf = soft[:, u % 2]
                dve.wait_ge(sc_pe, u + 1)
                if u >= 2:
                    dve.wait_ge(pt_pe, sum(len(unit_keys(units[v][0])[1]) for v in range(u - 1)))
                src = ps[:, 0:GRP, 0:nk]
                if t == 4:
                    dve.tensor_scalar(S, src, HD ** -0.5, None, ALU.mult).then_inc(sc_m, 1)
                else:
                    lo = {0: C_SW + P, 3: C_SW3}.get(t, C_SW)
                    m = cst[:, lo:lo + nk].unsqueeze(1).to_broadcast([P, GRP, nk])
                    dve.scalar_tensor_tensor(S, src, HD ** -0.5, m, ALU.mult, ALU.add).then_inc(sc_m, 1)
                dve.wait_ge(sc_m, u + 1)
                ch.step(dve.tensor_reduce(sf[:, 0, :], S, AX.X, ALU.max))
                ch.step(dve.tensor_tensor(sf[:, 0, :], sf[:, 0, :], sink[:, GRP * g:GRP * g + GRP], ALU.max))
                dve.tensor_tensor(sf[:, 3, :], sink[:, GRP * g:GRP * g + GRP], sf[:, 0, :], ALU.subtract)
                dve.tensor_scalar(sf[:, 1, :], sf[:, 0, :], -1.0, None, ALU.mult).then_inc(sc_mx, 1)

            def softmax_back(u):
                t, g = units[u]
                nk = len(unit_keys(t)[1]) * P
                sf = soft[:, u % 2]
                dve.wait_ge(sc_e, u + 1)
                ch.step(dve.tensor_tensor(sf[:, 2, :], sf[:, 2, :], sf[:, 3, :], ALU.add))
                ch.step(dve.reciprocal(sf[:, 4, :], sf[:, 2, :]))
                for j in range(GRP):
                    s = Sbuf[:, u % 2, j * BANK:j * BANK + nk]
                    a = dve.tensor_scalar(s, s, sf[:, 4, j:j + 1], None, ALU.mult)
                a.then_inc(sc_n, 1)

            softmax_front(0)
            for u in range(len(units)):
                if u + 1 < len(units):
                    softmax_front(u + 1)
                softmax_back(u)
            dve.wait_ge(kv_st, 32)
            ch2 = Chain(dve, dve2_step)
            def gates_dve(n, last):
                gate_split(sp, n, 0, AHEAD, KT)
                gate_split(sp, n, 1, 0, 8)
                gate_split(sp, n, 2, 0, AHEAD)
                for b in range(NT):
                    bank_done(dve, gt_pe, n * 4 + 1, b, n * 48 + (P_GATE + sum(GATE_PIECES[1]) - 1))
                    dve.wait_ge(gt_act, n * 10 + (b + 1))
                    dve.tensor_tensor(mrow[:, b, :], ps[:, b, :], sg[:, b, :], ALU.mult).then_inc(gt_dve, 1)
                gate_split(sp, n, 2, AHEAD, KT)
                gate_split(sp, n, 3, 0, 8)
                if not last:
                    gate_split(sp, n + 1, 0, 0, AHEAD)
                for b in range(NT):
                    bank_done(dve, gt_pe, n * 4 + 3, b, n * 48 + (P_GATE + sum(GATE_PIECES[3]) - 1))
                    dve.wait_ge(gt_act, n * 10 + (NT + b + 1))
                    dve.wait_ge(gt_dve, n * 10 + (2 * NT + b))
                    ch2.step(dve.tensor_tensor(mtmp, ps[:, b, :], sg[:, b, :], ALU.mult))
                    dve.tensor_tensor(mrow[:, b, :], mrow[:, b, :], mtmp, ALU.add).then_inc(gt_dve, 1)

            gate_split(sp, 0, 0, 0, AHEAD)
            with dve.Fori(0, 3) as n:
                ch2.enter(n, NT)
                gates_dve(n, False)
                ch2.leave(3)
            gates_dve(3, True)
            def out_dve(n, last):
                out_pieces(sp, dve, n, AHEAD, KT)
                if not last:
                    out_pieces(sp, dve, n + 1, 0, AHEAD)
                for b in range(NT):
                    who = b // 4
                    bank_done(dve, wo_pe, n, b, n * KT + (P_OUT + KT - 1))
                    dve.wait_ge(wo_ev, n * NT + (NT + b))
                    cols = ds(n * BANK, BANK)
                    ch2.step(dve.tensor_tensor(wtmp[:, b % 2, :], ps[:, b, :], gt1[:, who, cols], ALU.mult))
                    xv = x1[:, b, cols]
                    dve.tensor_tensor(xv, xv, wtmp[:, b % 2, :], ALU.add).then_inc(wo_ev, 1)

            out_pieces(sp, dve, 0, 0, AHEAD)
            dve.wait_ge(wo_ld, 16 * 2)
            dve.wait_ge(xr_ld, 16 * NT)
            with dve.Fori(0, 3) as n:
                ch2.enter(n, NT)
                out_dve(n, False)
                ch2.leave(3)
            out_dve(3, True)
            dve.wait_ge(wo_ld, 16 * 10)
            for who in range(2):
                a = dve.scalar_tensor_tensor(A2[:, who, :], A2[:, who, :], 1.0, g2, ALU.add, ALU.mult)
            ch.step(a)
            for t in range(NT):
                who = t // 4
                dve.wait_ge(n2_sq, t + 1)
                ch.step(dve.reciprocal(stat[:, NT + t:NT + t + 1], stat[:, NT + t:NT + t + 1]))
                if t >= 2:
                    dve.wait_ge(n2_tr, t - 1)
                    dve.wait_ge(n2_st[t % 2], 16 * (t // 2))
                ch.step(dve.scalar_tensor_tensor(h2row[:, t % 2], x1[:, t, :], stat[:, NT + t:NT + t + 1], A2[:, who, :],
                                                 ALU.mult, ALU.mult))
                dve.tensor_tensor(h2row[:, t % 2], h2row[:, t % 2], B2[:, who, :], ALU.add).then_inc(n2_h, 1)
            a0, a1 = aff[:, 0], aff[:, 1]
            dve.wait_ge(lg_pe, NT)
            lg = ps[:, 4, 0:NT * NE].rearrange("p (t e) -> p t e", t=NT)
            ch.step(dve.tensor_reduce(a1[:, :, 0], lg, AX.X, ALU.max))
            dve.tensor_tensor(a0, lg, a1[:, :, 0:1].to_broadcast([P, NT, NE]), ALU.subtract).then_inc(af_e, 1)
            dve.wait_ge(af_e, 2)
            ch.step(dve.tensor_reduce(a1[:, :, 1], a0, AX.X, ALU.add))
            ch.step(dve.reciprocal(a1[:, :, 2], a1[:, :, 1]))
            dve.tensor_tensor(a0, a0, a1[:, :, 2:3].to_broadcast([P, NT, NE]), ALU.mult).then_inc(af_r, 1)
            dve.wait_ge(af_tr, 1)
            dve.tensor_copy(affT[0:NE, 0:LAT], ps[0:NE, 5, :])
            dve.tensor_copy(affT[0:NE, LAT:TOK], ps[0:NE, 6, 0:CTX]).then_inc(af_cp, 1)
            dve.wait_ge(af_cp, 1)
            for lo, n, at, cap in ((0, LAT, 0, CAP_L), (LAT, CTX, CAP_L, CAP_C)):
                a = affT[0:NE, lo:lo + n]
                for r in range(cap // 8):
                    v = vals[0:NE, at + 8 * r:at + 8 * r + 8]
                    ch.step(dve.max(v, a))
                    dve.max_index(idxu[0:NE, at + 8 * r:at + 8 * r + 8], v, a)
                    ch.step(dve.match_replace(a, v, a, -1.0))
            dve.tensor_copy(idxf[0:NE, 0:CAP_L], idxu[0:NE, 0:CAP_L])
            dve.tensor_scalar(idxf[0:NE, CAP_L:CAP], idxu[0:NE, CAP_L:CAP], float(LAT), None, ALU.add).then_inc(tk_d, 1)
            dve.wait_ge(tk_tr, 1)
            dve.tensor_copy(idxT[0:CAP, 0:NE], ps[0:CAP, 7, 0:NE]).then_inc(tk_cp, 1)
            dve.tensor_copy(idxT[0:CAP, NE:NE + 2], ps[0:CAP, 7, 0:2]).then_inc(tk_cp, 1)
            dve.tensor_copy(gateT[0:CAP, :], ps[0:CAP, 7, NE:2 * NE]).then_inc(tk_cp, 1)
            def low_xs():
                for dst, src in xs_parts:
                    n = src.shape[1]
                    a = dve.tensor_tensor(xsT[:, 1, dst:dst + n, :], src, xsT[:, 0, dst:dst + n, :].bitcast(F32),
                                          ALU.subtract)
                a.then_inc(xs_l, 1)

            def low_expert(e, lo, hi):
                for j in range(lo, hi):
                    s = j % SP
                    dve.wait_ge(piece_high, e * EXP_G + (P_EXP + j + 1))
                    dve.tensor_tensor(spE[:, s, 1, :], exp_slot[j % ESLOTS], spE[:, s, 0, :].bitcast(F32), ALU.subtract)\
                       .then_inc(piece_ready, 1)

            dve.wait_ge(xs_h, 1)
            low_xs()
            low_expert(0, 0, AHEAD)

            def expert_dve(e, last):
                low_expert(e, AHEAD, 19)
                dve.wait_ge(hd_s, e + 1)
                dve.tensor_tensor(hid[0:CAP, :], hid[0:CAP, :], ps[0:CAP, 2:4, :].rearrange("p b n -> p (b n)"),
                                  ALU.mult).then_inc(hd_r, 1)
                dve.wait_ge(hd_h, e + 1)
                for dst, src in hid_parts:
                    n = src.shape[1]
                    a = dve.tensor_tensor(hidT[:, 1, dst:dst + n, :], src, hidT[:, 0, dst:dst + n, :].bitcast(F32),
                                          ALU.subtract)
                a.then_inc(hd_cp, 1)
                dve.wait_ge(xs_h, e + 2)
                low_xs()
                low_expert(e, 19, EXP_G)
                if not last:
                    low_expert(e + 1, 0, AHEAD)
                dve.wait_ge(piece_used, e * EXP_G + (SP + P_EXP + EXP_G))
                dve.wait_ge(ye_free, e + 1)
                dve.scalar_tensor_tensor(ye[0:CAP, :], ps[0:CAP, 4:8, :].rearrange("p b n -> p (b n)"),
                                         gateT[0:CAP, ds(e, 1)], gt2[0:CAP, :], ALU.mult, ALU.mult).then_inc(ye_r, 1)

            with dve.Fori(0, NE - 1) as e:
                expert_dve(e, False)
            expert_dve(NE - 1, True)
            dve.wait_ge(gf_ld, 16)
            for t in range(NT):
                dve.wait_ge(y_sq, t + 1)
                ch.step(dve.reciprocal(stat[:, NT + t:NT + t + 1], stat[:, NT + t:NT + t + 1]))
                y = yrow[:, t, :]
                dve.scalar_tensor_tensor(y, y, stat[:, NT + t:NT + t + 1], gfin, ALU.mult, ALU.mult).then_inc(y_r, 1)


INS = ["x_prompt", "x_sample", "state_gla_fwd", "state_gla_bwd", "cache_k", "cache_v", "c", "c_ctx", "w_mod", "b_mod",
       "g_norm1", "w_in", "w_dec_f", "b_dec_f", "w_dec_b", "b_dec_b", "g_gla", "attn_sink", "w_branch_a",
       "w_branch_b", "w_out", "g_norm2", "w_router", "w_exp_gate", "w_exp_up", "w_exp_down", "g_final"]
OUTS = [("y_prompt", (1, CTX, D)), ("y_sample", (1, LAT, D)), ("ns_fwd", (1, 1, GH, GK, GV)),
        ("ns_bwd", (1, 1, GH, GK, GV)), ("nk", (1, 1, CTX, SKV, HD)), ("nv", (1, 1, CTX, SKV, HD))]


def kernel(**inputs):
    import concourse.bacc as bacc
    from concourse.bass_utils import run_bass_kernel_spmd

    nc = bacc.Bacc("TRN2", target_bir_lowering=False, num_devices=1)
    arrays = {name: np.ascontiguousarray(inputs[name]) for name in INS}
    arrays["consts"] = constants()
    T = {name: nc.dram_tensor(name, a.shape, F32, kind="ExternalInput").ap() for name, a in arrays.items()}
    for name, shape in OUTS:
        T[name] = nc.dram_tensor(name, shape, F32, kind="ExternalOutput").ap()
    build(nc, T)
    r = run_bass_kernel_spmd(nc, [arrays], core_ids=[0])
    return tuple(r.results[0][name] for name, _ in OUTS)
```

```python
from contextlib import ExitStack

import numpy as np

import concourse.bass as bass
from concourse import mybir

F32 = mybir.dt.float32
F32R = mybir.dt.float32r
I32 = mybir.dt.int32
U32 = mybir.dt.uint32
ALU = mybir.AluOpType
ACT = mybir.ActivationFunctionType
AX = mybir.AxisListType
ds = bass.ds

P = 128
D = 2048
KT = D // P
LAT, CTX = 512, 128
TOK = LAT + CTX
NT = TOK // P
EPS = 1e-6
BANK = 512

GH, GK, GV, RANK = 4, 128, 256, 16
TAU = 16.0
CH = 64
NCH = TOK // CH
LCH = LAT // CH

SH, SKV, HD = 16, 4, 64
GRP = SH // SKV

NE, FF = 16, 1024
FT = FF // P
CAP_L = 2 * LAT // NE
CAP_C = 2 * CTX // NE
CAP = CAP_L + CAP_C

COL_GV = 2 * GH * GK
COL_GR = COL_GV + GH * GV
COL_GA = COL_GR + GH * GV
COL_SQ = COL_GA + 2 * RANK
COL_SKV = COL_SQ + SH * HD
COL_GATE_A = COL_SKV + 2 * SKV * HD
COL_GATE_B = COL_GATE_A + D

SLOTS = 4
SLOT = 2048

G_MOD = 0
G_A = G_MOD + 2 * KT
G_M2 = G_A + 4 * 4
G_A2 = G_M2 + 8 * 4
G_M3 = G_A2 + 5 * 4
G_GATE = G_M3 + 4 * 4
G_OUT = G_GATE + 4 * 12
G_M4 = G_OUT + 4 * 4
G_M_COL = [G_M2 + 4 * c for c in range(8)] + [G_M3 + 4 * c for c in range(4)] + [G_M4 + 4 * c for c in range(4)]
EXP_G = 3 * 8
ESLOTS = 8

TA, TB = 3 * P, TOK - 3 * P

X_SQUARE, X_SCALE, X_TRANSPOSE, X_COPY = [[lag + 4 * t for t in range(NT)] for lag in (6, 7, 9, 10)]

MSLOTS = 3
SP = 4
AHEAD = 3
P_A = 0
P_GATE = P_A + 9 * KT
P_OUT = P_GATE + 4 * 48
GATE_PIECES = ((0, KT), (KT, 8), (KT + 8, KT), (2 * KT + 8, 8))
P_EXP = P_OUT + 4 * KT
P_END = P_EXP + NE * EXP_G

C_ID, C_MF, C_MB, C_RST, C_SW, C_SW3, C_COS, C_SIN, C_PERM = np.cumsum(
    [0, 128, 128, 128, 640, 512, 384, 512, 512]).tolist()
C_END = C_PERM + 128


def constants():
    c = np.zeros((P, C_END), np.float32)
    i = np.arange(P)
    c[:, C_ID:C_ID + P] = np.eye(P)
    same = i[:, None] // CH == i[None, :] // CH
    c[:, C_MF:C_MF + P] = same & (i[:, None] <= i[None, :])
    c[:, C_MB:C_MB + P] = same & (i[:, None] >= i[None, :])
    c[:, C_RST:C_RST + TOK] = (np.arange(TOK) % CH != 0)[None, :]
    before = np.where(i[None, :] >= i[:, None], 0.0, -1e30)
    after = np.where(i[None, :] <= i[:, None], 0.0, -1e30)
    c[:, C_SW:C_SW + P] = before
    c[:, C_SW + 2 * P:C_SW + 3 * P] = after
    c[:, C_SW3:C_SW3 + P] = before
    npair = HD // 4
    inv = (np.float32(10000.0) ** (-np.arange(npair, dtype=np.float32) / np.float32(npair))).astype(np.float32)
    tok = np.arange(LAT)
    d = i % HD
    pos = np.where((d < HD // 2)[:, None], (tok // 64)[None, :], (tok % 64)[None, :]).astype(np.float32)
    ang = pos * inv[d % npair][:, None]
    c[:, C_COS:C_COS + LAT] = np.cos(ang)
    c[:, C_SIN:C_SIN + LAT] = np.sin(ang)
    for m in range(P):
        if m % (2 * npair) < npair:
            c[m + npair, C_PERM + m] = -1.0
        else:
            c[m - npair, C_PERM + m] = 1.0
    return c


U_PLACE = [(5, 0, 3, 0), (6, 0, 4, 0), (5, 1, 3, 0), (6, 1, 4, 0), (5, 0, 7, 3), (6, 0, 8, 4), (5, 1, 7, 3),
           (6, 1, 8, 4), (5, 0, 9, 7)]


class Chain:

    def __init__(self, eng, sem):
        self.eng, self.sem, self.base, self.n = eng, sem, 0, 0

    def step(self, ins):
        ins.then_inc(self.sem, 1)
        self.n += 1
        self.eng.wait_ge(self.sem, self.base + self.n)

    def enter(self, i, per):
        self.start = self.n
        self.base = i * per
        self.per = per

    def leave(self, count):
        assert self.n - self.start == self.per, (self.n - self.start, self.per)
        self.n = self.start + count * self.per
        self.base = 0


def build(nc, T):
    w_mod = T["w_mod"][0].rearrange("(k p) n -> p k n", p=P)
    w_in = T["w_in"][0].rearrange("(k p) n -> p k n", p=P)
    w_a = T["w_branch_a"][0].rearrange("(k p) n -> p k n", p=P)
    w_b = T["w_branch_b"][0].rearrange("(k p) n -> p k n", p=P)
    w_out = T["w_out"][0].rearrange("(k p) n -> p k n", p=P)
    w_eg = T["w_exp_gate"][0].rearrange("e (p k) n -> e p k n", p=P)
    w_eu = T["w_exp_up"][0].rearrange("e (p k) n -> e p k n", p=P)
    w_ed = T["w_exp_down"][0].rearrange("e (p k) n -> e p k n", p=P)
    x_lat, x_ctx = T["x_sample"][0], T["x_prompt"][0]
    x_of = [x_lat[t * P:(t + 1) * P, :] for t in range(4)] + [x_ctx]
    y_of = [T["y_sample"][0][t * P:(t + 1) * P, :] for t in range(4)] + [T["y_prompt"][0]]
    mod_dram = nc.dram_tensor("mod_rows", [2, 6 * D], F32, kind="Internal").ap()
    h2_dram = nc.dram_tensor("h2_rows", [TOK, D], F32, kind="Internal").ap()
    mT_dram = nc.dram_tensor("merged_T", [P, KT, TOK], F32, kind="Internal").ap()
    y_dram = nc.dram_tensor("y_rows", [TOK, D], F32, kind="Internal").ap()

    def row_bcast(row, n=P):
        return row.partition_broadcast(n)

    with ExitStack() as ctx:
        def sb(name, shape, dt=F32):
            return ctx.enter_context(nc.sbuf_tensor(name, shape, dt))

        def sem(name):
            return ctx.enter_context(nc.semaphore(name))

        ps = ctx.enter_context(nc.psum_tensor("ps", [P, 8, BANK], F32))
        cst = sb("cst", [P, C_END])
        ring = sb("ring", [P, SLOTS, SLOT])
        hT = sb("hT", [P, KT, TOK])
        ar_at = nc.sbuf_base
        ar = sb("ar", [P, 30288])
        modc = sb("modc", [P, 2, BANK])
        condT = sb("condT", [P, KT, 2])
        stat = sb("stat", [P, 2 * NT])
        decay = sb("decay", [P, 2, NCH])
        rs_gla = sb("rs_gla", [P, NT * GH])
        sink = sb("sink", [P, SH])
        soft = sb("soft", [P, 2, 5, GRP])
        aff = sb("aff", [P, 2, NT, 16])
        idxT = sb("idxT", [P, NE + 2], U32)
        gateT = sb("gateT", [P, NE])
        epsb = sb("epsb", [P, 1])
        gidx = sb("gidx", [CAP, 1], U32)
        sidx = sb("sidx", [CAP, 1], U32)

        part = decay

        ident = cst[:, C_ID:C_ID + P]

        def area(at, *dims):
            n = int(np.prod(dims))
            v = ar[:, at:at + n]
            if len(dims) == 2:
                v = v.rearrange("p (a b) -> p a b", a=dims[0])
            if len(dims) == 3:
                v = v.rearrange("p (a b c) -> p a b c", a=dims[0], b=dims[1])
            return v

        def split_area(name, at, *dims):
            return nc.alloc_sbuf_tensor_at(name, [P, *dims], F32R, offset=ar_at + 4 * at)

        def hT_area(at, n):
            return hT[:, :, :].rearrange("p k t -> p (k t)")[:, at:at + n]

        modS = split_area("split_modulation", 0, MSLOTS, 2, SLOT)
        modrow = area(MSLOTS * 2 * SLOT, 2 * D)
        junk = area(8 * D, D)
        xrow = area(9 * D, NT, D)
        cond = area(14 * D, P)
        condR = split_area("split_cond", 14 * D + P, KT, 4)
        bgT = area(28864, 3 * KT)
        modT = area(28928, 2 * KT, 2)
        gqT, gkT = area(0, GH, TOK), area(2560, GH, TOK)
        gv = area(5120, NT, GH * GV)
        og = area(10240, NT, GH * GV)
        gaT = area(15360, TOK)
        wdec = area(16000, 2, GH * GK)
        st = area(17024, 2, 10, GV)
        tz, tg, tc, tB, tD, xq0, xk, ks = [area(22144 + TOK * i, TOK) for i in range(8)]
        xq2 = (xq0, area(29568, TOK))
        aTm = area(27264, 2, TOK)
        glag = area(28544, GH * GV)
        oT = area(0, 8, TOK)
        sil, onr = area(5120, 2, BANK), area(6144, 2, BANK)
        swT = area(5120, 8, TOK)
        skT = area(10240, SKV, TOK + P)
        svr = area(13312, NT + 1, SKV * HD)
        skr = area(14848, NT + 1, SKV * 2 * HD)
        Sbuf = area(17920, 2, GRP * BANK)
        pT = area(22016, 2, 4 * BANK)
        rp = area(27264, 2, BANK)
        krow_out = area(28544, SKV * HD)
        spW = split_area("split_weights", 18000, SP, 2, BANK)
        spX = split_area("split_tokens", 18000 + SP * 2 * BANK, SP, 2, TOK)
        mTc = area(10240, 4, TOK)
        mT_last = {12 + k: mTc[:, k, :] for k in range(4)}
        sg = area(15424, NT, BANK)
        mrow = area(27216, NT, BANK)
        mtmp = area(29776, BANK)
        x1 = area(0, NT, D)
        gt1 = area(13312, 2, D)
        wtmp = area(27216, NT, BANK)
        junkx = area(10240, D)
        A2 = hT_area(0, 2 * D).rearrange("p (a b) -> p a b", a=2)
        B2 = hT_area(2 * D, 2 * D).rearrange("p (a b) -> p a b", a=2)
        arows = area(12800, D)
        gt2 = area(28240, D)
        h2row = area(17408, 3, D)
        h2T = area(17408 + 3 * D, 2, KT, P)
        wrt = area(12800, KT, NE)
        lgT = area(13312, TOK)
        affT = area(25856, TOK)
        vals, idxf = area(26496, CAP), area(26576, CAP)
        idxu = area(26656, CAP).bitcast(U32)
        xs = area(0, D)
        xsT = split_area("split_xsT", 2048, 2, KT, CAP)
        hidT = split_area("split_hidT", 4608, 2, FT, CAP)
        hid = area(5888, FF)
        ye = area(6912, D)
        spE = split_area("split_experts", 8960, SP, 2, SLOT)
        exp_slot = [hT_area(i * SLOT, SLOT) for i in range(5)] + [area(25344, SLOT), ring[:, 0, :], ring[:, 1, :]]
        gfin = ring[:, 2, :]
        yrow = area(0, NT, D)
        junk2 = area(NT * D, D)

        s_cst = sem("consts_loaded")
        slot_ready = [sem(f"slot_ready{s}") for s in range(SLOTS)]
        slot_used = sem("slots_used")
        exp_ready = [sem(f"expert_slot_ready{s}") for s in range(ESLOTS)]
        piece_high, piece_ready, piece_used = sem("pieces_high"), sem("pieces_ready"), sem("pieces_used")
        mT_st, mT_free, mT_ld, xs_h, xs_l, hd_h = (sem("merged_stored"), sem("merged_free"), sem("merged_loaded"),
                                                   sem("xs_high"), sem("xs_low"), sem("hidden_high"))
        s_condT, s_condS, s_eps = sem("cond_transposed"), sem("cond_silu"), sem("eps_set")
        md_high, md_used, mr_a, mr_d, s_mT, mb_ld, rows_ld, h_m = (
            sem("mod_granule_high"), sem("mod_granule_used"), sem("mod_rows_by_act"), sem("mod_rows_by_dve"),
            sem("mod_rows_transposed"), sem("mod_bias"), sem("rows_loaded"), sem("h_modulated"))
        mc_ev, mc_st = sem("mod_column_evacuated"), [sem("mod_column_added0"), sem("mod_column_added1")]
        x_ld, h_sq, h_row, h_tr, h_cp = ([sem(f"x_loaded{t}") for t in range(NT)], sem("x_squared"), sem("h_rows"),
                                         sem("h_transposed"), sem("h_copied"))
        pj_pe, pj_ev = sem("projected"), sem("projection_evacuated")
        ga_w, s_wdec, ga_pe, ga_ev = sem("decay_in_loaded"), sem("decay_w_loaded"), sem("ga_product"), sem("ga_ready")
        wdec0 = sem("wdec_cleared")
        z_pe, z_ab, z_mn, z_ln, g_b, g_e, g_m = (
            sem("z_product"), sem("z_abs_read"), sem("z_min_read"), sem("z_log"), sem("gla_cumsum"),
                                           sem("gla_exp"), sem("gla_scaled"))
        kt_pe, kt_cp, at_pe, at_cp = sem("kst_transposed"), sem("kst_copied"), sem("aT_product"), sem("aT_masked")
        u_pe, s_up, o_pe, o_ev = sem("U_product"), sem("state_updated"), sem("o_product"), sem("o_evacuated")
        st_ld, st_out, o_sq = [sem("state0_loaded"), sem("state1_loaded")], sem("state_stored"), sem("o_squared")
        gr_o, gr_tr, gr_cp = sem("gr_gated"), sem("gr_transposed"), sem("gr_copied")
        sq_pm, sq_rp, kv_ld = sem("rope_permuted"), sem("roped"), sem("cache_loaded")
        k_dup, k_tr, k_cp, k_pm, k_rp, kv_st = (sem("k_doubled"), sem("k_transposed"), sem("k_copied"),
                                                sem("k_permuted"), sem("k_roped"), sem("cache_stored"))
        sc_pe, sc_m, sc_mx, sc_e, sc_n = sem("scores"), sem("scores_masked"), sem("scores_max"), sem("probs_exp"), sem("probs")
        pt_pe, pt_cp, pv_pe, pv_cp = sem("p_transposed"), sem("pT_copied"), sem("pv_product"), sem("pv_copied")
        gt_pe, gt_act, gt_dve = sem("gate_products"), sem("gate_sigmoid"), sem("gate_merged")
        mt_pe, mt_cp = sem("merged_transposed"), sem("merged_copied")
        wo_ld, xr_ld, wo_pe, wo_rd, wo_ev = (sem("gate1_loaded"), sem("x_again_loaded"), sem("out_products"),
                                              sem("out_product_read"), sem("x1_ready"))
        ar_ld, ar_f, ar_st, ab_ld, wr_ld, g2_ld, sq_part = (
            sem("scale2_rows_loaded"), sem("scale2_folded"), sem("scale2_stored"), sem("norm2_rows_loaded"),
            sem("w_router_loaded"), sem("gate2_loaded"), sem("first_squares"))
        n2_b, lg_cp, lr_pe = sem("first_squares_summed"), sem("logits_copied"), sem("logit_rows")
        n2_sq, n2_h, n2_tr, n2_cp, n2_st, lg_pe = (sem("x1_squared"), sem("h2_row"), sem("h2_transposed"),
                                                   sem("h2_copied"), [sem(f"h2_stored{i}") for i in range(3)],
                                                   sem("logits"))
        af_e, af_r, af_tr, af_cp, tk_d, tk_tr, tk_cp = (sem("aff_exp"), sem("aff_rows"), sem("aff_transposed"),
                                                        sem("aff_copied"), sem("topk"), sem("topk_transposed"), sem("topk_ready"))
        gi_cp, xs_ld, xs_tr = sem("gather_index"), sem("xs_gathered"), sem("xs_transposed")
        hd_s, hd_r, hd_tr, hd_cp, ye_r, ye_st = (
            sem("gate_silu"), sem("hidden"), sem("hidden_transposed"), sem("hidden_copied"),
            sem("expert_out"), sem("expert_added"))
        y_ld, y_sq, y_r = [sem(f"y_loaded{t}") for t in range(NT)], sem("y_squared"), sem("y_ready")
        gf_ld, y_sto = sem("gfinal_loaded"), sem("y_out")
        act_step, dve_step, dve2_step, pool_step = sem("act_step"), sem("dve_step"), sem("dve_loop_step"), sem("pool_step")
        loads_issued, rows_issued = sem("loads_issued"), sem("rows_issued")
        ye_free, x1_st = sem("ye_free"), sem("x1_stored")

        def gate_split(sp, n, q, lo, hi):
            first = GATE_PIECES[q][0]
            sp.pieces(P_GATE + first, n * 48, G_GATE + first // 4, n * 3, (hT, oT, hT, swT)[q], lo, hi)

        def out_pieces(sp, eng, n, lo, hi):
            if lo == 0:
                eng.wait_ge(mT_ld, 16 * 3)
            sp.pieces(P_OUT, n * KT, G_OUT, n, hT, lo, min(hi, 12))
            sp.pieces(P_OUT, n * KT, G_OUT, n, mT_last, max(lo, 12), hi)

        units = [(t, g) for t in range(NT) for g in range(SKV)]

        def unit_keys(t):
            if t == NT - 1:
                return [(LAT, P)], [NT - 1]
            lo, hi = max(t - 1, 0), min(t + 1, LAT // P - 1)
            return [(lo * P, (hi - lo + 1) * P), (TOK, P)], [*range(lo, hi + 1), NT]

        def copy_pT(act, u, n):
            for i, _ in enumerate(unit_keys(units[u][0])[1]):
                act.wait_ge(pt_pe, n + 1)
                if u >= 2:
                    act.wait_ge(pv_pe, u - 1)
                act.activation(pT[:, u % 2, i * BANK:(i + 1) * BANK], ps[:, 4 + n % 2, :], ACT.Copy).then_inc(pt_cp, 1)
                n += 1
            return n

        def copy_o(act, u):
            t, g = units[u]
            act.wait_ge(pv_pe, u + 1)
            act.activation(swT[:, 2 * g:2 * g + 2, t * P:(t + 1) * P],
                           ps[:, 6, 0:2 * P].rearrange("p (c q) -> p c q", c=2), ACT.Copy).then_inc(pv_cp, 1)

        def parts(*places):
            return [(k, ps[:, b, at * CAP:(at + n) * CAP].rearrange("p (k t) -> p k t", k=n)) for k, b, at, n in places]

        xs_parts = parts((0, 2, 0, 6), (6, 3, 0, 6), (12, 1, 2, 4))
        hid_parts = parts((0, 0, 0, 6), (6, 1, 0, 2))

        def bank_done(eng, done, before, b, last):
            if b < 4:
                eng.wait_ge(done, before * 4 + (b + 1))
            else:
                eng.wait_ge(piece_used, last + (SP + 1))

        class Split:

            def __init__(self, eng, high):
                self.eng, self.high = eng, high

            def pieces(self, first, turn, granule, gturn, src, lo, hi):
                for k in range(lo, hi):
                    s, g = (first + k) % SP, granule + k // 4
                    raw = ring[:, g % SLOTS, :].rearrange("p (k n) -> p k n", k=4)[:, k % 4, :]
                    if self.high:
                        if k % 4 == 0:
                            self.eng.wait_ge(slot_ready[g % SLOTS], gturn * 16 + 16 * (g // SLOTS + 1))
                        self.eng.wait_ge(piece_used, turn + (first + k + 1))
                        self.eng.activation(spW[:, s, 0, :], raw, ACT.Copy)
                        self.eng.activation(spX[:, s, 0, :], (src[k] if type(src) is dict else src[:, k, :]), ACT.Copy).then_inc(piece_high, 1)
                    else:
                        self.eng.wait_ge(piece_high, turn + (first + k + 1))
                        a = self.eng.tensor_tensor(spW[:, s, 1, :], raw, spW[:, s, 0, :].bitcast(F32), ALU.subtract)
                        if k % 4 == 3:
                            a.then_inc(slot_used, 1)
                        self.eng.tensor_tensor(spX[:, s, 1, :], (src[k] if type(src) is dict else src[:, k, :]), spX[:, s, 0, :].bitcast(F32),
                                               ALU.subtract).then_inc(piece_ready, 1)

            def chunk(self, i, lo=0, hi=KT):
                self.pieces(P_A + KT * i, 0, G_A + 4 * i if i < 4 else G_A2 + 4 * (i - 4), 0, hT, lo, hi)

        block = ctx.enter_context(nc.Block())

        @block.sync
        def _(sync):
            def load(g, src, dst=None):
                first, turn = g
                s = first % SLOTS
                sync.wait_ge(slot_used, first + turn + 1)
                sync.sem_inc(loads_issued, 1)
                out = ring[:, s, :] if dst is None else dst(ring[:, s, :])
                sync.dma_start(out, src).then_inc(slot_ready[s], 16)

            def k4(v):
                return v.rearrange("p (k n) -> p k n", k=4)

            def k2(v):
                return v.rearrange("p (k n) -> p k n", k=2)

            def modulation(first, count, col):
                with sync.Fori(0, count) as c:
                    for j in range(4):
                        load((first + j, c * 4), w_mod[:, 4 * j:4 * j + 4, ds(c * BANK + col, BANK)], k4)

            def projection(first, count, col):
                with sync.Fori(0, count) as c:
                    for j in range(4):
                        load((first + j, c * 4), w_in[:, 4 * j:4 * j + 4, ds(c * BANK + col, BANK)], k4)

            with sync.Fori(0, 2) as m:
                for j in range(KT):
                    load((G_MOD + j, m * KT), w_mod[:, j, ds(m * D, D)])
            projection(G_A, 4, 0)
            modulation(G_M2, 8, 2 * D)
            projection(G_A2, 2, COL_GR)
            projection(G_A2 + 8, 3, COL_SQ)
            modulation(G_M3, 4, 4 * D)
            with sync.Fori(0, 4) as n:
                for half, (col, w) in enumerate(((COL_GATE_A, w_a), (COL_GATE_B, w_b))):
                    for j in range(4):
                        load((G_GATE + 6 * half + j, n * 12), w_in[:, 4 * j:4 * j + 4, ds(n * BANK + col, BANK)], k4)
                    for j in range(2):
                        load((G_GATE + 6 * half + 4 + j, n * 12), w[:, 4 * j:4 * j + 4, ds(n * BANK, BANK)], k4)
            with sync.Fori(0, 4) as n:
                for j in range(4):
                    load((G_OUT + j, n * 4), w_out[:, 4 * j:4 * j + 4, ds(n * BANK, BANK)], k4)
            modulation(G_M4, 4, 5 * D)
            sync.wait_ge(n2_h, NT)
            with sync.Fori(0, NE) as e:
                def expert(j, src, dst=None):
                    sync.wait_ge(piece_ready, e * EXP_G + (P_EXP + j + 1 - ESLOTS))
                    if j == 5:
                        sync.wait_ge(tk_cp, 3)
                    if j == 6:
                        sync.wait_ge(slot_used, SLOTS + G_M4 + 16)
                    sync.sem_inc(loads_issued, 1)
                    out = exp_slot[j % ESLOTS]
                    sync.dma_start(out if dst is None else dst(out), src).then_inc(exp_ready[j % ESLOTS], 16)

                for j in range(8):
                    expert(2 * j, w_eg[ds(e, 1), :, 2 * j:2 * j + 2, :].squeeze(0), k2)
                    expert(2 * j + 1, w_eu[ds(e, 1), :, 2 * j:2 * j + 2, :].squeeze(0), k2)
                for j in range(8):
                    expert(16 + j, w_ed[ds(e, 1), :, j, :].squeeze(0))

        @block.gpsimd
        def _(pool):
            pool.dma_start(cst[:, 0:P], T["consts"][:, 0:P]).then_inc(rows_ld, 16)
            for at, src in ((0, T["c"][0]), (KT, T["c_ctx"]), (2 * KT, T["b_mod"][0, 0:2 * D]), (4 * KT, T["g_norm1"][0])):
                rows = src.rearrange("(k p) -> k p", p=P)
                pool.dma_start(cond[at:at + rows.shape[0], :], rows).then_inc(rows_ld, 16)
            for t in range(NT):
                pool.dma_start(xrow[:, t, :], x_of[t]).then_inc(x_ld[t], 16)
            pool.dma_start(cst[:, P:], T["consts"][:, P:]).then_inc(s_cst, 16)
            pool.dma_start(sink[:, :], row_bcast(T["attn_sink"][0])).then_inc(s_cst, 16)
            for who in range(2):
                pool.dma_start(mod_dram[who:who + 1, 2 * D:6 * D], T["b_mod"][0:1, 2 * D:6 * D]).then_inc(mb_ld, 16)
            def mod_load(dst, who, part, s, n=P):
                pool.dma_start(dst, row_bcast(mod_dram[who, part * D:(part + 1) * D], n)).then_inc(s, 16)

            def mod_columns(first, count):
                for i in range(first, first + count):
                    pool.wait_ge(mc_ev, i + 1)
                    pool.dma_start(mod_dram[:, 2 * D + i * BANK:2 * D + (i + 1) * BANK], modc[0:2, i % 2, :],
                                   accum_op=ALU.add).then_inc(mc_st[i % 2], 16)

            pool.wait_ge(mb_ld, 32)
            pool.wait_ge(h_m, KT)
            pool.wait_ge(wdec0, 1)
            for dr, (w, b) in enumerate((("w_dec_f", "b_dec_f"), ("w_dec_b", "b_dec_b"))):
                pool.dma_start(wdec[RANK * dr:RANK * dr + RANK, dr, :], T[w][0]).then_inc(s_wdec, 16)
                pool.dma_start(wdec[2 * RANK:2 * RANK + 1, dr, :], T[b]).then_inc(s_wdec, 16)
            pool.dma_start(glag, row_bcast(T["g_gla"][0])).then_inc(s_wdec, 16)
            pool.wait_ge(piece_used, SP + 4 * KT)
            for s in range(2 * GH):
                h, dr = s // 2, s % 2
                src = T["state_gla_bwd" if dr else "state_gla_fwd"][0, 0, h]
                if s >= 2:
                    pool.wait_ge(o_pe, 3 * (s - 1))
                    pool.wait_ge(s_up, 9 * (s - 1))
                    final = T["ns_bwd" if (s - 2) % 2 else "ns_fwd"][0, 0, (s - 2) // 2]
                    pool.dma_start(final, st[:, s % 2, 9, :]).then_inc(st_out, 16)
                pool.dma_start(st[:, s % 2, 0, :], src).then_inc(st_ld[s % 2], 16)
                if s >= 2:
                    mod_columns(s - 2, 1)
            for s in range(2 * GH, 2 * GH + 2):
                pool.wait_ge(s_up, 9 * (s - 1))
                final = T["ns_bwd" if (s - 2) % 2 else "ns_fwd"][0, 0, (s - 2) // 2]
                pool.dma_start(final, st[:, s % 2, 9, :]).then_inc(st_out, 16)
            mod_columns(2 * GH - 2, 2)
            pool.wait_ge(st_out, 16 * 2 * GH)
            pool.wait_ge(gr_tr, 10)
            kc = T["cache_k"][0, 0].rearrange("s h d -> s h d")
            skr_c = skr[:, NT, :].rearrange("p (h e d) -> p h e d", h=SKV, e=2)
            for e in range(2):
                pool.dma_start(skr_c[:, :, e, :], kc).then_inc(kv_ld, 16)
            pool.dma_start(svr[:, NT, :], T["cache_v"][0, 0].rearrange("s h d -> s (h d)")).then_inc(kv_ld, 16)
            pool.wait_ge(k_dup, 3 * NT + 1)
            pool.dma_start(T["nk"][0, 0].rearrange("s h d -> s (h d)"), krow_out).then_inc(kv_st, 16)
            pool.dma_start(T["nv"][0, 0].rearrange("s h d -> s (h d)"), svr[:, NT - 1, :]).then_inc(kv_st, 16)
            mod_columns(8, 4)
            pool.wait_ge(mc_st[0], 16 * 6)
            pool.wait_ge(mc_st[1], 16 * 6)
            pool.wait_ge(pv_pe, len(units))
            pool.dma_start(arows[0:2, :], mod_dram[:, 4 * D:5 * D]).then_inc(ar_ld, 16)
            for half in range(2):
                cols = slice(half * 2 * BANK, (half + 1) * 2 * BANK)
                g = modc[0:2, :, :].rearrange("p a n -> p (a n)")
                pool.dma_start(g, row_bcast(T["g_norm2"][0, cols], 2)).then_inc(ar_ld, 16)
                pool.wait_ge(ar_ld, 16 * (half + 2))
                pool.tensor_scalar(arows[0:2, cols], arows[0:2, cols], 1.0, None, ALU.add).then_inc(ar_f, 1)
                pool.wait_ge(ar_f, 2 * half + 1)
                pool.tensor_tensor(arows[0:2, cols], arows[0:2, cols], g, ALU.mult).then_inc(ar_f, 1)
                pool.wait_ge(ar_f, 2 * half + 2)
            pool.dma_start(mod_dram[:, 4 * D:5 * D], arows[0:2, :]).then_inc(ar_st, 16)
            pool.wait_ge(ar_st, 16)
            pool.dma_start(wrt, T["w_router"][0].rearrange("(k p) e -> p k e", p=P)).then_inc(wr_ld, 16)
            for n in range(3):
                pool.wait_ge(mt_cp, NT * (n + 1) + 1)
                pool.dma_start(mT_dram[:, 4 * n:4 * n + 4, :], mTc).then_inc(mT_st, 16)
                pool.wait_ge(mT_st, 16 * (n + 1))
                pool.sem_inc(mT_free, 1)
            pool.wait_ge(piece_ready, P_GATE + 3 * 48 + GATE_PIECES[3][0])
            for n in range(3):
                pool.dma_start(hT[:, 4 * n:4 * n + 4, :], mT_dram[:, 4 * n:4 * n + 4, :]).then_inc(mT_ld, 16)
            pool.wait_ge(piece_used, SP + P_OUT)
            for t in range(NT):
                pool.dma_start(x1[:, t, :], x_of[t]).then_inc(xr_ld, 16)
            pool.wait_ge(gt_dve, 9 * NT)
            for who in range(2):
                mod_load(gt1[:, who, :], who, 2, wo_ld)
            pool.wait_ge(piece_ready, P_EXP)
            for who in range(2):
                mod_load(A2[:, who, :], who, 4, ab_ld)
                mod_load(B2[:, who, :], who, 3, ab_ld)
            for t in range(NT):
                pool.wait_ge(n2_sq, t + 1)
                pool.dma_start(y_dram[t * P:(t + 1) * P, :], x1[:, t, :]).then_inc(x1_st, 16)
                pool.wait_ge(n2_h, t + 1)
                pool.dma_start(h2_dram[t * P:(t + 1) * P, :], h2row[:, t % 3]).then_inc(n2_st[t % 3], 16)
            pool.wait_ge(tk_cp, 3)
            for i, n in enumerate((2, 2, 1)):
                pool.wait_ge(n2_st[i], 16 * n)
            pool.wait_ge(x1_st, 16 * NT)

            def gather(col):
                pool.tensor_copy(gidx[:, :], col).then_inc(gi_cp, 1)

            def gather_rows():
                pool.indirect_dma_start(xs[0:CAP, :], None, h2_dram, bass.IndirectOffsetOnAxis(ap=gidx[:, :], axis=0))\
                    .then_inc(xs_ld, 16)

            gather(idxT[0:CAP, 0:1])
            pool.wait_ge(gi_cp, 1)
            gather_rows()
            mod_columns(12, 3)
            pool.wait_ge(xs_tr, 1)
            gather(idxT[0:CAP, 1:2])
            pool.wait_ge(gi_cp, 2)
            gather_rows()
            mod_columns(15, 1)
            for i in range(2):
                pool.wait_ge(mc_st[i], 16 * 8)
            mod_load(gt2[0:CAP_L, :], 0, 5, g2_ld, CAP_L)
            mod_load(gt2[CAP_L:CAP, :], 1, 5, g2_ld, CAP_C)
            pool.wait_ge(slot_used, SLOTS + G_M4 + 16)
            pool.dma_start(gfin, row_bcast(T["g_final"])).then_inc(gf_ld, 16)
            with pool.Fori(0, NE) as e:
                pool.wait_ge(xs_tr, e + 2)
                pool.wait_ge(xs_ld, e * 16 + 32)
                gather(idxT[0:CAP, ds(e + 2, 1)])
                pool.wait_ge(gi_cp, e + 3)
                pool.sem_inc(rows_issued, 1)
                gather_rows()
                pool.tensor_copy(sidx[:, :], idxT[0:CAP, ds(e, 1)]).then_inc(pool_step, 1)
                pool.wait_ge(pool_step, e + 1)
                pool.wait_ge(ye_r, e + 2)
                pool.sem_inc(rows_issued, 1)
                pool.indirect_dma_start(y_dram, bass.IndirectOffsetOnAxis(ap=sidx[:, :], axis=0), ye[0:CAP, :], None,
                                        compute_op=ALU.add).then_inc(ye_st, 16)
                pool.wait_ge(ye_st, e * 16 + 16)
                pool.sem_inc(ye_free, 1)
            pool.wait_ge(xs_ld, 16 * (NE + 2))
            for t in range(NT):
                pool.dma_start(yrow[:, t, :], y_dram[t * P:(t + 1) * P, :]).then_inc(y_ld[t], 16)
            for t in range(NT):
                pool.wait_ge(y_r, t + 1)
                pool.dma_start(y_of[t], yrow[:, t, :]).then_inc(y_sto, 16)
            pool.wait_ge(y_sto, 16 * NT)
            pool.wait_ge(kv_st, 32)
            pool.wait_ge(st_out, 16 * 2 * GH)

        @block.tensor
        def _(pe):
            def slot(first, turn):
                s = first % SLOTS
                pe.wait_ge(slot_ready[s], turn * 16 + 16 * (first // SLOTS + 1))
                return ring[:, s, :]

            pe.sem_inc(slot_used, SLOTS)
            pe.sem_inc(piece_used, SP)
            pe.wait_ge(rows_ld, 80)
            n = 5 * KT
            pe.transpose(ps[:, 4, 0:n], cond[0:n, :], ident[0:n, 0:n]).then_inc(s_condT, 1)

            def h_transposes(t):
                pe.wait_ge(h_row, t + 1)
                for q in range(4):
                    if t:
                        pe.wait_ge(h_cp, 4 * (t - 1) + q + 1)
                    for k in range(4 * q, 4 * q + 4):
                        mm = pe.transpose(ps[:, 4 + q, (k % 4) * P:(k % 4 + 1) * P],
                                          xrow[:, t, k * P:(k + 1) * P], ident)
                    mm.then_inc(h_tr, 1)

            pe.wait_ge(s_condS, 2)
            for i in range(2 * KT):
                k, s = i % KT, i % MSLOTS
                if i == KT:
                    pe.wait_ge(mr_a, 1)
                    pe.wait_ge(mr_d, 1)
                if i in X_TRANSPOSE:
                    h_transposes(X_TRANSPOSE.index(i))
                pe.wait_ge(slot_used, SLOTS + i + 1)
                for n in range(4):
                    pe.matmul(ps[0:4, n, :], condR[:, k, 0:4], modS[:, s, 0, n * BANK:(n + 1) * BANK],
                              start=(k == 0), stop=False, skip_group_check=True)
                for n in range(4):
                    mm = pe.matmul(ps[0:2, n, :], condR[:, k, 0:2], modS[:, s, 1, n * BANK:(n + 1) * BANK],
                                   start=False, stop=(k == KT - 1), skip_group_check=True)
                mm.then_inc(md_used, 1)
            pe.wait_ge(mr_a, 2)
            pe.wait_ge(mr_d, 2)
            pe.wait_ge(h_cp, 4 * NT)
            for i in range(2 * KT):
                mm = pe.transpose(ps[:, 4, 4 * i:4 * i + 4], modrow[0:4, i * P:(i + 1) * P], ident[0:4, 0:4])
            mm.then_inc(s_mT, 1)
            n_mod = 0

            def mod_granules(count):
                nonlocal n_mod
                for _ in range(count):
                    c, j = n_mod // 4, n_mod % 4
                    w = slot(G_M_COL[c] + j, 0).rearrange("p (k n) -> p k n", k=4)
                    if j == 0 and c:
                        pe.wait_ge(mc_ev, c)
                    for kk in range(4):
                        mm = pe.matmul(ps[0:2, 7 if c < 12 else 6, :], condT[:, 4 * j + kk, :], w[:, kk, :],
                                       start=(j == 0 and kk == 0), stop=(j == 3 and kk == 3))
                    mm.then_inc(slot_used, 1)
                    n_mod += 1

            def product(first, turn, n_k, bank_free, done):
                for k in range(n_k):
                    s = (first + k) % SP
                    pe.wait_ge(piece_ready, turn + (first + k + 1))
                    for b in range(NT):
                        if k == 0:
                            bank_free(b)
                        for x, w in ((0, 0), (0, 1), (1, 0)):
                            mm = pe.matmul(ps[:, b, :], spX[:, s, x, b * P:(b + 1) * P], spW[:, s, w, :],
                                           start=(k == 0 and x == w), stop=(k == n_k - 1 and x == 1))
                        if k == n_k - 1 and b < 4:
                            mm.then_inc(done, 1)
                    mm.then_inc(piece_used, 1)

            def product_T(first, turn, bank_free, done):
                for k in range(KT):
                    s = (first + k) % SP
                    pe.wait_ge(piece_ready, turn + (first + k + 1))
                    for c in range(4):
                        if k == 0:
                            bank_free(c)
                        for x, w in ((0, 0), (1, 0), (0, 1)):
                            mm = pe.matmul(ps[:, c, 0:TA], spW[:, s, w, c * P:(c + 1) * P], spX[:, s, x, 0:TA],
                                           start=(k == 0 and x == w), stop=(k == KT - 1 and w == 1))
                        if k == KT - 1:
                            mm.then_inc(done, 1)
                        if k == 0 and c == 0:
                            bank_free(4)
                        for x, w in ((0, 0), (1, 0), (0, 1)):
                            mm = pe.matmul(ps[:, 4 + c // 2, (c % 2) * TB:(c % 2 + 1) * TB],
                                           spW[:, s, w, c * P:(c + 1) * P],
                                           spX[:, s, x, TA:TOK], start=(k == 0 and c % 2 == 0 and x == w),
                                           stop=(k == KT - 1 and w == 1), skip_group_check=True)
                    mm.then_inc(piece_used, 1)

            def chunks(first, count, rows):
                with pe.Fori(0, count) as c:
                    def bank_free(b):
                        pe.wait_ge(pj_ev, c * NT + (NT * first + b + 1))
                    if rows:
                        product(P_A + KT * first, c * KT, KT, bank_free, pj_pe)
                    else:
                        product_T(P_A + KT * first, c * KT, bank_free, pj_pe)

            pe.wait_ge(s_cst, 32)
            chunks(0, 2, False)
            chunks(2, 2, True)
            pe.wait_ge(ga_w, 16)
            gaw = ar[:, 27264:27264 + KT * 2 * RANK].rearrange("p (k n) -> p k n", k=KT)
            for k in range(KT):
                pe.matmul(ps[0:2 * RANK, 5, :], gaw[:, k, :], hT[:, k, 0:LAT], start=(k == 0), stop=(k == KT - 1))
                mm = pe.matmul(ps[0:2 * RANK, 6, 0:CTX], gaw[:, k, :], hT[:, k, LAT:TOK],
                               start=(k == 0), stop=(k == KT - 1))
            mm.then_inc(ga_pe, 1)
            pe.wait_ge(ga_ev, 2)
            pe.wait_ge(s_wdec, 80)
            pe.wait_ge(pj_ev, NT * 5)

            def z_product(s, part):
                w = wdec[0:2 * RANK + 1, s % 2, s // 2 * GK:(s // 2 + 1) * GK]
                lo, n = ((0, LAT), (LAT, CTX))[part]
                if s or part:
                    pe.wait_ge(z_mn, 2 * s + part)
                pe.matmul(ps[:, 4, 0:n], w, gaT[0:2 * RANK + 1, lo:lo + n], start=True, stop=True).then_inc(z_pe, 1)

            z_product(0, 0)
            mod_granules(1)
            z_product(0, 1)
            for s in range(2 * GH):
                h, dr = s // 2, s % 2
                xq = xq2[dr]
                pe.wait_ge(g_m, s + 1)
                if s:
                    pe.wait_ge(s_up, 9 * s)
                for t in range(NT):
                    mm = pe.transpose(ps[:, 5 + t // 4, (t % 4) * P:(t % 4 + 1) * P], tD[:, t * P:(t + 1) * P], ident)
                mm.then_inc(kt_pe, 1)
                if s:
                    pe.wait_ge(o_ev, 3 * s)
                for t in range(NT):
                    o = ps[:, 3, t * P:(t + 1) * P] if t < 4 else ps[:, 2, 2 * GV - P:2 * GV]
                    mm = pe.matmul(o, xk[:, t * P:(t + 1) * P], xq[:, t * P:(t + 1) * P], start=True, stop=True,
                                   skip_group_check=True)
                mm.then_inc(at_pe, 1)
                if s + 1 < 2 * GH:
                    z_product(s + 1, 0)
                mod_granules(1)
                order = ([9, 8] if dr else [8, 9]) + (list(range(7, 0, -1)) if dr else list(range(7)))
                pe.wait_ge(kt_cp, s + 1)
                for u, c in enumerate(order):
                    lo, t = (c % 2) * CH, c // 2
                    bank, half, _, freed = U_PLACE[u]
                    if freed:
                        pe.wait_ge(s_up, 9 * s + freed)
                    pe.matmul(ps[:, bank, half * GV:(half + 1) * GV],
                              ks[lo:lo + CH, t * P:(t + 1) * P], gv[lo:lo + CH, t, h * GV:(h + 1) * GV],
                              start=True, stop=True, skip_group_check=True).then_inc(u_pe, 1)
                if s + 1 < 2 * GH:
                    z_product(s + 1, 1)
                    mod_granules(3)
                else:
                    mod_granules(2)
                pe.wait_ge(at_cp, s + 1)
                for i, t in enumerate([4, 3, 2, 1, 0] if dr else [4, 0, 1, 2, 3]):
                    o = ps[:, t // 2, (t % 2) * GV:(t % 2 + 1) * GV]
                    mm = pe.matmul(o, aTm[:, dr, t * P:(t + 1) * P], gv[:, t, h * GV:(h + 1) * GV],
                                   start=True, stop=False, skip_group_check=True)
                    for c in ([2 * t + 1, 2 * t] if dr else [2 * t, 2 * t + 1]):
                        lo = (c % 2) * CH
                        if c >= LCH:
                            if c == order[0]:
                                continue
                            state = st[:, dr, 8, :]
                            pe.wait_ge(s_up, 9 * s + 1)
                        else:
                            n = 7 - c if dr else c
                            state = st[:, dr, n, :]
                            if n:
                                pe.wait_ge(s_up, 9 * s + 2 + n)
                            else:
                                pe.wait_ge(st_ld[dr], 16 * (h + 1))
                        mm = pe.matmul(o[lo:lo + CH, :], xq[:, c * CH:(c + 1) * CH], state,
                                       start=False, stop=True, skip_group_check=True)
                    if i % 2 == 0:
                        mm.then_inc(o_pe, 1)
            pe.wait_ge(o_ev, 2 * GH * 3)
            with pe.Fori(0, 2) as c:
                def bank_free(b):
                    pe.wait_ge(pj_ev, c * NT + (NT * 4 + b + 1))
                product(P_A + KT * 4, c * KT, KT, bank_free, pj_pe)
                for b in range(NT):
                    pe.wait_ge(gr_o, c * NT + (b + 1))
                    pe.wait_ge(gr_cp, c * NT + (b + 1 + (b == 0)))
                    for q in range(4):
                        mm = pe.transpose(ps[:, 5 + b % 2, q * P:(q + 1) * P], onr[:, b % 2, q * P:(q + 1) * P], ident)
                    mm.then_inc(gr_tr, 1)
            pe.wait_ge(gr_cp, 2 + 2 * NT)
            chunks(6, 2, False)
            chunks(8, 1, True)
            for i in range(8):
                pe.wait_ge(pj_ev, NT * (8 + i // 4))
                if i >= 2:
                    pe.wait_ge(sq_rp, i - 1)
                pe.matmul(ps[:, 5 + i % 2, :], cst[:, C_PERM:C_PERM + P], swT[:, i, 0:LAT],
                          start=True, stop=True).then_inc(sq_pm, 1)
            pe.wait_ge(k_dup, 3 * NT + 1)
            pe.wait_ge(kv_ld, 48)
            pe.wait_ge(sq_rp, 8)
            for g in range(SKV):
                if g:
                    pe.wait_ge(k_cp, 2 * g)
                for t in range(NT + 1):
                    mm = pe.transpose(ps[:, t // 4, (t % 4) * P:(t % 4 + 1) * P],
                                      skr[:, t, g * 2 * HD:(g + 1) * 2 * HD], ident)
                mm.then_inc(k_tr, 1)
                pe.wait_ge(k_cp, 2 * g + 2)
                if g >= 2:
                    pe.wait_ge(k_rp, g - 1)
                pe.matmul(ps[:, 2 + g % 2, :], cst[:, C_PERM:C_PERM + P], skT[:, g, 0:LAT],
                          start=True, stop=True).then_inc(k_pm, 1)
            pe.wait_ge(k_rp, SKV)

            def scores(u):
                t, g = units[u]
                keys, _ = unit_keys(t)
                if u:
                    pe.wait_ge(sc_m, u)
                for j in range(GRP):
                    lo, ch = (j % 2) * HD, 2 * g + j // 2
                    at = 0
                    for a, n in keys:
                        mm = pe.matmul(ps[:, j, at:at + n], swT[lo:lo + HD, ch, t * P:(t + 1) * P],
                                       skT[lo:lo + HD, g, a:a + n], start=True, stop=True, skip_group_check=True)
                        at += n
                mm.then_inc(sc_pe, 1)

            n_pt = 0
            scores(0)
            for u, (t, g) in enumerate(units):
                if u + 1 < len(units):
                    scores(u + 1)
                _, blocks = unit_keys(t)
                if u % 5 < 4:
                    mod_granules(1)
                pe.wait_ge(sc_n, u + 1)
                for i, _ in enumerate(blocks):
                    if n_pt >= 2:
                        pe.wait_ge(pt_cp, n_pt - 1)
                    for j in range(GRP):
                        mm = pe.transpose(ps[:, 4 + n_pt % 2, j * P:(j + 1) * P],
                                          Sbuf[:, u % 2, j * BANK + i * P:j * BANK + (i + 1) * P], ident)
                    mm.then_inc(pt_pe, 1)
                    n_pt += 1
                if u:
                    pe.wait_ge(pv_cp, u)
                for half in range(2):
                    lo = half * HD
                    for i, vt in enumerate(blocks):
                        pe.wait_ge(pt_cp, n_pt - len(blocks) + i + 1)
                        mm = pe.matmul(ps[lo:lo + HD, 6, 0:2 * P], svr[:, vt, g * HD:(g + 1) * HD],
                                       pT[:, u % 2, i * BANK:(i + 1) * BANK].rearrange(
                                           "p (c e q) -> p c e q", c=2, e=2)[:, :, half, :],
                                       start=(i == 0), stop=(i == len(blocks) - 1), skip_group_check=True)
                mm.then_inc(pv_pe, 1)
            pe.wait_ge(pv_cp, len(units))

            def merged_transposes(n):
                for b in range(NT):
                    pe.wait_ge(gt_dve, n * 10 + (2 * NT + b + 1))
                    pe.wait_ge(mt_cp, n * NT + (1 if b < 3 else b - 1))
                    for q in range(4):
                        mm = pe.transpose(ps[:, 5 + b % 3, q * P:(q + 1) * P], mrow[:, b, q * P:(q + 1) * P], ident)
                    mm.then_inc(mt_pe, 1)

            def gate_products(n, before):
                for q, (first, n_k) in enumerate(GATE_PIECES):
                    def bank_free(b):
                        if q == 0:
                            pe.wait_ge(gt_dve, n * 10 + (b + 1))
                        elif q == 2:
                            pe.wait_ge(gt_dve, n * 10 + (NT + b + 1))
                        else:
                            pe.wait_ge(gt_act, n * 10 + (5 * (q // 2) + b + 1))
                    product(P_GATE + first, n * 48, n_k, bank_free, gt_pe)
                    if q == 0 and before is not None:
                        merged_transposes(before)

            gate_products(0, None)
            with pe.Fori(1, 4) as n:
                gate_products(n, n - 1)
            merged_transposes(3)
            pe.wait_ge(mt_cp, 4 * NT + 1)
            pe.wait_ge(gt_dve, 9 * NT)
            with pe.Fori(0, 4) as n:
                def bank_free(b):
                    pe.wait_ge(wo_rd, n * NT + (b + 1))
                product(P_OUT, n * KT, KT, bank_free, wo_pe)
            pe.wait_ge(sq_part, NT)
            mod_granules(3)
            pe.wait_ge(wo_rd, 5 * NT)

            def h2_bank(j):
                return (0, 2)[j % 2]

            def logits(j):
                t, half = j // 2, j % 2
                if j == 0:
                    pe.wait_ge(wr_ld, 16)
                pe.wait_ge(n2_cp, j + 1)
                for k in range(8 * half, 8 * half + 8):
                    o = ps[0:NE, 4, t * P:(t + 1) * P] if t < 4 else ps[0:NE, 7, 0:CTX]
                    mm = pe.matmul(o, wrt[:, k, :], h2T[:, t % 2, k, :],
                                   start=(k == 0), stop=(k == KT - 1), skip_group_check=True)
                if half:
                    mm.then_inc(lg_pe, 1)

            for j in range(2 * NT):
                t, half = j // 2, j % 2
                pe.wait_ge(n2_h, t + 1)
                if j >= 2:
                    pe.wait_ge(n2_cp, j - 1)
                for k in range(8):
                    col = (8 * half + k) * P
                    mm = pe.transpose(ps[:, h2_bank(j) + k // 4, (k % 4) * P:(k % 4 + 1) * P],
                                      h2row[:, t % 3, col:col + P], ident)
                mm.then_inc(n2_tr, 1)
                if j:
                    logits(j - 1)
            logits(2 * NT - 1)
            pe.wait_ge(lg_cp, 2)
            for t in range(NT):
                mm = pe.transpose(ps[:, 0, t * NE:(t + 1) * NE], lgT[0:NE, t * P:(t + 1) * P], ident[0:NE, 0:NE])
            mm.then_inc(lr_pe, 1)
            pe.wait_ge(af_r, 1)
            for t in range(NT):
                mm = pe.transpose(ps[0:NE, 5 + 2 * (t // 4), (t % 4) * P:(t % 4 + 1) * P], aff[:, 0, t, :], ident)
            mm.then_inc(af_tr, 1)
            mod_granules(7)
            pe.wait_ge(tk_d, 1)
            pe.transpose(ps[0:CAP, 7, 0:NE], idxf[0:NE, :], ident[0:NE, 0:NE])
            pe.transpose(ps[0:CAP, 7, NE:2 * NE], vals[0:NE, :], ident[0:NE, 0:NE]).then_inc(tk_tr, 1)

            def xs_transposes(bank1_free=None):
                v = xs[0:CAP, :].rearrange("r (p k) -> r k p", k=KT)
                for k in range(KT):
                    o = xs_bank(k)
                    if k == 12 and bank1_free is not None:
                        pe.wait_ge(hd_cp, bank1_free)
                    mm = pe.transpose(o, v[:, k, :], ident[0:CAP, 0:CAP])
                mm.then_inc(xs_tr, 1)

            def xs_bank(k):
                b, i = ((2, k) if k < 6 else (3, k - 6)) if k < 12 else (1, k - 12 + 2)
                return ps[:, b, i * CAP:(i + 1) * CAP]

            mod_granules(3)
            pe.wait_ge(xs_ld, 16)
            pe.wait_ge(af_cp, 1)
            xs_transposes()
            mod_granules(3)
            pe.wait_ge(mc_ev, 16)
            with pe.Fori(0, NE) as e:
                pe.wait_ge(xs_l, e + 1)
                for j in range(16):
                    g, up = j // 2, j % 2
                    s = j % SP
                    pe.wait_ge(piece_ready, e * EXP_G + (P_EXP + j + 1))
                    for kk in range(2):
                        k = 2 * g + kk
                        for x, w in ((0, 0), (0, 1), (1, 0)):
                            for n in range(2):
                                col = kk * FF + n * BANK
                                mm = pe.matmul(ps[0:CAP, 2 * up + n, :], xsT[:, x, k, :], spE[:, s, w, col:col + BANK],
                                               start=(k == 0 and x == w), stop=(k == KT - 1 and x == 1))
                    mm.then_inc(piece_used, 1)
                pe.wait_ge(hd_r, e + 1)
                v = hid[0:CAP, :].rearrange("r (p k) -> r k p", k=FT)
                for k in range(FT):
                    mm = pe.transpose(ps[:, k // 6, (k % 6) * CAP:(k % 6 + 1) * CAP], v[:, k, :], ident[0:CAP, 0:CAP])
                mm.then_inc(hd_tr, 1)
                pe.wait_ge(xs_ld, e * 16 + 32)
                xs_transposes(e + 1)
                pe.wait_ge(hd_cp, e + 1)
                pe.wait_ge(ye_r, e + 1)
                for k in range(FT):
                    s = (16 + k) % SP
                    pe.wait_ge(piece_ready, e * EXP_G + (P_EXP + 16 + k + 1))
                    for x, w in ((0, 0), (0, 1), (1, 0)):
                        for n in range(4):
                            mm = pe.matmul(ps[0:CAP, 4 + n, :], hidT[:, x, k, :], spE[:, s, w, n * BANK:(n + 1) * BANK],
                                           start=(k == 0 and x == w), stop=(k == FT - 1 and x == 1))
                    mm.then_inc(piece_used, 1)

        @block.scalar
        def _(act):
            ch = Chain(act, act_step)
            act.wait_ge(s_condT, 1)
            ch.step(act.activation(condT[:, :, :].rearrange("p k w -> p w k"),
                                   ps[:, 4, 0:2 * KT].rearrange("p (w k) -> p w k", w=2), ACT.Silu))
            act.activation(condR[:, :, 0:2], condT[:, :, :], ACT.Copy).then_inc(s_condS, 1)
            act.wait_ge(s_eps, 1)

            def mod_evacuated(m):
                act.wait_ge(md_used, KT * (m + 1))
                act.activation(modrow[0:4, m * D + 2 * BANK:(m + 1) * D].rearrange("p (b n) -> p b n", b=2),
                               ps[0:4, 2:4, :], ACT.Copy).then_inc(mr_a, 1)

            for i in range(2 * KT):
                act.wait_ge(slot_ready[i % SLOTS], 16 * (i // SLOTS + 1))
                if i >= MSLOTS:
                    act.wait_ge(md_used, i - MSLOTS + 1)
                act.activation(modS[:, i % MSLOTS, 0, :], ring[:, i % SLOTS, :], ACT.Copy).then_inc(md_high, 1)
                if i in X_SQUARE:
                    t = X_SQUARE.index(i)
                    act.wait_ge(x_ld[t], 16)
                    ch.step(act.activation(junk, xrow[:, t, :], ACT.Square, accum_out=stat[:, t:t + 1]))
                    act.activation(stat[:, NT + t:NT + t + 1], stat[:, t:t + 1], ACT.Sqrt, scale=1.0 / D,
                                   bias=epsb[:, :]).then_inc(h_sq, 1)
                if i in X_COPY:
                    t = X_COPY.index(i)
                    for q in range(4):
                        act.wait_ge(h_tr, 4 * t + q + 1)
                        act.activation(hT[:, 4 * q:4 * q + 4, t * P:(t + 1) * P],
                                       ps[:, 4 + q, :].rearrange("p (k t) -> p k t", k=4), ACT.Copy).then_inc(h_cp, 1)
                if i == KT + 1:
                    mod_evacuated(0)
            mod_evacuated(1)
            gaw = ar[:, 27264:27264 + KT * 2 * RANK].rearrange("p (k n) -> p k n", k=KT)
            act.dma_start(gaw, w_in[:, :, COL_GA:COL_SQ]).then_inc(ga_w, 16)

            n_col = 0

            def mod_column():
                nonlocal n_col
                act.wait_ge(slot_used, SLOTS + G_M_COL[n_col] + 4)
                if n_col >= 2:
                    act.wait_ge(mc_st[n_col % 2], 16 * (n_col // 2))
                act.activation(modc[0:2, n_col % 2, :], ps[0:2, 7 if n_col < 12 else 6, :], ACT.Copy).then_inc(mc_ev, 1)
                n_col += 1

            sp = Split(act, True)
            for k in range(KT):
                act.wait_ge(h_m, k + 1)
                sp.chunk(0, k, k + 1)
            for i, dst in enumerate((gqT, gkT)):
                if i:
                    sp.chunk(i, AHEAD)
                sp.chunk(i + 1, 0, AHEAD)
                for b in range(4):
                    bank_done(act, pj_pe, i, b, P_A + KT * i + KT - 1)
                    act.activation(dst[:, b, 0:TA], ps[:, b, 0:TA], ACT.Copy).then_inc(pj_ev, 1)
                bank_done(act, pj_pe, i, 4, P_A + KT * i + KT - 1)
                act.activation(dst[:, :, TA:TOK], ps[:, 4:6, :].rearrange("p b (c t) -> p (b c) t", c=2), ACT.Copy)\
                    .then_inc(pj_ev, 1)
            for i in range(2):
                sp.chunk(2 + i, AHEAD)
                if i == 0:
                    sp.chunk(3, 0, AHEAD)
                for b in range(NT):
                    bank_done(act, pj_pe, 2 + i, b, P_A + KT * (2 + i) + KT - 1)
                    act.activation(gv[:, b, i * BANK:(i + 1) * BANK], ps[:, b, :], ACT.Copy).then_inc(pj_ev, 1)
            act.wait_ge(ga_pe, 1)
            act.wait_ge(wdec0, 1)
            act.activation(gaT[0:2 * RANK, 0:LAT], ps[0:2 * RANK, 5, :], ACT.Copy).then_inc(ga_ev, 1)
            act.activation(gaT[0:2 * RANK, LAT:TOK], ps[0:2 * RANK, 6, 0:CTX], ACT.Copy).then_inc(ga_ev, 1)

            def gla_logs(s):
                if s:
                    act.wait_ge(g_b, s)
                act.wait_ge(z_pe, 2 * s + 1)
                act.activation(tz[:, 0:LAT], ps[:, 4, :], ACT.Abs).then_inc(z_ab, 1)
                act.wait_ge(z_pe, 2 * s + 2)
                act.activation(tz[:, LAT:TOK], ps[:, 4, 0:CTX], ACT.Abs).then_inc(z_ab, 1)
                act.wait_ge(z_ab, 2 * s + 2)
                ch.step(act.activation(tz, tz, ACT.Exp, scale=-1.0))
                act.activation(tz, tz, ACT.Ln, bias=1.0).then_inc(z_ln, 1)

            def gla_exps(s):
                act.wait_ge(g_b, s + 1)
                if s >= 2:
                    act.wait_ge(o_pe, 3 * (s - 1))
                    act.wait_ge(s_up, 9 * (s - 1))
                act.activation(xq2[s % 2], tB, ACT.Exp, scale=1.0 / TAU)
                if s:
                    act.wait_ge(at_pe, s)
                act.activation(xk, tB, ACT.Exp, scale=-1.0 / TAU)
                act.activation(tD, tD, ACT.Exp, scale=1.0 / TAU)
                act.activation(decay[:, s % 2, :], tc.rearrange("p (c t) -> p c t", t=CH)[:, :, CH - 1], ACT.Exp,
                               scale=1.0 / TAU).then_inc(g_e, 1)

            gla_logs(0)
            gla_exps(0)
            for s in range(2 * GH):
                act.wait_ge(kt_pe, s + 1)
                if s:
                    act.wait_ge(u_pe, 9 * s)
                act.activation(ks[:, 0:LAT], ps[:, 5, :], ACT.Copy)
                act.activation(ks[:, LAT:TOK], ps[:, 6, 0:P], ACT.Copy).then_inc(kt_cp, 1)
                if s + 1 < 2 * GH:
                    gla_logs(s + 1)
                    gla_exps(s + 1)
                mod_column()
                if s % 2:
                    h = s // 2
                    act.wait_ge(o_ev, 3 * (s + 1))
                    for t in range(NT):
                        ch.step(act.activation(tz[:, 0:GV], og[:, t, h * GV:(h + 1) * GV], ACT.Square,
                                               accum_out=rs_gla[:, t * GH + h:t * GH + h + 1]))
            act.activation(rs_gla[:, :], rs_gla[:, :], ACT.Sqrt, scale=1.0 / GV, bias=epsb[:, :]).then_inc(o_sq, 1)
            act.wait_ge(st_out, 16 * 2 * GH)
            sp.chunk(4, 0, AHEAD)
            for c in range(2):
                sp.chunk(4 + c, AHEAD)
                sp.chunk(5 + c, 0, AHEAD)
                for b in range(NT):
                    n = c * NT + b
                    bank_done(act, pj_pe, 4 + c, b, P_A + KT * (4 + c) + KT - 1)
                    if n >= 2:
                        act.wait_ge(gr_o, n - 1)
                    act.activation(sil[:, n % 2, :], ps[:, b, :], ACT.Silu).then_inc(pj_ev, 1)
                for b in range(NT):
                    n = c * NT + b
                    act.wait_ge(gr_tr, n + 1)
                    act.activation(oT[:, 4 * c:4 * c + 4, b * P:(b + 1) * P],
                                   ps[:, 5 + b % 2, :].rearrange("p (k t) -> p k t", k=4), ACT.Copy).then_inc(gr_cp, 1)
            for i in range(2):
                sp.chunk(6 + i, AHEAD)
                sp.chunk(7 + i, 0, AHEAD)
                for b in range(4):
                    bank_done(act, pj_pe, 6 + i, b, P_A + KT * (6 + i) + KT - 1)
                    act.activation(swT[:, 4 * i + b, 0:TA], ps[:, b, 0:TA], ACT.Copy).then_inc(pj_ev, 1)
                bank_done(act, pj_pe, 6 + i, 4, P_A + KT * (6 + i) + KT - 1)
                act.activation(swT[:, 4 * i:4 * i + 4, TA:TOK], ps[:, 4:6, :].rearrange("p b (c t) -> p (b c) t", c=2),
                               ACT.Copy).then_inc(pj_ev, 1)
            sp.chunk(8, AHEAD)
            for b in range(NT):
                bank_done(act, pj_pe, 8, b, P_A + KT * 8 + KT - 1)
                kd = skr[:, b, :].rearrange("p (h e d) -> p h e d", h=SKV, e=2)
                kp = ps[:, b, 0:SKV * HD].rearrange("p (h d) -> p h d", h=SKV)
                act.activation(kd[:, :, 0, :], kp, ACT.Copy).then_inc(k_dup, 1)
                act.activation(kd[:, :, 1, :], kp, ACT.Copy).then_inc(k_dup, 1)
                if b == NT - 1:
                    act.activation(krow_out, ps[:, b, 0:SKV * HD], ACT.Copy).then_inc(k_dup, 1)
                act.activation(svr[:, b, :], ps[:, b, SKV * HD:2 * SKV * HD], ACT.Copy).then_inc(k_dup, 1)
            for g in range(SKV):
                act.wait_ge(k_tr, g + 1)
                act.activation(skT[:, g, 0:LAT], ps[:, 0, :], ACT.Copy).then_inc(k_cp, 1)
                act.activation(skT[:, g, LAT:TOK + P], ps[:, 1, 0:2 * P], ACT.Copy).then_inc(k_cp, 1)

            def softmax_exps(u):
                blocks = unit_keys(units[u][0])[1]
                act.wait_ge(sc_mx, u + 1)
                sf = soft[:, u % 2]
                act.activation(sf[:, 3, :], sf[:, 3, :], ACT.Exp)
                for j in range(GRP):
                    s = Sbuf[:, u % 2, j * BANK:j * BANK + len(blocks) * P]
                    a = act.activation(s, s, ACT.Exp, bias=sf[:, 1, j:j + 1], accum_out=sf[:, 2, j:j + 1])
                a.then_inc(sc_e, 1)

            n_pt = 0
            softmax_exps(0)
            for u in range(len(units)):
                n_pt = copy_pT(act, u, n_pt)
                if u + 1 < len(units):
                    softmax_exps(u + 1)
                copy_o(act, u)
                while n_col < 8 + sum(v % 5 < 4 for v in range(u + 1)) // 4:
                    mod_column()

            def merged_copies(n):
                act.wait_ge(mT_free, n + 1)
                for b in range(NT):
                    act.wait_ge(mt_pe, n * NT + (b + 1))
                    act.activation(mTc[:, :, b * P:(b + 1) * P],
                                   ps[:, 5 + b % 3, :].rearrange("p (k t) -> p k t", k=4), ACT.Copy).then_inc(mt_cp, 1)

            def gates_act(n, first, last):
                gate_split(sp, n, 0, AHEAD, KT)
                for q in (0, 2):
                    gate_split(sp, n, q + 1, 0, AHEAD)
                    for b in range(NT):
                        bank_done(act, gt_pe, n * 4 + q, b, n * 48 + (P_GATE + sum(GATE_PIECES[q]) - 1))
                        act.activation(sg[:, b, :], ps[:, b, :], ACT.Sigmoid).then_inc(gt_act, 1)
                    if q == 0 and not first:
                        merged_copies(n - 1)
                    gate_split(sp, n, q + 1, AHEAD, 8)
                    if q == 0:
                        gate_split(sp, n, 2, 0, KT)
                if not last:
                    gate_split(sp, n + 1, 0, 0, AHEAD)

            gate_split(sp, 0, 0, 0, AHEAD)
            gates_act(0, True, False)
            with act.Fori(1, 3) as n:
                gates_act(n, False, False)
            gates_act(3, False, True)
            merged_copies(3)
            out_pieces(sp, act, 0, 0, AHEAD)
            with act.Fori(0, 3) as n:
                out_pieces(sp, act, n, AHEAD, KT)
                out_pieces(sp, act, n + 1, 0, AHEAD)
            for t in range(NT):
                out_pieces(sp, act, 3, AHEAD + 2 * t, AHEAD + 2 * t + 2)
                act.wait_ge(wo_ev, 3 * NT)
                act.activation(ps[:, 5:8, :].rearrange("p b n -> p (b n)"), x1[:, t, 0:3 * BANK], ACT.Square,
                               accum_out=part[:, 0, t:t + 1]).then_inc(sq_part, 1)
                act.wait_ge(sq_part, t + 1)
            out_pieces(sp, act, 3, AHEAD + 2 * NT, KT)
            for t in range(NT):
                act.wait_ge(wo_ev, 3 * NT + t + 1)
                ch.step(act.activation(junkx[:, 0:BANK], x1[:, t, 3 * BANK:], ACT.Square, accum_out=stat[:, t:t + 1]))
                act.wait_ge(n2_b, 1)
                act.activation(stat[:, NT + t:NT + t + 1], stat[:, t:t + 1], ACT.Sqrt, scale=1.0 / D,
                               bias=part[:, 1, t:t + 1]).then_inc(n2_sq, 1)
            for j in range(2 * NT):
                t, half = j // 2, j % 2
                bank = (0, 2)[j % 2]
                act.wait_ge(n2_tr, j + 1)
                if t >= 2:
                    act.wait_ge(lg_pe, t - 1)
                act.activation(h2T[:, t % 2, 8 * half:8 * half + 8], ps[:, bank:bank + 2, :].rearrange(
                    "p b (k t) -> p (b k) t", k=4), ACT.Copy).then_inc(n2_cp, 1)
            act.wait_ge(lg_pe, NT)
            act.activation(lgT[0:NE, 0:LAT], ps[0:NE, 4, :], ACT.Copy).then_inc(lg_cp, 1)
            act.activation(lgT[0:NE, LAT:TOK], ps[0:NE, 7, 0:CTX], ACT.Copy).then_inc(lg_cp, 1)
            act.wait_ge(af_e, 1)
            act.activation(aff[:, 0], aff[:, 0], ACT.Exp).then_inc(af_e, 1)

            def copy_xs():
                for dst, src in xs_parts:
                    a = act.activation(xsT[:, 0, dst:dst + src.shape[1], :], src, ACT.Copy)
                a.then_inc(xs_h, 1)

            def split_expert(e, lo, hi):
                for j in range(lo, hi):
                    s = j % SP
                    act.wait_ge(exp_ready[j % ESLOTS], e * (16 * EXP_G // ESLOTS) + 16 * (j // ESLOTS + 1))
                    act.wait_ge(piece_used, e * EXP_G + (P_EXP + j + 1))
                    act.activation(spE[:, s, 0, :], exp_slot[j % ESLOTS], ACT.Copy).then_inc(piece_high, 1)

            mod_column()
            mod_column()
            mod_column()
            act.wait_ge(xs_tr, 1)
            copy_xs()
            mod_column()
            split_expert(0, 0, AHEAD)

            def expert_act(e, last):
                split_expert(e, AHEAD, 19)
                act.wait_ge(piece_used, e * EXP_G + (SP + P_EXP + 16))
                act.activation(hid[0:CAP, :], ps[0:CAP, 0:2, :].rearrange("p b n -> p (b n)"), ACT.Silu).then_inc(hd_s, 1)
                act.wait_ge(hd_tr, e + 1)
                for dst, src in hid_parts:
                    a = act.activation(hidT[:, 0, dst:dst + src.shape[1], :], src, ACT.Copy)
                a.then_inc(hd_h, 1)
                act.wait_ge(xs_tr, e + 2)
                copy_xs()
                split_expert(e, 19, EXP_G)
                if not last:
                    split_expert(e + 1, 0, AHEAD)

            with act.Fori(0, NE - 1) as e:
                expert_act(e, False)
            expert_act(NE - 1, True)
            for t in range(NT):
                act.wait_ge(y_ld[t], 16)
                ch.step(act.activation(junk2, yrow[:, t, :], ACT.Square, accum_out=stat[:, t:t + 1]))
                act.activation(stat[:, NT + t:NT + t + 1], stat[:, t:t + 1], ACT.Sqrt, scale=1.0 / D,
                               bias=epsb[:, :]).then_inc(y_sq, 1)

        @block.vector
        def _(dve):
            ch = Chain(dve, dve_step)
            dve.memset(epsb[:, :], EPS).then_inc(s_eps, 1)
            dve.sem_inc(pj_ev, NT)
            dve.sem_inc(gt_dve, NT)
            dve.sem_inc(wo_rd, NT)
            dve.sem_inc(gr_cp, 2)
            dve.sem_inc(mt_cp, 1)
            dve.sem_inc(mT_free, 1)
            dve.sem_inc(ye_free, 1)
            dve.sem_inc(ye_r, 1)
            dve.wait_ge(s_condS, 1)
            dve.tensor_copy(bgT, ps[:, 4, 2 * KT:5 * KT])
            dve.tensor_tensor(condR[:, :, 2:4], condT[:, :, :], condR[:, :, 0:2].bitcast(F32), ALU.subtract)\
               .then_inc(s_condS, 1)

            def mod_evacuated(m):
                dve.wait_ge(md_used, KT * (m + 1))
                dve.tensor_copy(modrow[0:4, m * D:m * D + 2 * BANK].rearrange("p (b n) -> p b n", b=2),
                                ps[0:4, 0:2, :]).then_inc(mr_d, 1)

            for i in range(2 * KT):
                dve.wait_ge(md_high, i + 1)
                dve.tensor_tensor(modS[:, i % MSLOTS, 1, :], ring[:, i % SLOTS, :],
                                  modS[:, i % MSLOTS, 0, :].bitcast(F32), ALU.subtract).then_inc(slot_used, 1)
                if i in X_SCALE:
                    t = X_SCALE.index(i)
                    r = stat[:, NT + t:NT + t + 1]
                    dve.wait_ge(h_sq, t + 1)
                    ch.step(dve.reciprocal(r, r))
                    dve.tensor_scalar(xrow[:, t, :], xrow[:, t, :], r, None, ALU.mult).then_inc(h_row, 1)
                if i == KT + 1:
                    mod_evacuated(0)
            mod_evacuated(1)
            dve.wait_ge(s_mT, 1)
            m4 = ps[:, 4, 0:8 * KT].rearrange("p (k w) -> p k w", w=4)
            ch.step(dve.tensor_copy(modT, m4[:, :, 0:2]))
            ch.step(dve.tensor_tensor(modT, modT, m4[:, :, 2:4], ALU.add))
            ch.step(dve.tensor_tensor(modT, modT, bgT[:, 0:2 * KT].unsqueeze(2).to_broadcast([P, 2 * KT, 2]), ALU.add))
            sc = modT[:, KT:2 * KT, :]
            ch.step(dve.scalar_tensor_tensor(sc, sc, 1.0, bgT[:, 2 * KT:3 * KT].unsqueeze(2).to_broadcast([P, KT, 2]),
                                             ALU.add, ALU.mult))

            def modulate(k):
                for who, v in enumerate((hT[:, k, 0:LAT], hT[:, k, LAT:TOK])):
                    a = dve.tensor_scalar(v, v, modT[:, KT + k, who:who + 1], modT[:, k, who:who + 1], ALU.mult, ALU.add)
                a.then_inc(h_m, 1)

            sp = Split(dve, False)
            dve.wait_ge(h_cp, 4 * NT)
            for k in range(AHEAD):
                modulate(k)
            for k in range(KT):
                if k + AHEAD < KT:
                    modulate(k + AHEAD)
                sp.chunk(0, k, k + 1)
            dve.memset(gaT[2 * RANK:2 * RANK + 1, :], 1.0)
            dve.memset(wdec[0:2 * RANK + 1, :, :], 0.0).then_inc(wdec0, 1)
            for i in range(1, 4):
                sp.chunk(i)
            dve.wait_ge(s_cst, 32)
            dve.wait_ge(ga_pe, 1)
            ch.step(dve.memset(aTm, 0.0))

            def z_min(s, part):
                lo, n = ((0, LAT), (LAT, CTX))[part]
                dve.wait_ge(z_ab, 2 * s + part + 1)
                dve.tensor_scalar(tg[:, lo:lo + n], ps[:, 4, 0:n], 0.0, None, ALU.min).then_inc(z_mn, 1)

            def gla_decays(s):
                dr = s % 2
                dve.wait_ge(z_mn, 2 * s + 2)
                dve.wait_ge(z_ln, s + 1)
                ch.step(dve.tensor_tensor(tg, tg, tz, ALU.subtract))
                if s:
                    dve.wait_ge(g_e, s)
                ch.step(dve.tensor_tensor_scan(tc, cst[:, C_RST:C_RST + TOK], tg, 0.0, ALU.mult, ALU.add))
                c3 = tc.rearrange("p (c t) -> p c t", t=CH)
                total = c3[:, :, CH - 1:CH].to_broadcast([P, NCH, CH])
                if s:
                    dve.wait_ge(kt_pe, s)
                if dr:
                    dve.tensor_tensor(tD, tc, tg, ALU.subtract)
                    ch.step(dve.tensor_tensor(tB.rearrange("p (c t) -> p c t", t=CH), total, c3, ALU.subtract))
                    dve.tensor_tensor(tB, tB, tg, ALU.add).then_inc(g_b, 1)
                else:
                    dve.tensor_tensor(tD.rearrange("p (c t) -> p c t", t=CH), total, c3, ALU.subtract)
                    dve.tensor_copy(tB, tc).then_inc(g_b, 1)

            def gla_scaled(s):
                h, xq = s // 2, xq2[s % 2]
                dve.wait_ge(g_e, s + 1)
                dve.tensor_tensor(tD, gkT[:, h, :], tD, ALU.mult)
                dve.scalar_tensor_tensor(xq, gqT[:, h, :], float(GK) ** -0.5, xq, ALU.mult, ALU.mult)
                dve.tensor_tensor(xk, gkT[:, h, :], xk, ALU.mult).then_inc(g_m, 1)

            z_min(0, 0)
            z_min(0, 1)
            gla_decays(0)
            gla_scaled(0)
            for s in range(2 * GH):
                h, dr = s // 2, s % 2
                dve.wait_ge(at_pe, s + 1)
                mask = cst[:, C_MB if dr else C_MF:][:, 0:P].bitcast(I32)
                if s >= 2:
                    dve.wait_ge(o_pe, 3 * (s - 1))
                for t in range(NT):
                    src = ps[:, 3, t * P:(t + 1) * P] if t < 4 else ps[:, 2, 2 * GV - P:2 * GV]
                    a = dve.copy_predicated(aTm[:, dr, t * P:(t + 1) * P], mask, src)
                a.then_inc(at_cp, 1)
                if s + 1 < 2 * GH:
                    z_min(s + 1, 0)
                order = ([9, 8] if dr else [8, 9]) + (list(range(7, 0, -1)) if dr else list(range(7)))
                if s >= 2:
                    dve.wait_ge(st_out, 16 * (s - 1))
                dve.wait_ge(st_ld[dr], 16 * (h + 1))
                for u, c in enumerate(order):
                    bank, half, made, _ = U_PLACE[u]
                    U = ps[:, bank, half * GV:(half + 1) * GV]
                    dve.wait_ge(u_pe, 9 * s + made)
                    if u == 0:
                        dve.tensor_copy(st[:, dr, 8, :], U).then_inc(s_up, 1)
                        dve.wait_ge(s_up, 9 * s + 1)
                        continue
                    src, dst = (8, 9) if u == 1 else (u - 2, u - 1)
                    dve.scalar_tensor_tensor(st[:, dr, dst, :], st[:, dr, src, :], decay[:, dr, c:c + 1], U,
                                             ALU.mult, ALU.add).then_inc(s_up, 1)
                    dve.wait_ge(s_up, 9 * s + u + 1)
                if s + 1 < 2 * GH:
                    z_min(s + 1, 1)
                    gla_decays(s + 1)
                    gla_scaled(s + 1)
                for i, b in enumerate((2, 1, 0) if dr else (2, 0, 1)):
                    n = 1 if b == 2 else 2
                    src = ps[:, b, 0:n * GV].rearrange("p (t v) -> p t v", t=n)
                    dst = og[:, 2 * b:2 * b + n, h * GV:(h + 1) * GV]
                    dve.wait_ge(o_pe, 3 * s + i + 1)
                    if dr:
                        dve.tensor_tensor(dst, dst, src, ALU.add).then_inc(o_ev, 1)
                    else:
                        dve.tensor_copy(dst, src).then_inc(o_ev, 1)
                if dr == 0:
                    dve.wait_ge(o_ev, 3 * (s + 1))
            dve.wait_ge(o_sq, 1)
            ch.step(dve.reciprocal(rs_gla[:, :], rs_gla[:, :]))
            sp.chunk(4, 0, AHEAD)
            for c in range(2):
                sp.chunk(4 + c, AHEAD)
                sp.chunk(5 + c, 0, AHEAD)
                for b in range(NT):
                    n = c * NT + b
                    dve.wait_ge(pj_ev, NT * (5 + c) + b + 1)
                    if n >= 2:
                        dve.wait_ge(gr_tr, n - 1 + (b == 0))
                    o = onr[:, b % 2, :]
                    for hh in range(2):
                        h = 2 * c + hh
                        a = dve.scalar_tensor_tensor(o[:, hh * GV:(hh + 1) * GV], og[:, b, h * GV:(h + 1) * GV],
                                                     rs_gla[:, b * GH + h:b * GH + h + 1],
                                                     glag[:, h * GV:(h + 1) * GV], ALU.mult, ALU.mult)
                    ch.step(a)
                    dve.tensor_tensor(o, o, sil[:, n % 2, :], ALU.mult).then_inc(gr_o, 1)
            sp.chunk(6, AHEAD)
            sp.chunk(7)
            sp.chunk(8)
            for i in range(8):
                dve.wait_ge(pj_ev, NT * (8 + i // 4))
                if i >= 1:
                    dve.wait_ge(sq_rp, i)
                ch.step(dve.tensor_tensor(rp[:, 0, :], swT[:, i, 0:LAT], cst[:, C_COS:C_COS + LAT], ALU.mult))
                dve.wait_ge(sq_pm, i + 1)
                ch.step(dve.tensor_tensor(rp[:, 1, :], ps[:, 5 + i % 2, :], cst[:, C_SIN:C_SIN + LAT], ALU.mult))
                dve.tensor_tensor(swT[:, i, 0:LAT], rp[:, 0, :], rp[:, 1, :], ALU.add).then_inc(sq_rp, 1)
            for g in range(SKV):
                dve.wait_ge(k_cp, 2 * g + 2)
                if g:
                    dve.wait_ge(k_rp, g)
                else:
                    dve.wait_ge(sq_rp, 8)
                ch.step(dve.tensor_tensor(rp[:, 0, :], skT[:, g, 0:LAT], cst[:, C_COS:C_COS + LAT], ALU.mult))
                dve.wait_ge(k_pm, g + 1)
                ch.step(dve.tensor_tensor(rp[:, 1, :], ps[:, 2 + g % 2, :], cst[:, C_SIN:C_SIN + LAT], ALU.mult))
                dve.tensor_tensor(skT[:, g, 0:LAT], rp[:, 0, :], rp[:, 1, :], ALU.add).then_inc(k_rp, 1)

            def softmax_front(u):
                t, g = units[u]
                _, blocks = unit_keys(t)
                nk = len(blocks) * P
                S = Sbuf[:, u % 2, :].rearrange("p (j n) -> p j n", j=GRP)[:, :, 0:nk]
                sf = soft[:, u % 2]
                dve.wait_ge(sc_pe, u + 1)
                if u >= 2:
                    dve.wait_ge(pt_pe, sum(len(unit_keys(units[v][0])[1]) for v in range(u - 1)))
                src = ps[:, 0:GRP, 0:nk]
                if t == 4:
                    dve.tensor_scalar(S, src, HD ** -0.5, None, ALU.mult).then_inc(sc_m, 1)
                else:
                    lo = {0: C_SW + P, 3: C_SW3}.get(t, C_SW)
                    m = cst[:, lo:lo + nk].unsqueeze(1).to_broadcast([P, GRP, nk])
                    dve.scalar_tensor_tensor(S, src, HD ** -0.5, m, ALU.mult, ALU.add).then_inc(sc_m, 1)
                dve.wait_ge(sc_m, u + 1)
                ch.step(dve.tensor_reduce(sf[:, 0, :], S, AX.X, ALU.max))
                ch.step(dve.tensor_tensor(sf[:, 0, :], sf[:, 0, :], sink[:, GRP * g:GRP * g + GRP], ALU.max))
                dve.tensor_tensor(sf[:, 3, :], sink[:, GRP * g:GRP * g + GRP], sf[:, 0, :], ALU.subtract)
                dve.tensor_scalar(sf[:, 1, :], sf[:, 0, :], -1.0, None, ALU.mult).then_inc(sc_mx, 1)

            def softmax_back(u):
                t, g = units[u]
                nk = len(unit_keys(t)[1]) * P
                sf = soft[:, u % 2]
                dve.wait_ge(sc_e, u + 1)
                ch.step(dve.tensor_tensor(sf[:, 2, :], sf[:, 2, :], sf[:, 3, :], ALU.add))
                ch.step(dve.reciprocal(sf[:, 4, :], sf[:, 2, :]))
                for j in range(GRP):
                    s = Sbuf[:, u % 2, j * BANK:j * BANK + nk]
                    a = dve.tensor_scalar(s, s, sf[:, 4, j:j + 1], None, ALU.mult)
                a.then_inc(sc_n, 1)

            softmax_front(0)
            for u in range(len(units)):
                softmax_back(u)
                if u + 1 < len(units):
                    softmax_front(u + 1)
            dve.wait_ge(kv_st, 32)
            ch2 = Chain(dve, dve2_step)
            def gates_dve(n, last):
                gate_split(sp, n, 0, AHEAD, KT)
                gate_split(sp, n, 1, 0, 8)
                gate_split(sp, n, 2, 0, AHEAD)
                for b in range(NT):
                    bank_done(dve, gt_pe, n * 4 + 1, b, n * 48 + (P_GATE + sum(GATE_PIECES[1]) - 1))
                    dve.wait_ge(gt_act, n * 10 + (b + 1))
                    dve.tensor_tensor(mrow[:, b, :], ps[:, b, :], sg[:, b, :], ALU.mult).then_inc(gt_dve, 1)
                gate_split(sp, n, 2, AHEAD, KT)
                gate_split(sp, n, 3, 0, 8)
                if not last:
                    gate_split(sp, n + 1, 0, 0, AHEAD)
                for b in range(NT):
                    bank_done(dve, gt_pe, n * 4 + 3, b, n * 48 + (P_GATE + sum(GATE_PIECES[3]) - 1))
                    dve.wait_ge(gt_act, n * 10 + (NT + b + 1))
                    dve.wait_ge(gt_dve, n * 10 + (2 * NT + b))
                    ch2.step(dve.tensor_tensor(mtmp, ps[:, b, :], sg[:, b, :], ALU.mult))
                    dve.tensor_tensor(mrow[:, b, :], mrow[:, b, :], mtmp, ALU.add).then_inc(gt_dve, 1)

            gate_split(sp, 0, 0, 0, AHEAD)
            with dve.Fori(0, 3) as n:
                ch2.enter(n, NT)
                gates_dve(n, False)
                ch2.leave(3)
            gates_dve(3, True)
            def out_dve(n, last):
                out_pieces(sp, dve, n, AHEAD, KT)
                if not last:
                    out_pieces(sp, dve, n + 1, 0, AHEAD)
                for b in range(NT):
                    who = b // 4
                    bank_done(dve, wo_pe, n, b, n * KT + (P_OUT + KT - 1))
                    cols = ds(n * BANK, BANK)
                    dve.tensor_tensor(wtmp[:, b, :], ps[:, b, :], gt1[:, who, cols], ALU.mult).then_inc(wo_rd, 1)
                for b in range(NT):
                    dve.wait_ge(wo_rd, n * NT + (NT + b + 1))
                    xv = x1[:, b, ds(n * BANK, BANK)]
                    dve.tensor_tensor(xv, xv, wtmp[:, b, :], ALU.add).then_inc(wo_ev, 1)
                if last:
                    dve.wait_ge(sq_part, NT)
                    dve.tensor_scalar(part[:, 1, 0:NT], part[:, 0, 0:NT], 1.0 / D, EPS, ALU.mult, ALU.add).then_inc(n2_b, 1)

            out_pieces(sp, dve, 0, 0, AHEAD)
            dve.wait_ge(wo_ld, 16 * 2)
            dve.wait_ge(xr_ld, 16 * NT)
            with dve.Fori(0, 3) as n:
                out_dve(n, False)
            out_dve(3, True)
            dve.wait_ge(ab_ld, 64)
            for t in range(NT):
                who = t // 4
                dve.wait_ge(n2_sq, t + 1)
                ch.step(dve.reciprocal(stat[:, NT + t:NT + t + 1], stat[:, NT + t:NT + t + 1]))
                if t >= 3:
                    dve.wait_ge(n2_tr, 2 * (t - 2))
                    dve.wait_ge(n2_st[t % 3], 16)
                ch.step(dve.scalar_tensor_tensor(h2row[:, t % 3], x1[:, t, :], stat[:, NT + t:NT + t + 1], A2[:, who, :],
                                                 ALU.mult, ALU.mult))
                dve.tensor_tensor(h2row[:, t % 3], h2row[:, t % 3], B2[:, who, :], ALU.add).then_inc(n2_h, 1)
            a0, a1 = aff[:, 0], aff[:, 1]
            dve.wait_ge(lr_pe, 1)
            lg = ps[:, 0, 0:NT * NE].rearrange("p (t e) -> p t e", t=NT)
            ch.step(dve.tensor_reduce(a1[:, :, 0], lg, AX.X, ALU.max))
            dve.tensor_tensor(a0, lg, a1[:, :, 0:1].to_broadcast([P, NT, NE]), ALU.subtract).then_inc(af_e, 1)
            dve.wait_ge(af_e, 2)
            ch.step(dve.tensor_reduce(a1[:, :, 1], a0, AX.X, ALU.add))
            ch.step(dve.reciprocal(a1[:, :, 2], a1[:, :, 1]))
            dve.tensor_tensor(a0, a0, a1[:, :, 2:3].to_broadcast([P, NT, NE]), ALU.mult).then_inc(af_r, 1)
            dve.wait_ge(af_tr, 1)
            dve.tensor_copy(affT[0:NE, 0:LAT], ps[0:NE, 5, :])
            dve.tensor_copy(affT[0:NE, LAT:TOK], ps[0:NE, 7, 0:CTX]).then_inc(af_cp, 1)
            dve.wait_ge(af_cp, 1)
            for lo, n, at, cap in ((0, LAT, 0, CAP_L), (LAT, CTX, CAP_L, CAP_C)):
                a = affT[0:NE, lo:lo + n]
                for r in range(cap // 8):
                    v = vals[0:NE, at + 8 * r:at + 8 * r + 8]
                    ch.step(dve.max(v, a))
                    dve.max_index(idxu[0:NE, at + 8 * r:at + 8 * r + 8], v, a)
                    ch.step(dve.match_replace(a, v, a, -1.0))
            dve.tensor_copy(idxf[0:NE, 0:CAP_L], idxu[0:NE, 0:CAP_L])
            dve.tensor_scalar(idxf[0:NE, CAP_L:CAP], idxu[0:NE, CAP_L:CAP], float(LAT), None, ALU.add).then_inc(tk_d, 1)
            dve.wait_ge(tk_tr, 1)
            dve.tensor_copy(idxT[0:CAP, 0:NE], ps[0:CAP, 7, 0:NE]).then_inc(tk_cp, 1)
            dve.tensor_copy(idxT[0:CAP, NE:NE + 2], ps[0:CAP, 7, 0:2]).then_inc(tk_cp, 1)
            dve.tensor_copy(gateT[0:CAP, :], ps[0:CAP, 7, NE:2 * NE]).then_inc(tk_cp, 1)
            def low_xs():
                for dst, src in xs_parts:
                    n = src.shape[1]
                    a = dve.tensor_tensor(xsT[:, 1, dst:dst + n, :], src, xsT[:, 0, dst:dst + n, :].bitcast(F32),
                                          ALU.subtract)
                a.then_inc(xs_l, 1)

            def low_expert(e, lo, hi):
                for j in range(lo, hi):
                    s = j % SP
                    dve.wait_ge(piece_high, e * EXP_G + (P_EXP + j + 1))
                    dve.tensor_tensor(spE[:, s, 1, :], exp_slot[j % ESLOTS], spE[:, s, 0, :].bitcast(F32), ALU.subtract)\
                       .then_inc(piece_ready, 1)

            dve.wait_ge(xs_h, 1)
            low_xs()
            low_expert(0, 0, AHEAD)

            def expert_dve(e, last):
                low_expert(e, AHEAD, 19)
                dve.wait_ge(hd_s, e + 1)
                dve.tensor_tensor(hid[0:CAP, :], hid[0:CAP, :], ps[0:CAP, 2:4, :].rearrange("p b n -> p (b n)"),
                                  ALU.mult).then_inc(hd_r, 1)
                dve.wait_ge(hd_h, e + 1)
                for dst, src in hid_parts:
                    n = src.shape[1]
                    a = dve.tensor_tensor(hidT[:, 1, dst:dst + n, :], src, hidT[:, 0, dst:dst + n, :].bitcast(F32),
                                          ALU.subtract)
                a.then_inc(hd_cp, 1)
                dve.wait_ge(xs_h, e + 2)
                low_xs()
                low_expert(e, 19, EXP_G)
                if not last:
                    low_expert(e + 1, 0, AHEAD)
                dve.wait_ge(piece_used, e * EXP_G + (SP + P_EXP + EXP_G))
                dve.wait_ge(g2_ld, 32)
                dve.wait_ge(ye_free, e + 1)
                dve.scalar_tensor_tensor(ye[0:CAP, :], ps[0:CAP, 4:8, :].rearrange("p b n -> p (b n)"),
                                         gateT[0:CAP, ds(e, 1)], gt2[0:CAP, :], ALU.mult, ALU.mult).then_inc(ye_r, 1)

            with dve.Fori(0, NE - 1) as e:
                expert_dve(e, False)
            expert_dve(NE - 1, True)
            dve.wait_ge(gf_ld, 16)
            for t in range(NT):
                dve.wait_ge(y_sq, t + 1)
                ch.step(dve.reciprocal(stat[:, NT + t:NT + t + 1], stat[:, NT + t:NT + t + 1]))
                y = yrow[:, t, :]
                dve.scalar_tensor_tensor(y, y, stat[:, NT + t:NT + t + 1], gfin, ALU.mult, ALU.mult).then_inc(y_r, 1)


INS = ["x_prompt", "x_sample", "state_gla_fwd", "state_gla_bwd", "cache_k", "cache_v", "c", "c_ctx", "w_mod", "b_mod",
       "g_norm1", "w_in", "w_dec_f", "b_dec_f", "w_dec_b", "b_dec_b", "g_gla", "attn_sink", "w_branch_a",
       "w_branch_b", "w_out", "g_norm2", "w_router", "w_exp_gate", "w_exp_up", "w_exp_down", "g_final"]
OUTS = [("y_prompt", (1, CTX, D)), ("y_sample", (1, LAT, D)), ("ns_fwd", (1, 1, GH, GK, GV)),
        ("ns_bwd", (1, 1, GH, GK, GV)), ("nk", (1, 1, CTX, SKV, HD)), ("nv", (1, 1, CTX, SKV, HD))]


def kernel(**inputs):
    import concourse.bacc as bacc
    from concourse.bass_utils import run_bass_kernel_spmd

    nc = bacc.Bacc("TRN2", target_bir_lowering=False, num_devices=1)
    arrays = {name: np.ascontiguousarray(inputs[name]) for name in INS}
    arrays["consts"] = constants()
    T = {name: nc.dram_tensor(name, a.shape, F32, kind="ExternalInput").ap() for name, a in arrays.items()}
    for name, shape in OUTS:
        T[name] = nc.dram_tensor(name, shape, F32, kind="ExternalOutput").ap()
    build(nc, T)
    r = run_bass_kernel_spmd(nc, [arrays], core_ids=[0])
    return tuple(r.results[0][name] for name, _ in OUTS)
```
